# Optimizing a Trainium2 kernel written in Bass

```python
import math
import jax, jax.numpy as jnp
from jax import lax
import numpy as np

D_MODEL = 1024
BATCH = 1
SEQ = 256
DEPTH = 2

GRID_W = 64
CTX_LEN = 256
EPS = 1e-6
ROPE_THETA = 10000.0
NEG = -1e30

HEAD_DIM = 64
BLOCK = 128
WINDOW = 128
FOURIER_DIM = D_MODEL // 2
FOURIER_GROUPS = 4
FOURIER_GROUP_DIM = FOURIER_DIM // FOURIER_GROUPS
WIN_HEADS = (D_MODEL // 2) // HEAD_DIM
WIN_KV_HEADS = WIN_HEADS // 4
MIX_IN_DIM = FOURIER_DIM + (WIN_HEADS + 2 * WIN_KV_HEADS) * HEAD_DIM
DIFF_HEADS = D_MODEL // (2 * HEAD_DIM)
FFN_DIM = 2816
N_EXPERTS = 8
TOP_K = 2
EXPERT_DIM = 7 * D_MODEL // 2

kernel_name = "hybrid_fourier_window_diffattn_moe_dit"

def rmsnorm(x, g):
    xf = x.astype(jnp.float32)
    y = xf * lax.rsqrt(jnp.mean(xf * xf, axis=-1, keepdims=True) + EPS)
    return (y * g.astype(jnp.float32)).astype(x.dtype)

def modulate(x, g, shift, scale):
    return rmsnorm(x, g) * (1 + scale) + shift

def rope_tables(rows_count):
    rows = jnp.repeat(jnp.arange(rows_count), GRID_W).astype(jnp.float32)
    cols = jnp.tile(jnp.arange(GRID_W), rows_count).astype(jnp.float32)
    axis_dim = HEAD_DIM // 2
    inv = ROPE_THETA ** (-jnp.arange(0, axis_dim, 2, dtype=jnp.float32) / axis_dim)
    ar = rows[:, None] * inv
    ac = cols[:, None] * inv
    return (jnp.cos(ar)[:, None, :], jnp.sin(ar)[:, None, :],
            jnp.cos(ac)[:, None, :], jnp.sin(ac)[:, None, :])

def rope_axis(p, cos, sin):
    p1, p2 = jnp.split(p, 2, axis=-1)
    return jnp.concatenate([p1 * cos - p2 * sin, p2 * cos + p1 * sin], axis=-1)

def apply_rope2d(x, rope):
    cos_r, sin_r, cos_c, sin_c = rope
    half = x.shape[-1] // 2
    out = jnp.concatenate([rope_axis(x[..., :half], cos_r, sin_r),
                           rope_axis(x[..., half:], cos_c, sin_c)], axis=-1)
    return out.astype(x.dtype)

def fourier_mix(u):
    uf = u.astype(jnp.float32)
    return jnp.real(jnp.fft.fft2(uf, axes=(1, 3), norm="ortho")).astype(u.dtype)

def sink_column(sink, lead_shape, hkv, g):
    s = sink.astype(jnp.float32).reshape((1,) * (len(lead_shape) - 3) + (hkv, g, 1, 1))
    return jnp.broadcast_to(s, lead_shape + (1,))

def window_attention(q, k, v, kc, vc, sink):
    B, L, Hq, d = q.shape
    Hkv = k.shape[2]
    G = Hq // Hkv
    C = kc.shape[1]
    nb = L // BLOCK
    scale = d ** -0.5
    qb = q.reshape(B, nb, BLOCK, Hkv, G, d)
    pad = ((0, 0), (BLOCK, BLOCK), (0, 0), (0, 0))
    kp = jnp.pad(k, pad).reshape(B, nb + 2, BLOCK, Hkv, d)
    vp = jnp.pad(v, pad).reshape(B, nb + 2, BLOCK, Hkv, d)
    kw = jnp.concatenate([kp[:, :-2], kp[:, 1:-1], kp[:, 2:]], axis=2)
    vw = jnp.concatenate([vp[:, :-2], vp[:, 1:-1], vp[:, 2:]], axis=2)
    blk = jnp.arange(nb)[:, None, None]
    qabs = blk * BLOCK + jnp.arange(BLOCK)[None, :, None]
    kabs = (blk - 1) * BLOCK + jnp.arange(3 * BLOCK)[None, None, :]
    valid = (jnp.abs(qabs - kabs) <= WINDOW) & (kabs >= 0) & (kabs < L)
    s_loc = jnp.einsum('bnqhgd,bnkhd->bnhgqk', qb, kw).astype(jnp.float32) * scale
    s_loc = jnp.where(valid[None, :, None, None], s_loc, NEG)
    s_ctx = jnp.einsum('bnqhgd,bkhd->bnhgqk', qb, kc).astype(jnp.float32) * scale
    s_sink = sink_column(sink, s_loc.shape[:-1], Hkv, G)
    p = jax.nn.softmax(jnp.concatenate([s_ctx, s_loc, s_sink], axis=-1), axis=-1)
    p_ctx = p[..., :C].astype(v.dtype)
    p_loc = p[..., C:C + 3 * BLOCK].astype(v.dtype)
    o = (jnp.einsum('bnhgqk,bkhd->bnqhgd', p_ctx, vc)
         + jnp.einsum('bnhgqk,bnkhd->bnqhgd', p_loc, vw))
    return o.reshape(B, L, Hq * d)

def context_gqa_attention(q, k, v, sink):
    B, C, Hq, d = q.shape
    Hkv = k.shape[2]
    G = Hq // Hkv
    qg = q.reshape(B, C, Hkv, G, d)
    s = jnp.einsum('bqhgd,bkhd->bhgqk', qg, k).astype(jnp.float32) * (d ** -0.5)
    s_sink = sink_column(sink, s.shape[:-1], Hkv, G)
    p = jax.nn.softmax(jnp.concatenate([s, s_sink], axis=-1), axis=-1)[..., :C]
    o = jnp.einsum('bhgqk,bkhd->bqhgd', p.astype(v.dtype), v)
    return o.reshape(B, C, Hq * d)

def fourier_window_mixer(hx, hc, w_in, w_out, sink, rope, need_ctx):
    def split_proj(h):
        B, L, _ = h.shape
        z = h @ w_in
        o1 = FOURIER_DIM
        o2 = o1 + WIN_HEADS * HEAD_DIM
        o3 = o2 + WIN_KV_HEADS * HEAD_DIM
        f = z[..., :o1].reshape(B, L, FOURIER_GROUPS, FOURIER_GROUP_DIM)
        q = z[..., o1:o2].reshape(B, L, WIN_HEADS, HEAD_DIM)
        k = z[..., o2:o3].reshape(B, L, WIN_KV_HEADS, HEAD_DIM)
        v = z[..., o3:].reshape(B, L, WIN_KV_HEADS, HEAD_DIM)
        return f, q, k, v
    fx, qx, kx, vx = split_proj(hx)
    fc, qc, kc, vc = split_proj(hc)
    B, L, _ = hx.shape
    qx = apply_rope2d(qx, rope)
    kx = apply_rope2d(kx, rope)
    ox = jnp.concatenate([fourier_mix(fx).reshape(B, L, FOURIER_DIM),
                          window_attention(qx, kx, vx, kc, vc, sink)], axis=-1) @ w_out
    if not need_ctx:
        return ox, None
    C = hc.shape[1]
    oc = jnp.concatenate([fourier_mix(fc).reshape(B, C, FOURIER_DIM),
                          context_gqa_attention(qc, kc, vc, sink)], axis=-1) @ w_out
    return ox, oc

def diff_attend(q, k, v, lam):
    s = jnp.einsum('bqhcd,bkhcd->bhcqk', q, k).astype(jnp.float32) * (q.shape[-1] ** -0.5)
    p = jax.nn.softmax(s, axis=-1)
    w = p[:, :, 0] - lam * p[:, :, 1]
    return jnp.einsum('bhqk,bkhe->bqhe', w.astype(v.dtype), v)

def diff_mixer(hx, hc, w_qkv, w_out, lam_vec, subln_g, lam_init, rope, need_ctx):
    def proj(h, use_rope):
        B, L, _ = h.shape
        q, k, v = jnp.split(h @ w_qkv, 3, axis=-1)
        q = q.reshape(B, L, 2 * DIFF_HEADS, HEAD_DIM)
        k = k.reshape(B, L, 2 * DIFF_HEADS, HEAD_DIM)
        if use_rope:
            q = apply_rope2d(q, rope)
            k = apply_rope2d(k, rope)
        q = q.reshape(B, L, DIFF_HEADS, 2, HEAD_DIM)
        k = k.reshape(B, L, DIFF_HEADS, 2, HEAD_DIM)
        v = v.reshape(B, L, DIFF_HEADS, 2 * HEAD_DIM)
        return q, k, v
    lv = lam_vec.astype(jnp.float32)
    lam = jnp.exp(jnp.sum(lv[0] * lv[1])) - jnp.exp(jnp.sum(lv[2] * lv[3])) + lam_init
    qx, kx, vx = proj(hx, True)
    qc, kc, vc = proj(hc, False)
    B, L, _ = hx.shape
    nb = L // BLOCK
    k_all = jnp.concatenate([kc, kx], axis=1)
    v_all = jnp.concatenate([vc, vx], axis=1)
    qb = jnp.moveaxis(qx.reshape(B, nb, BLOCK, DIFF_HEADS, 2, HEAD_DIM), 1, 0)
    ob = lax.map(lambda qblk: diff_attend(qblk, k_all, v_all, lam), qb)
    ox = jnp.moveaxis(ob, 0, 1).reshape(B, L, DIFF_HEADS, 2 * HEAD_DIM)
    ox = (rmsnorm(ox, subln_g) * (1.0 - lam_init)).reshape(B, L, D_MODEL) @ w_out
    if not need_ctx:
        return ox, None
    C = hc.shape[1]
    oc = diff_attend(qc, kc, vc, lam)
    oc = (rmsnorm(oc, subln_g) * (1.0 - lam_init)).reshape(B, C, D_MODEL) @ w_out
    return ox, oc

def swiglu(h, w_in, w_out):
    g, u = jnp.split(h @ w_in, 2, axis=-1)
    return (jax.nn.silu(g) * u) @ w_out

def moe_swiglu(h, router_w, w_in, w_out):
    logits = jnp.einsum('btd,de->bte', h, router_w).astype(jnp.float32)
    top_vals, top_idx = lax.top_k(logits, TOP_K)
    gates = jax.nn.softmax(top_vals, axis=-1)
    combine = jnp.sum(jax.nn.one_hot(top_idx, N_EXPERTS, dtype=jnp.float32) * gates[..., None], axis=-2)
    out = jnp.zeros_like(h)
    for e in range(N_EXPERTS):
        out = out + combine[..., e:e + 1].astype(h.dtype) * swiglu(h, w_in[e], w_out[e])
    return out

def lambda_init_fn(layer):
    return 0.8 - 0.6 * math.exp(-0.3 * layer)

def setup_inputs(seed: int = 0) -> dict:
    key = jax.random.key(seed)
    ks = jax.random.split(key, 20)
    n_even = (DEPTH + 1) // 2
    n_odd = DEPTH // 2
    f32 = jnp.float32

    def w(k, shape, fan_in, gain=1.0):
        return jax.random.normal(k, shape, f32) * (gain * fan_in ** -0.5)

    return {
        "x": jax.random.normal(ks[0], (BATCH, SEQ, D_MODEL), f32),
        "c": jax.random.normal(ks[1], (BATCH, D_MODEL), f32),
        "ctx": jax.random.normal(ks[2], (BATCH, CTX_LEN, D_MODEL), f32),
        "c_ctx": jax.random.normal(ks[3], (D_MODEL,), f32),
        "ada_w": w(ks[4], (DEPTH, D_MODEL, 6 * D_MODEL), D_MODEL, 0.5),
        "ada_b": 0.01 * jax.random.normal(ks[5], (DEPTH, 6 * D_MODEL), f32),
        "norm_g": 1.0 + 0.01 * jax.random.normal(ks[6], (DEPTH, 4, D_MODEL), f32),
        "mix_in_w": w(ks[7], (n_even, D_MODEL, MIX_IN_DIM), D_MODEL),
        "mix_out_w": w(ks[8], (n_even, D_MODEL, D_MODEL), D_MODEL),
        "win_sink": 0.5 * jax.random.normal(ks[9], (n_even, WIN_HEADS), f32),
        "diff_qkv_w": w(ks[10], (n_odd, D_MODEL, 3 * D_MODEL), D_MODEL),
        "diff_out_w": w(ks[11], (n_odd, D_MODEL, D_MODEL), D_MODEL),
        "diff_lambda": 0.1 * jax.random.normal(ks[12], (n_odd, 4, HEAD_DIM), f32),
        "diff_subln_g": 1.0 + 0.01 * jax.random.normal(ks[13], (n_odd, 2 * HEAD_DIM), f32),
        "ffn_in_w": w(ks[14], (n_even, D_MODEL, 2 * FFN_DIM), D_MODEL),
        "ffn_out_w": w(ks[15], (n_even, FFN_DIM, D_MODEL), FFN_DIM),
        "router_w": w(ks[16], (n_odd, D_MODEL, N_EXPERTS), D_MODEL),
        "expert_in_w": w(ks[17], (n_odd, N_EXPERTS, D_MODEL, 2 * EXPERT_DIM), D_MODEL),
        "expert_out_w": w(ks[18], (n_odd, N_EXPERTS, EXPERT_DIM, D_MODEL), EXPERT_DIM),
    }

def reference(x, c, ctx, c_ctx, ada_w, ada_b, norm_g, mix_in_w, mix_out_w, win_sink,
              diff_qkv_w, diff_out_w, diff_lambda, diff_subln_g,
              ffn_in_w, ffn_out_w, router_w, expert_in_w, expert_out_w):
    n_tok = x.shape[1]
    ROWS = n_tok // GRID_W
    rope = rope_tables(ROWS)
    for layer in range(DEPTH):
        j = layer // 2
        even = layer % 2 == 0
        need_ctx = layer < DEPTH - 1
        mod_x = (jax.nn.silu(c) @ ada_w[layer] + ada_b[layer])[:, None, :]
        mod_c = jax.nn.silu(c_ctx) @ ada_w[layer] + ada_b[layer]
        sh1x, sc1x, g1x, sh2x, sc2x, g2x = jnp.split(mod_x, 6, axis=-1)
        sh1c, sc1c, g1c, sh2c, sc2c, g2c = jnp.split(mod_c, 6, axis=-1)

        def channel(h):
            if even:
                return swiglu(h, ffn_in_w[j], ffn_out_w[j])
            return moe_swiglu(h, router_w[j], expert_in_w[j], expert_out_w[j])

        hx = modulate(x, norm_g[layer, 0], sh1x, sc1x)
        hc = modulate(ctx, norm_g[layer, 0], sh1c, sc1c)
        if even:
            yx, yc = fourier_window_mixer(hx, hc, mix_in_w[j], mix_out_w[j], win_sink[j], rope, need_ctx)
        else:
            yx, yc = diff_mixer(hx, hc, diff_qkv_w[j], diff_out_w[j], diff_lambda[j], diff_subln_g[j],
                                lambda_init_fn(layer), rope, need_ctx)
        x = x + g1x * rmsnorm(yx, norm_g[layer, 1])
        hx = modulate(x, norm_g[layer, 2], sh2x, sc2x)
        x = x + g2x * rmsnorm(channel(hx), norm_g[layer, 3])
        if need_ctx:
            ctx = ctx + g1c * rmsnorm(yc, norm_g[layer, 1])
            hc = modulate(ctx, norm_g[layer, 2], sh2c, sc2c)
            ctx = ctx + g2c * rmsnorm(channel(hc), norm_g[layer, 3])
    return x


_drawn_inputs = setup_inputs


def setup_inputs(seed=0):
    import zlib

    import numpy as np

    out = dict(_drawn_inputs(seed))
    spreads = {}
    factors = {'norm_g': 3.357, 'win_sink': 64.0, 'diff_subln_g': 26.904}
    for name, (base, spread) in spreads.items():
        noise = np.random.default_rng([zlib.crc32(name.encode()), seed]).standard_normal(out[name].shape)
        drawn = base * np.exp(spread * noise) if base else spread * noise
        out[name] = __import__('jax').numpy.asarray(drawn.astype(out[name].dtype))
    for name, factor in factors.items():
        out[name] = (out[name] * factor).astype(out[name].dtype)
    return out
```

```python
from contextlib import ExitStack
import math

import numpy as np

import concourse.bass as bass
from concourse import mybir

F32 = mybir.dt.float32
F32R = mybir.dt.float32r
I32 = mybir.dt.int32
ACT = mybir.ActivationFunctionType
ALU = mybir.AluOpType
AX_X = mybir.AxisListType.X

P = 128
D = 1024
DK = D // P
SEQ = 256
TILES = 4
XT = 2
EPS = 1e-6
NEG = -1e30
HD = 64
FFN = 2816
FG = FFN // 256
NE = 8
ED = 3584
EJ = ED // 512
SCALE = HD ** -0.5
LAM_INIT = 0.8 - 0.6 * math.exp(-0.3)

RAW = 6
SPL = 3
BLK = 2048

ADA_CH = 12
B_ADA0 = 0
B_MIXIN = 8
B_ATT0 = 13
B_MIXOUT = 37
B_FFNIN = 41
B_FFNOUT = B_FFNIN + 2 * FG
B_QKV = B_FFNOUT + FG
B_ATT1 = B_QKV + 12
B_DOUT = B_ATT1 + 16
B_MOE = B_DOUT + 4
IN_BLOCKS = 4 * EJ
OUT_BLOCKS = ED // 256
EB = IN_BLOCKS + OUT_BLOCKS
assert EB % RAW == 0 and EB % SPL == 0
ATT0_CHUNKS = [2, 2, 2, 2, 1, 1, 1, 1]

T_ID, T_TRI, T_ROPE, T_DFT = 0, 128, 384, 576
T_MOE = T_DFT + 1280
T_ALL = T_MOE + 128 * 3 + 16


def constant_tables():
    t = np.zeros((P, T_ALL), np.float64)
    r = np.arange(P)
    t[:, T_ID:T_ID + P] = np.eye(P)
    t[:, T_TRI:T_TRI + P] = np.where(r[None, :] > r[:, None], NEG, 0)
    t[:, T_TRI + P:T_TRI + 2 * P] = np.where(r[None, :] < r[:, None], NEG, 0)
    inv = np.float32(10000.0) ** (-np.arange(0, 32, 2, dtype=np.float32) / np.float32(32))
    for tile in range(XT):
        tok = tile * P + r
        for axis, pos in enumerate((tok // 64, tok % 64)):
            ang = (pos[:, None].astype(np.float32) * inv[None, :]).astype(np.float64)
            at = T_ROPE + tile * 32 + axis * 16
            t[:, at:at + 16] = np.cos(ang)
            t[:, at + 64:at + 80] = np.sin(ang)
            t[:, at + 128:at + 144] = -np.sin(ang)
    lp = np.arange(SEQ)
    for c in range(2):
        ang = 2 * np.pi * (((c * P + r)[:, None] * lp[None, :]) % SEQ) / SEQ
        t[:, T_DFT + c * 512:T_DFT + c * 512 + 256] = np.cos(ang)
        t[:, T_DFT + c * 512 + 256:T_DFT + c * 512 + 512] = np.sin(ang)
    ang = 2 * np.pi * ((r[:, None] * r[None, :]) % P) / P
    norm = 1 / math.sqrt(SEQ * P)
    t[:, T_DFT + 1024:T_DFT + 1152] = np.cos(ang) * norm
    t[:, T_DFT + 1152:T_DFT + 1280] = -np.sin(ang) * norm
    t[:, T_MOE:T_MOE + P] = r[:, None] < r[None, :]
    t[:, T_MOE + P:T_MOE + 2 * P] = 1
    t[:, T_MOE + 2 * P:T_MOE + 3 * P] = r[None, :]
    t[:, T_MOE + 3 * P:] = np.tile(np.arange(8) - 8, 2)[None, :]
    return t.astype(np.float32)


def backbone(nc, x, c, ctx_in, c_ctx, ada_w, ada_b, norm_g, mix_in_w, mix_out_w, win_sink, diff_qkv_w,
             diff_out_w, diff_lambda, diff_subln_g, ffn_in_w, ffn_out_w, router_w, expert_in_w,
             expert_out_w, tables, out):
    stack = ExitStack()

    def sb(name, shape, dt=F32):
        return stack.enter_context(nc.sbuf_tensor(name, shape, dt))

    RES = sb("residual", [P, TILES, D])
    WRAW = sb("w_raw", [P, RAW, BLK])
    WHI = sb("w_hi", [P, SPL, BLK], F32R)
    WLO = sb("w_lo", [P, SPL, BLK], F32R)
    ID = sb("ident", [P, P])
    CST = sb("cond_stationary", [P, DK, P], F32R)
    MROW = sb("mod_rows", [40, 2, P])
    COL = sb("mod_cols", [P, 40])
    ACOL = sb("scale_cols", [P, 2, DK])
    SS = sb("sumsq", [P, 16])
    MS = sb("meansq", [P, 16])
    STD = sb("std", [P, 16])
    Y0 = sb("rstd0", [P, 16])
    Y1 = sb("rstd_tmp", [P, 16])
    RSTD = sb("rstd", [P, 16])
    SINK = sb("sink", [P, 8])
    MX = sb("row_max", [P, 4])
    NEGM = sb("neg_max", [P, 4])
    TS = sb("sink_shifted", [P, 4])
    ES = sb("sink_exp", [P, 4])
    SUMS = sb("row_sums", [P, 4])
    RL = sb("row_recip", [P, 4])
    NRL = sb("row_recip_lam", [P, 4])
    LAM = sb("lam", [P, 4])
    GSUB = sb("subln_col", [P, 2])
    CNT = sb("overflow", [1, 1], I32)

    RW = sb("router", [P, DK, NE])
    LG = sb("logits", [P, 10, XT, NE])
    G9 = sb("gates", [P, XT, NE])
    PA = sb("pos_assign", [P, NE + 1, 2, XT])
    CUR = sb("cur_pa", [P, 2, XT])
    GS = sb("gate_slot", [P, 1])

    def area(*specs):
        with ExitStack() as s:
            return [s.enter_context(nc.sbuf_tensor(n, sh, dt)) for n, sh, dt in specs]

    W0 = 8192
    HT, WORK, MODB, T2 = area(("h_t", [P, 2, DK, 512], F32R), ("work", [P, 12288], F32),
                              ("mod_buf", [P, 1536], F32), ("tables", [P, 512], F32))
    _, ASP = area(("pad_a", [P, W0 + 12288], F32), ("act_split", [P, 2, 2, 512], F32R))
    ZT, P1, PT1 = area(("z_t1", [P, 2, DK, 256], F32R), ("p1", [P, 4, 512], F32), ("pt1", [P, 4, 256], F32))
    (HTE, YS, PTR, YACC, ONEHOT, SIL, TM) = area(
        ("h_te", [P, 2, DK, P], F32R), ("y_split", [P, 2, D], F32R), ("onehot_t", [P, 2 * P], F32R),
        ("y_acc", [P, XT, D], F32), ("onehot", [P, XT, P], F32), ("silu_g", [P, 2, 512], F32),
        ("moe_tables", [P, 400], F32))
    _, ACTT, ACTN, HN = area(("pad_b", [P, W0 + 4096], F32), ("act_t", [P, 2, ED // P, P], F32R),
                             ("act_n", [P, 2, 512], F32), ("h_nat", [P, XT, D], F32))
    _, HTF = area(("pad_c", [P, W0 + 4096], F32), ("h_tf", [P, DK, 256], F32))
    def work(off, *dims):
        n = int(np.prod(dims))
        v = WORK[:, off:off + n]
        if len(dims) == 1:
            return v
        names = "abcd"[:len(dims)]
        return v.rearrange(f"p ({' '.join(names)}) -> p {' '.join(names)}",
                           **{k: d for k, d in zip(names[1:], dims[1:])})

    F_N = work(0, TILES, 512)
    V0 = work(2048, TILES, P)
    QT0 = work(2560, 4, 512)
    KT0 = work(4608, 512)
    PR0 = work(5120, 4, 512)
    PT0 = work(7168, 4, 512)
    DFT = work(9216, 1280)
    AT0 = work(5120, 2, 512)
    K_N = work(6144, TILES, P)
    ROT0 = work(6656, 512)
    QROT = work(10496, 512)
    Q_N = work(7168, TILES, 512)
    ACTF = work(0, FFN // P, 512)
    SILF = work(11264, 2, 512)
    V1 = work(0, TILES, D)
    QT1 = work(4096, DK, 256)
    KT1 = work(6144, DK, 512)
    NAT = work(10240, TILES, 512)
    OA = work(10240, XT, D)
    ROT1 = MODB[:, 0:512]
    XN = {0: work(5120, TILES, D), 1: work(0, TILES, D), 2: work(0, TILES, D)}
    TF = {0: work(0, 2, 512), 1: work(4096, 2, 512), 2: work(4096, 2, 512)}
    POST = {0: (work(5120, 2, D), work(7168, D), work(8192, D), work(9216, D)),
            1: (work(0, 2, D), work(2048, D), work(3072, D), work(4096, D)),
            2: (work(6144, 1, D), work(7168, D), work(8192, D), work(9216, D)),
            3: (work(0, 1, D), work(1024, D), work(2048, D), work(3072, D))}
    SCB, SHB, NGB = work(0, D), work(1024, D), work(2048, D)
    MR, BI, SH = MODB[0:2, 0:512], MODB[0:2, 512:1024], MODB[0:2, 1024:1536]
    TRI, ROPE = T2[:, 0:256], T2[:, 256:448]
    UPPER, ONES, IOTA, IOTA8 = TM[:, 0:P], TM[:, P:2 * P], TM[:, 2 * P:3 * P], TM[:, 3 * P:3 * P + 16]

    mod = nc.dram_tensor("mod_scratch", [2, 2, 6 * D], F32, kind="Internal").ap()
    ps = stack.enter_context(nc.psum_tensor("ps", [P, 8, 512], F32))

    def sem(name):
        return stack.enter_context(nc.semaphore(name))

    rows_in = [sem(f"rows_in{i}") for i in range(3)]
    landed = [sem(f"landed{i}") for i in range(RAW)]
    (hi_done, lo_done, used, res_in, tab_in, crow_in, crow_silu, cond_tr, cond_hi, cond_lo, 
     ada_shift, ada_row, bias_in, mod_stored, cols_tr, ms_ready, std_ready, xn_ready, norm_tr,
     tf_ready, ht_hi, ht_lo, dch, f_copied, q_ctx, kv_ctx, kv_x, q_x, qk_tr, qk_evac, dft1, at_ready, dft2,
     z_hi, z_lo, scores, negmax, exps, prob_scaled, p_tr, pt_even, pt_odd, pv_done, sq_done, gate_in,
     post_done, silu_done, act_done, asp_hi, asp_lo, asp_half, nat_ctx, nat_x, nat_tr, nat_evac, v_even,
     v_odd, small_in, lam_dve, lam_exp, o_raw, o_norm, o_tr, lam_in, hn_done, h_tr, h_evac, logits_rdy, d_ready, e_ready,
     assign_rdy, pos_rdy, flag_rdy, onehot_rdy, gather_rdy, hte_hi, hte_lo, tr_ready, act_hi, act_lo,
     y_hi, y_lo, ptt_ready, pt_done, gs_done, comb_rdy, acc_done, cur_done, fin_chain, out_done,
     fin_rdy, moe_in) = [sem(n) for n in (
        "hi_done lo_done used res_in tab_in crow_in crow_silu cond_tr cond_hi cond_lo "
        "ada_shift ada_row bias_in mod_stored cols_tr ms_ready std_ready xn_ready norm_tr "
        "tf_ready ht_hi ht_lo dch f_copied q_ctx kv_ctx kv_x q_x qk_tr qk_evac dft1 at_ready dft2 "
        "z_hi z_lo scores negmax exps prob_scaled p_tr pt_even pt_odd pv_done sq_done gate_in "
        "post_done silu_done act_done asp_hi asp_lo asp_half nat_ctx nat_x nat_tr nat_evac v_even "
        "v_odd small_in lam_dve lam_exp o_raw o_norm o_tr lam_in hn_done h_tr h_evac logits_rdy d_ready e_ready "
        "assign_rdy pos_rdy flag_rdy onehot_rdy gather_rdy hte_hi hte_lo tr_ready act_hi act_lo "
        "y_hi y_lo ptt_ready pt_done gs_done comb_rdy acc_done cur_done fin_chain out_done "
        "fin_rdy moe_in").split()]

    def cols512(w, k0, c0):
        return [(w[k0 * P:(k0 + 4) * P, c0:c0 + 512].rearrange("(k p) n -> p k n", p=P), (4, 512), 0, P)]

    def rows256(w, k0):
        return [(w[k0 * P:(k0 + 2) * P, 0:D].rearrange("(k p) n -> p k n", p=P), (2, D), 0, P)]

    def ada_chunk(q):
        w = ada_w[q // ADA_CH]
        return [cols512(w, 4 * h, 512 * (q % ADA_CH)) for h in range(2)]

    blocks = []
    for q in range(4):
        blocks += ada_chunk(q)
    mw = mix_in_w[0]
    for n in range(2):
        blocks += [cols512(mw, 4 * h, 512 * n) for h in range(2)]
    blocks.append([(mw[:, 1024:1280].rearrange("(k p) n -> p k n", p=P), (8, 256), 0, P)])
    for q in range(4, 16):
        blocks += ada_chunk(q)
    for n in range(2):
        blocks += cols512(mix_out_w[0], 0, 512 * n),
        src = mix_out_w[0, 512:1024, 512 * n:512 * n + 512].rearrange("(g j d) n -> g d j n", g=2, j=4)
        blocks.append([(src[g], (4, 512), HD * g, HD) for g in range(2)])
    for i in range(FG):
        for h in range(2):
            blocks.append([(ffn_in_w[0, 512 * h:512 * h + 512, FFN * u + 256 * i:FFN * u + 256 * i + 256]
                            .rearrange("(k p) n -> p k n", p=P), (4, 2, 256, u), 0, P) for u in range(2)])
    for m in range(FG):
        blocks.append(rows256(ffn_out_w[0], 2 * m))
    for n in range(6):
        blocks += [cols512(diff_qkv_w[0], 4 * h, 512 * n) for h in range(2)]
    for q in range(16, 24):
        blocks += ada_chunk(q)
    for n in range(2):
        blocks += [cols512(diff_out_w[0], 4 * h, 512 * n) for h in range(2)]
    assert len(blocks) == B_MOE

    def slot_view(slot, dims, p0, pn):
        v = WRAW[p0:p0 + pn, slot, :]
        if len(dims) == 4:
            return v.rearrange("p (k u n) -> p k u n", k=dims[0], u=2)[:, :, dims[3], :]
        return v.rearrange("p (k n) -> p k n", k=dims[0])

    land_at, total = [], [0] * RAW
    for b, parts in enumerate(blocks):
        total[b % RAW] += 16 * len(parts)
        land_at.append(total[b % RAW])

    def moe_base(rnd):
        return B_MOE + NE * EB * rnd

    def moe_landed(rnd, x_, i):
        s = (B_MOE + i) % RAW
        firsts = [j for j in range(EB) if (B_MOE + j) % RAW == s]
        per = sum(16 * moe_parts(j) for j in firsts)
        upto = sum(16 * moe_parts(j) for j in firsts if j <= i)
        return total[s] + rnd * NE * per + x_ * per + upto

    def moe_parts(i):
        return 2 if i < IN_BLOCKS else 1

    ATT0_U = [B_ATT0 + 2 * sum(ATT0_CHUNKS[:g]) for g in range(9)]
    ATT1_U = [B_ATT1 + 2 * g for g in range(9)]

    def ada_end(q):
        if q < 4:
            return 2 * q + 2
        return (B_ATT0 + 2 * (q - 4) if q < 16 else B_ATT1 + 2 * (q - 16)) + 2

    block = stack.enter_context(nc.Block())

    @block.sync
    def _(sp):
        for b, parts in enumerate(blocks):
            if b >= RAW:
                sp.wait_ge(lo_done, b - RAW + 1)
            for src, dims, p0, pn in parts:
                sp.dma_start(slot_view(b % RAW, dims, p0, pn), src).then_inc(landed[b % RAW], 16)
            if b == 3:
                for t in range(TILES):
                    src = (x if t < XT else ctx_in)[0, (t % 2) * P:(t % 2 + 1) * P, :]
                    sp.dma_start(RES[:, t, :], src).then_inc(res_in, 16)

        def experts(rnd):
            with sp.Fori(0, NE) as e:
                for i in range(EB):
                    slot = (B_MOE + i) % RAW
                    sp.wait_ge(lo_done, moe_base(rnd) + e * EB + (i - RAW + 1))
                    if i < IN_BLOCKS:
                        j, k0 = i // 4, 2 * (i % 4)
                        for u in range(2):
                            src = expert_in_w[0, e, k0 * P:(k0 + 2) * P, ED * u + 512 * j:ED * u + 512 * j + 512]
                            sp.dma_start(slot_view(slot, (2, 2, 512, u), 0, P),
                                         src.rearrange("(k p) n -> p k n", p=P)).then_inc(landed[slot], 16)
                    else:
                        k0 = 2 * (i - IN_BLOCKS)
                        src = expert_out_w[0, e, k0 * P:(k0 + 2) * P, :].rearrange("(k p) n -> p k n", p=P)
                        sp.dma_start(slot_view(slot, (2, D), 0, P), src).then_inc(landed[slot], 16)

        experts(0)
        sp.wait_ge(flag_rdy, 1)
        more = sp.value_load(CNT[0:1, 0:1], min_val=0, max_val=1)
        with sp.If(more > 0):
            experts(1)
        sp.end_ifs()
        for t in range(XT):
            sp.wait_ge(fin_rdy, t + 1)
            sp.dma_start(out[0, t * P:(t + 1) * P, :], RES[:, t, :]).then_inc(out_done, 16)
        sp.wait_ge(out_done, 16 * XT)

    @block.gpsimd
    def _(pool):
        pool.dma_start(ID[:], tables[:, T_ID:T_ID + P]).then_inc(crow_in, 16)
        pool.dma_start(MROW[0:8, 0, :], c[0].rearrange("(k p) -> k p", p=P)).then_inc(crow_in, 16)
        pool.dma_start(MROW[8:16, 0, :], c_ctx.rearrange("(k p) -> k p", p=P)).then_inc(crow_in, 16)

        def bias(q):
            if q:
                pool.wait_ge(ada_row, q)
            src = ada_b[q // ADA_CH:q // ADA_CH + 1, 512 * (q % ADA_CH):512 * (q % ADA_CH) + 512]
            pool.dma_start(BI, src.broadcast_to([2, 512])).then_inc(bias_in, 16)

        def store(q):
            pool.wait_ge(ada_row, q + 1)
            dst = mod[q // ADA_CH, :, 512 * (q % ADA_CH):512 * (q % ADA_CH) + 512]
            pool.dma_start(dst, MR).then_inc(mod_stored, 16)

        def mod_rows(s):
            layer, piece, gi, need = [(0, 0, 0, 4), (0, 3, 2, 10), (1, 0, 0, 16)][s]
            pool.wait_ge(mod_stored, 16 * need)
            if s == 2:
                pool.wait_ge(cols_tr, 1)
            for st in range(2):
                src = mod[layer, st, piece * D:(piece + 2) * D].rearrange("(k p) -> k p", p=P)
                pool.dma_start(MROW[16 * st:16 * st + 16, s % 2, :], src).then_inc(rows_in[s], 16)
            pool.dma_start(MROW[32:40, s % 2, :], norm_g[layer, gi].rearrange("(k p) -> k p", p=P)).then_inc(rows_in[s], 16)

        def gate_rows(p):
            layer, piece, gi = [(0, 2, 1), (0, 5, 3), (1, 2, 1), (1, 5, 3)][p]
            gb, ngb = POST[p][0], POST[p][1]
            for st in range(gb.shape[1]):
                src = mod[layer, st:st + 1, piece * D:(piece + 1) * D]
                pool.dma_start(gb[:, st, :], src.broadcast_to([P, D])).then_inc(gate_in, 16)
            pool.dma_start(ngb, norm_g[layer, gi:gi + 1, :].broadcast_to([P, D])).then_inc(gate_in, 16)

        bias(0)
        pool.dma_start(T2[:, 0:448], tables[:, T_TRI:T_TRI + 448]).then_inc(tab_in, 16)
        pool.dma_start(DFT, tables[:, T_DFT:T_DFT + 1280]).then_inc(tab_in, 16)
        pool.dma_start(SINK[:], win_sink.broadcast_to([P, 8])).then_inc(tab_in, 16)
        pool.dma_start(GSUB[:, 0:1], diff_subln_g.rearrange("a p -> p a")).then_inc(small_in, 16)
        pool.dma_start(RW[:], router_w[0].rearrange("(k p) e -> p k e", p=P)).then_inc(small_in, 16)
        for q in range(4):
            store(q)
            bias(q + 1)
        pool.wait_ge(cond_hi, 1)
        mod_rows(0)
        for q in range(4, 16):
            store(q)
            if q < 15:
                bias(q + 1)
        mod_rows(1)
        mod_rows(2)
        pool.wait_ge(mod_stored, 16 * 12)
        pool.wait_ge(pv_done, 8)
        gate_rows(0)
        pool.wait_ge(used, B_FFNOUT + 5)
        gate_rows(1)
        pool.wait_ge(used, B_QKV)
        pool.dma_start(ROPE, tables[:, T_ROPE:T_ROPE + 192]).then_inc(tab_in, 16)
        lam_row = diff_lambda.rearrange("a b d -> a (b d)")
        pool.dma_start(T2[:, 0:256], lam_row.broadcast_to([P, 256])).then_inc(lam_in, 16)
        bias(16)
        for q in range(16, 24):
            store(q)
            if q < 23:
                bias(q + 1)
        pool.wait_ge(mod_stored, 16 * 24)
        pool.wait_ge(pv_done, 16)
        gate_rows(2)
        pool.dma_start(SCB, mod[1, 0:1, 4 * D:5 * D].broadcast_to([P, D])).then_inc(moe_in, 16)
        pool.dma_start(SHB, mod[1, 0:1, 3 * D:4 * D].broadcast_to([P, D])).then_inc(moe_in, 16)
        pool.dma_start(NGB, norm_g[1, 2:3, :].broadcast_to([P, D])).then_inc(moe_in, 16)
        pool.wait_ge(post_done, 10)
        pool.dma_start(TM[:], tables[:, T_MOE:T_MOE + 400]).then_inc(moe_in, 16)
        pool.wait_ge(hn_done, 2)
        gate_rows(3)

    @block.scalar
    def _(act):
        at = [0]

        def hi_upto(n):
            for b in range(at[0], min(n, B_MOE)):
                act.wait_ge(landed[b % RAW], land_at[b])
                if b >= SPL:
                    act.wait_ge(used, b - SPL + 1)
                act.activation(WHI[:, b % SPL, :], WRAW[:, b % RAW, :], ACT.Copy).then_inc(hi_done, 1)
            at[0] = max(at[0], n)

        def sqrt(ev, n):
            act.wait_ge(ms_ready, ev + 1)
            act.activation(STD[:, 0:n], MS[:, 0:n], ACT.Sqrt).then_inc(std_ready, 1)

        def shift(q):
            act.wait_ge(used, ada_end(q))
            if q:
                act.wait_ge(ada_row, q)
            act.activation(SH, ps[32:34, 7, :], ACT.Copy).then_inc(ada_shift, 1)

        def norm_hi(s, u):
            for k in range(DK):
                hi_upto(u + SPL)
                act.wait_ge(tf_ready, s * DK + k + 1)
                act.activation(HT[:, 0, k, :], TF[s][:, k % 2, :], ACT.Copy).then_inc(ht_hi, 1)

        def squares(p, tiles, base):
            for t in range(tiles):
                if base + t:
                    act.wait_ge(sq_done, base + t)
                act.activation(POST[p][3].rearrange("p (a b) -> p a b", a=2), ps[:, t::4, :], ACT.Square,
                               accum_out=SS[:, t:t + 1]).then_inc(sq_done, 1)

        act.wait_ge(crow_in, 48)
        act.activation(MROW[0:16, 1, :], MROW[0:16, 0, :], ACT.Silu).then_inc(crow_silu, 1)
        act.wait_ge(cond_tr, 1)
        act.wait_ge(dch, 1)
        act.activation(CST[:, :, 0:2], ps[:, 7, 0:16].rearrange("p (s k) -> p k s", s=2),
                       ACT.Copy).then_inc(cond_hi, 1)
        hi_upto(SPL)
        for q in range(4):
            hi_upto(2 * q + 2 + SPL)
            shift(q)
        sqrt(0, 4)
        norm_hi(0, B_MIXIN)
        hi_upto(B_MIXIN + 2 + SPL)
        act.wait_ge(used, B_MIXIN + 2)
        act.activation(F_N, ps[:, 0:4, :], ACT.Copy).then_inc(f_copied, 1)
        hi_upto(B_MIXIN + 4 + SPL)
        act.wait_ge(used, B_MIXIN + 4)
        for t in range(2, 4):
            ins = act.activation(Q_N[:, t, :].rearrange("p (j g d) -> p g j d", g=2, j=4),
                                 ps[:, 4 + t, :].rearrange("p (g j d) -> p g j d", g=2, j=4), ACT.Copy)
        ins.then_inc(q_ctx, 1)
        hi_upto(B_MIXIN + 5 + SPL)
        act.wait_ge(used, B_MIXIN + 5)
        act.activation(K_N[:, 2:4, :], ps[:, 2:4, 0:P], ACT.Copy)
        act.activation(V0[:, 2:4, :], ps[:, 2:4, P:2 * P], ACT.Copy).then_inc(kv_ctx, 1)
        for n in range(9):
            if n < 8:
                act.wait_ge(dft1, n + 1)
                if n >= 2:
                    act.wait_ge(dft2, n - 1)
                act.activation(AT0[:, n % 2, :], ps[:, 4 + n % 2, :], ACT.Copy).then_inc(at_ready, 1)
            if n >= 1:
                u = n - 1
                act.wait_ge(dft2, u + 1)
                act.activation(HT[:, 0, u % 4, 256 * (u // 4):256 * (u // 4) + 256], ps[:, 6 + u % 2, 0:256],
                               ACT.Copy).then_inc(z_hi, 1)
        act.wait_ge(qk_tr, 1)
        act.activation(KT0, ps[:, 0, :], ACT.Copy).then_inc(qk_evac, 1)
        for j in range(4):
            act.wait_ge(qk_tr, j + 2)
            act.activation(QT0[:, j, :], ps[:, (j + 1) % 4, :], ACT.Copy).then_inc(qk_evac, 1)
        qn = 4
        for g in range(8):
            u = ATT0_U[g]
            nk = 512 if g < 4 else 256
            base = sum(4 if a < 4 else 2 for a in range(g))
            hi_upto(u + SPL)
            act.wait_ge(negmax, g + 1)
            for j in range(4):
                if g and j == 0:
                    act.wait_ge(p_tr, base)
                ins = act.activation(PR0[:, j, 0:nk], ps[:, j, 0:nk], ACT.Exp, bias=NEGM[:, j:j + 1], scale=SCALE,
                                     accum_out=SUMS[:, j:j + 1])
            act.activation(ES[:], TS[:], ACT.Exp).then_inc(exps, 1)
            hi_upto(u + 2 + SPL)
            shift(qn)
            for c_ in range(0, nk // P, 2):
                act.wait_ge(p_tr, base + c_ + 1)
                act.activation(PT0[:, c_, :], ps[:, 4, :], ACT.Copy).then_inc(pt_even, 1)
            if ATT0_CHUNKS[g] == 2:
                hi_upto(u + 4 + SPL)
                shift(qn + 1)
            qn += ATT0_CHUNKS[g]
            act.wait_ge(pv_done, g + 1)
            kv, t = g % 2, g // 2
            act.activation(HT[HD * kv:HD * kv + HD, 0, 4:8, t * P:t * P + P],
                           ps[HD * kv:HD * kv + HD, 6, :].rearrange("p (j q) -> p j q", j=4),
                           ACT.Copy).then_inc(z_hi, 1)
        hi_upto(B_MIXOUT + SPL)

        hi_upto(B_MIXOUT + 2 + SPL)
        hi_upto(B_FFNIN + SPL)
        act.wait_ge(used, B_FFNIN)
        squares(0, 4, 0)
        sqrt(1, 4)
        sqrt(2, 4)
        norm_hi(1, B_FFNIN)
        for i in range(FG):
            hi_upto(B_FFNIN + 2 * i + 1 + SPL)
            hi_upto(B_FFNIN + 2 * i + 2 + SPL)
            act.wait_ge(used, B_FFNIN + 2 * i + 2)
            if i:
                act.wait_ge(act_done, i)
            b0 = 4 * (i % 2)
            act.activation(SILF, ps[:, b0:b0 + 2, :], ACT.Silu).then_inc(silu_done, 1)
        for k in range(2 * FG):
            act.wait_ge(act_done, k // 2 + 1)
            if k >= 2:
                act.wait_ge(asp_half, k // 2) if k % 2 == 0 else act.wait_ge(used, B_FFNOUT + (k - 1) // 2)
            act.activation(ASP[:, 0, k % 2, :], ACTF[:, k, :], ACT.Copy).then_inc(asp_hi, 1)
            hi_upto(B_FFNOUT + k // 2 + SPL)
        hi_upto(B_QKV + SPL)
        act.wait_ge(used, B_QKV)
        squares(1, 4, 4)
        sqrt(3, 4)
        sqrt(4, 4)
        norm_hi(2, B_QKV)
        def nat_evac_q(n):
            act.wait_ge(nat_tr, n + 1)
            b0 = 4 * (n % 2)
            if n < 2:
                act.activation(QT1[:, 4 * n:4 * n + 4, :],
                               ps[:, b0 + 2:b0 + 4, :].rearrange("p b (j t) -> p (b j) t", j=2),
                               ACT.Copy).then_inc(nat_evac, 1)
            else:
                act.activation(KT1[:, 4 * (n - 2):4 * (n - 2) + 4, :], ps[:, b0:b0 + 4, :],
                               ACT.Copy).then_inc(nat_evac, 1)

        for n in range(6):
            b0 = 4 * (n % 2)
            hi_upto(B_QKV + 2 * n + 1 + SPL)
            hi_upto(B_QKV + 2 * n + 2 + SPL)
            act.wait_ge(used, B_QKV + 2 * n + 2)
            if n in (2, 3):
                act.wait_ge(nat_tr, n)
                act.activation(NAT[:, 2:4, :], ps[:, b0 + 2:b0 + 4, :], ACT.Copy).then_inc(nat_ctx, 1)
            if n >= 4:
                act.activation(V1[:, 0:2, 512 * (n - 4):512 * (n - 4) + 512], ps[:, b0:b0 + 2, :],
                               ACT.Copy).then_inc(v_even, 1)
            if 1 <= n <= 4:
                nat_evac_q(n - 1)
        act.wait_ge(lam_dve, 1)
        act.activation(LAM[:, 2:4], LAM[:, 0:2], ACT.Exp).then_inc(lam_exp, 1)
        for g in range(8):
            u = ATT1_U[g]
            hi_upto(u + SPL)
            act.wait_ge(negmax, 8 + g + 1)
            if g:
                act.wait_ge(p_tr, 24 + 2 * g)
            for j in range(4):
                ins = act.activation(P1[:, j, :], ps[:, j, :], ACT.Exp, bias=NEGM[:, j:j + 1], scale=SCALE,
                                     accum_out=SUMS[:, j:j + 1])
            ins.then_inc(exps, 1)
            hi_upto(u + 2 + SPL)
            shift(16 + g)
            act.wait_ge(p_tr, 24 + 2 * g + 1)
            act.wait_ge(pv_done, 8 + g)
            act.activation(PT1[:, 0:2, :], ps[:, 4, :].rearrange("p (c q) -> p c q", c=2),
                           ACT.Copy).then_inc(pt_even, 1)
        sqrt(5, 16)
        act.wait_ge(lam_dve, 2)
        for b in range(4):
            act.wait_ge(o_tr, b + 1)
            act.activation(ZT[:, 0, 2 * b:2 * b + 2, :], ps[:, b, :].rearrange("p (h t) -> p h t", h=2), ACT.Copy,
                           scale=GSUB[:, 1:2]).then_inc(z_hi, 1)
        hi_upto(B_DOUT + 2 + SPL)
        act.wait_ge(used, B_MOE)
        squares(2, 2, 8)
        sqrt(6, 2)
        sqrt(7, 2)
        act.wait_ge(h_tr, 1)
        act.activation(HTF[:].rearrange("p (b j) t -> p b (j t)", b=4), ps[:, 0:4, :], ACT.Copy).then_inc(h_evac, 1)
        act.wait_ge(d_ready, 1)
        act.activation(LG[:, 9, :, 0:1], LG[:, 9, :, 1:2], ACT.Exp).then_inc(e_ready, 1)

        def experts(rnd):
            base = moe_base(rnd)

            def hte(e):
                act.wait_ge(gather_rdy, 9 * rnd + e + 1)
                act.activation(HTE[:, 0, :, :], ps[:, 2:4, :].rearrange("p b (k s) -> p (b k) s", k=4),
                               ACT.Copy).then_inc(hte_hi, 1)

            def yhi(n, end):
                act.wait_ge(used, end)
                act.wait_ge(gs_done, n)
                act.activation(YS[:, 0, :].rearrange("p (a b) -> p a b", a=2), ps[:, 4:6, :], ACT.Copy,
                               scale=GS[:, 0:1]).then_inc(y_hi, 1)

            hte(0)
            with act.Fori(0, NE) as e:
                J = EJ * NE * rnd + e * EJ
                for i in range(EB):
                    s = (B_MOE + i) % RAW
                    act.wait_ge(landed[s], moe_landed(rnd, e, i))
                    act.wait_ge(used, base + e * EB + (i - SPL + 1))
                    act.activation(WHI[:, (B_MOE + i) % SPL, :], WRAW[:, s, :], ACT.Copy).then_inc(hi_done, 1)
                    if i == 2:
                        yhi(9 * rnd + e + 1, base + e * EB)
                    if i == 15:
                        act.wait_ge(ptt_ready, NE * rnd + e + 1)
                        act.activation(PTR[:], ps[:, 7, 0:2 * P], ACT.Copy).then_inc(pt_done, 1)
                    for j in range(EJ):
                        if i == 4 * j + 6:
                            act.wait_ge(used, base + e * EB + (4 * j + 4))
                            if j >= 2:
                                act.wait_ge(act_done, FG + J + (j - 1))
                            act.activation(SIL[:, j % 2, :], ps[:, 2 * (j % 2), :], ACT.Silu).then_inc(silu_done, 1)
                        if i == 4 * j + 9:
                            act.wait_ge(tr_ready, J + (j + 1))
                            act.activation(ACTT[:, 0, 4 * j:4 * j + 4, :],
                                           ps[:, 6, :].rearrange("p (k s) -> p k s", k=4),
                                           ACT.Copy).then_inc(act_hi, 1)
                    if i == 35:
                        hte(e + 1)
            yhi(9 * rnd + 9, base + NE * EB)

        experts(0)
        act.wait_ge(flag_rdy, 1)
        more = act.value_load(CNT[0:1, 0:1], min_val=0, max_val=1)
        with act.If(more > 0):
            experts(1)
        act.end_ifs()
        sqrt(8, 2)

    @block.tensor
    def _(pe):
        def mm(out_, l, r, first, last):
            return pe.matmul(out_, l, r, start=first, stop=last, skip_group_check=True)

        def split3(outs, lh, ll, whs, wls, first, last):
            for n, o in enumerate(outs):
                mm(o, lh, whs[n], first, False)
                mm(o, lh, wls[n], False, False)
            for n, o in enumerate(outs):
                ins = mm(o, ll, whs[n], False, last)
            return ins

        def ada(q, b):
            if q:
                pe.wait_ge(ada_row, q)
            for h in range(2):
                pe.wait_ge(lo_done, b + h + 1)
                for k in range(4):
                    for w in (WHI, WLO):
                        v = w[:, (b + h) % SPL, :].rearrange("p (k n) -> p k n", k=4)
                        ins = mm(ps[:, 7, :], CST[:, 4 * h + k, :], v[:, k, :], h == 0 and k == 0 and w is WHI,
                                 h == 1 and k == 3 and w is WLO)
                ins.then_inc(used, 1)

        def norm_tr_stage(s):
            pe.wait_ge(xn_ready, 4 * s + 4)
            pe.wait_ge(rows_in[s], 48)
            pe.transpose(ps[:, 0, 0:40], MROW[0:40, s % 2, :], ID[0:40, 0:40]).then_inc(cols_tr, 1)
            for k in range(DK):
                if k >= 4:
                    pe.wait_ge(tf_ready, s * DK + k - 3)
                for t in range(TILES):
                    ins = pe.transpose(ps[:, 4 + k % 4, t * P:(t + 1) * P], XN[s][:, t, k * P:(k + 1) * P], ID[:])
                ins.then_inc(norm_tr, 1)

        def linear(b, src, tiles, banks, halves=2):
            for h in range(halves):
                pe.wait_ge(lo_done, b + h + 1)
                wh = WHI[:, (b + h) % SPL, :].rearrange("p (k n) -> p k n", k=4)
                wl = WLO[:, (b + h) % SPL, :].rearrange("p (k n) -> p k n", k=4)
                for k in range(4):
                    kk = 4 * h + k
                    for t in tiles:
                        ins = split3([ps[:, banks + t, :]], src[:, 0, kk, t * P:(t + 1) * P],
                                     src[:, 1, kk, t * P:(t + 1) * P], [wh[:, k, :]], [wl[:, k, :]],
                                     kk == 0, kk == 7)
                ins.then_inc(used, 1)

        pe.wait_ge(crow_silu, 1)
        pe.transpose(ps[:, 7, 0:16], MROW[0:16, 1, :], ID[0:16, 0:16]).then_inc(cond_tr, 1)
        pe.wait_ge(cond_lo, 1)
        for q in range(4):
            ada(q, 2 * q)
        norm_tr_stage(0)
        pe.wait_ge(ht_lo, DK)
        linear(B_MIXIN, HT, range(4), 0)
        linear(B_MIXIN + 2, HT, range(4), 4)
        pe.wait_ge(f_copied, 1)
        b = B_MIXIN + 4
        pe.wait_ge(lo_done, b + 1)
        wh = WHI[:, b % SPL, :].rearrange("p (k n) -> p k n", k=8)
        wl = WLO[:, b % SPL, :].rearrange("p (k n) -> p k n", k=8)
        for t in range(TILES):
            for k in range(DK):
                ins = split3([ps[:, t, 0:256]], HT[:, 0, k, t * P:(t + 1) * P], HT[:, 1, k, t * P:(t + 1) * P],
                             [wh[:, k, :]], [wl[:, k, :]], k == 0, k == 7)
        ins.then_inc(used, 1)
        pe.wait_ge(tab_in, 48)
        pe.wait_ge(q_x, 1)
        pe.wait_ge(q_ctx, 1)
        for n in range(9):
            if n < 8:
                st, gr = n // 4, n % 4
                if n >= 2:
                    pe.wait_ge(at_ready, n - 1)
                for tt in range(2):
                    ins = mm(ps[:, 4 + n % 2, :], F_N[:, 2 * st + tt, gr * P:(gr + 1) * P],
                             DFT[:, 512 * tt:512 * tt + 512], tt == 0, tt == 1)
                ins.then_inc(dft1, 1)
            if n >= 1:
                u = n - 1
                pe.wait_ge(at_ready, u + 1)
                if u >= 2:
                    pe.wait_ge(z_lo, u - 1)
                mm(ps[:, 6 + u % 2, 0:256], DFT[:, 1024:1152], AT0[:, u % 2, 0:256], True, False)
                mm(ps[:, 6 + u % 2, 0:256], DFT[:, 1152:1280], AT0[:, u % 2, 256:512], False,
                   True).then_inc(dft2, 1)
        pe.wait_ge(kv_ctx, 1)
        pe.wait_ge(kv_x, 1)
        for t in range(TILES):
            ins = pe.transpose(ps[:, 0, t * P:(t + 1) * P], K_N[:, t, :], ID[:])
        ins.then_inc(qk_tr, 1)
        for j in range(4):
            if j == 3:
                pe.wait_ge(qk_evac, 1)
            for t in range(TILES):
                ins = pe.transpose(ps[:, (j + 1) % 4, t * P:(t + 1) * P], Q_N[:, t, j * P:(j + 1) * P], ID[:])
            ins.then_inc(qk_tr, 1)

        def scores0(g):
            t, kv = g // 2, g % 2
            p0 = HD * kv
            if g == 0:
                pe.wait_ge(qk_evac, 5)
            else:
                pe.wait_ge(exps, g)
            for j in range(4):
                q_ = QT0[p0:p0 + HD, j, t * P:(t + 1) * P]
                if t < XT:
                    mm(ps[:, j, :], q_, KT0[p0:p0 + HD, :], True, False)
                    far = P * (1 - t)
                    ins = mm(ps[:, j, far:far + P], ID[:], TRI[:, P * t:P * t + P], False, True)
                else:
                    ins = mm(ps[:, j, 0:256], q_, KT0[p0:p0 + HD, 256:512], True, True)
            ins.then_inc(scores, 1)

        scores0(0)
        pe.wait_ge(z_lo, 8)
        qn = 4
        trs = 0
        for g in range(8):
            u = ATT0_U[g]
            t, kv = g // 2, g % 2
            ada(qn, u)
            if g < 7:
                scores0(g + 1)
            pe.wait_ge(prob_scaled, g + 1)
            nk = 4 if g < 4 else 2
            for c_ in range(nk):
                if trs + c_ >= 2:
                    n_before = (trs + c_) // 2
                    pe.wait_ge(pt_even if c_ % 2 == 0 else pt_odd, n_before)
                for j in range(4):
                    ins = pe.transpose(ps[:, 4 + c_ % 2, j * P:(j + 1) * P], PR0[:, j, c_ * P:(c_ + 1) * P], ID[:])
                ins.then_inc(p_tr, 1)
            trs += nk
            if ATT0_CHUNKS[g] == 2:
                ada(qn + 1, u + 2)
            qn += ATT0_CHUNKS[g]
            pe.wait_ge(z_lo, 8 + g)
            for c_ in range(nk):
                pe.wait_ge(pt_even if c_ % 2 == 0 else pt_odd, (trs - nk) // 2 + c_ // 2 + 1)
                tk = c_ if g < 4 else c_ + 2
                ins = mm(ps[HD * kv:HD * kv + HD, 6, :], V0[:, tk, HD * kv:HD * kv + HD], PT0[:, c_, :],
                         c_ == 0, c_ == nk - 1)
            ins.then_inc(pv_done, 1)
        pe.wait_ge(z_lo, 16)
        linear(B_MIXOUT, HT, range(4), 0)
        linear(B_MIXOUT + 2, HT, range(4), 4)
        norm_tr_stage(1)
        pe.wait_ge(ht_lo, 2 * DK)
        for i in range(FG):
            if i >= 2:
                pe.wait_ge(act_done, i - 1)
            b0 = 4 * (i % 2)
            for h in range(2):
                b = B_FFNIN + 2 * i + h
                pe.wait_ge(lo_done, b + 1)
                wh = WHI[:, b % SPL, :].rearrange("p (k u n) -> p k u n", k=4, u=2)
                wl = WLO[:, b % SPL, :].rearrange("p (k u n) -> p k u n", k=4, u=2)
                for k in range(4):
                    kk = 4 * h + k
                    for u in range(2):
                        for f in range(2):
                            o = ps[:, b0 + 2 * u + f, :]
                            mm(o, wh[:, k, u, f * P:(f + 1) * P], HT[:, 0, kk, :], kk == 0, False)
                            mm(o, wh[:, k, u, f * P:(f + 1) * P], HT[:, 1, kk, :], False, False)
                            ins = mm(o, wl[:, k, u, f * P:(f + 1) * P], HT[:, 0, kk, :], False, kk == 7)
                ins.then_inc(used, 1)
        pe.wait_ge(act_done, FG)
        for m in range(FG):
            b = B_FFNOUT + m
            pe.wait_ge(lo_done, b + 1)
            wh = WHI[:, b % SPL, :].rearrange("p (k n) -> p k n", k=4)
            wl = WLO[:, b % SPL, :].rearrange("p (k n) -> p k n", k=4)
            for k in range(2):
                kk = 2 * m + k
                pe.wait_ge(asp_lo, kk + 1)
                for t in range(TILES):
                    ins = split3([ps[:, t, :], ps[:, 4 + t, :]], ASP[:, 0, k, t * P:(t + 1) * P],
                                 ASP[:, 1, k, t * P:(t + 1) * P], [wh[:, 2 * k + n, :] for n in range(2)],
                                 [wl[:, 2 * k + n, :] for n in range(2)], kk == 0, kk == 2 * FG - 1)
                ins.then_inc(asp_half if k == 0 else used, 1)
        norm_tr_stage(2)
        pe.wait_ge(ht_lo, 3 * DK)

        def nat_transposes(n):
            b0 = 4 * (n % 2)
            if n < 2:
                pe.wait_ge(nat_x, n + 1)
                for j in range(4):
                    for t in range(XT):
                        ins = pe.transpose(ps[:, b0 + 2 + j // 2, (j % 2) * 256 + t * P:(j % 2) * 256 + t * P + P],
                                           NAT[:, t, j * P:(j + 1) * P], ID[:])
            else:
                pe.wait_ge(nat_x, n + 1)
                pe.wait_ge(nat_ctx, n - 1)
                for j in range(4):
                    for t in range(TILES):
                        ins = pe.transpose(ps[:, b0 + j, t * P:(t + 1) * P], NAT[:, t, j * P:(j + 1) * P], ID[:])
            ins.then_inc(nat_tr, 1)

        for n in range(6):
            if n >= 2:
                pe.wait_ge(nat_evac, n - 1)
            linear(B_QKV + 2 * n, HT, range(2) if n < 2 else range(4), 4 * (n % 2))
            if 1 <= n <= 4:
                nat_transposes(n - 1)
        pe.wait_ge(v_even, 2)
        pe.wait_ge(v_odd, 2)

        def scores1(g):
            t, hp = g // 4, g % 4
            if g:
                pe.wait_ge(exps, 8 + g)
            else:
                pe.wait_ge(nat_evac, 4)
            for j in range(4):
                h, p0 = 2 * hp + j // 2, HD * (j % 2)
                ins = mm(ps[:, j, :], QT1[p0:p0 + HD, h, t * P:(t + 1) * P], KT1[p0:p0 + HD, h, :], True, True)
            ins.then_inc(scores, 1)

        scores1(0)
        for g in range(8):
            ada(16 + g, ATT1_U[g])
            if g < 7:
                scores1(g + 1)
            pe.wait_ge(prob_scaled, 8 + g + 1)
            for hb in range(2):
                if g:
                    pe.wait_ge(pt_even if hb == 0 else pt_odd, 12 + g)
                for cc in range(2):
                    for hh in range(2):
                        o = ps[:, 4 + hb, cc * 256 + hh * P:cc * 256 + hh * P + P]
                        ins = pe.transpose(o, P1[:, 2 * hh, (2 * hb + cc) * P:(2 * hb + cc + 1) * P], ID[:])
                ins.then_inc(p_tr, 1)
            if g:
                pe.wait_ge(o_raw, g)
            pe.wait_ge(pt_even, 12 + g + 1)
            pe.wait_ge(pt_odd, 12 + g + 1)
            for hh in range(2):
                h = 2 * (g % 4) + hh
                for c_ in range(4):
                    ins = mm(ps[:, 6, hh * P:(hh + 1) * P], PT1[:, c_, hh * P:(hh + 1) * P],
                             V1[:, c_, h * P:(h + 1) * P], c_ == 0, c_ == 3)
            ins.then_inc(pv_done, 1)
        pe.wait_ge(o_norm, 1)
        for b_ in range(4):
            for hh in range(2):
                for t in range(XT):
                    h = 2 * b_ + hh
                    ins = pe.transpose(ps[:, b_, hh * 256 + t * P:hh * 256 + t * P + P],
                                       OA[:, t, h * P:(h + 1) * P], ID[:])
            ins.then_inc(o_tr, 1)
        pe.wait_ge(z_lo, 20)
        linear(B_DOUT, ZT, range(2), 0)
        linear(B_DOUT + 2, ZT, range(2), 4)
        pe.wait_ge(hn_done, 2)
        for k in range(DK):
            for t in range(XT):
                ins = pe.transpose(ps[:, k // 2, (k % 2) * 256 + t * P:(k % 2) * 256 + t * P + P],
                                   HN[:, t, k * P:(k + 1) * P], ID[:])
        ins.then_inc(h_tr, 1)
        pe.wait_ge(h_evac, 1)
        pe.wait_ge(small_in, 32)
        for t in range(XT):
            for k in range(DK):
                ins = mm(ps[:, 4, t * NE:(t + 1) * NE], HTF[:, k, t * P:(t + 1) * P], RW[:, k, :], k == 0, k == DK - 1)
        ins.then_inc(logits_rdy, 1)
        pe.wait_ge(assign_rdy, 1)
        pe.wait_ge(moe_in, 64)
        A0, A1 = LG[:, 6, 0, :], LG[:, 6, 1, :]
        mm(ps[:, 5, 0:8], UPPER, A0, True, True)
        mm(ps[:, 5, 8:16], ONES, A0, True, False)
        mm(ps[:, 5, 8:16], UPPER, A1, False, True)
        mm(ps[:, 5, 16:24], ONES, A0, True, False)
        mm(ps[:, 5, 16:24], ONES, A1, False, True).then_inc(pos_rdy, 1)

        def experts(rnd):
            base = moe_base(rnd)

            def gather(n):
                pe.wait_ge(onehot_rdy, n)
                for k in range(DK):
                    for t in range(XT):
                        ins = mm(ps[:, 2 + k // 4, (k % 4) * P:(k % 4 + 1) * P], HN[:, t, k * P:(k + 1) * P],
                                 ONEHOT[:, t, :], t == 0, t == XT - 1)
                ins.then_inc(gather_rdy, 1)

            def combine(n, i):
                t, h = i // 2, i % 2
                pe.wait_ge(acc_done, n * 4 + (i + 1))
                for q in range(2):
                    ins = mm(ps[:, 7, :], PTR[:, t * P:(t + 1) * P], YS[:, q, 512 * h:512 * h + 512], q == 0, q == 1)
                ins.then_inc(comb_rdy, 1)

            gather(9 * rnd + 1)
            with pe.Fori(0, NE) as e:
                J = EJ * NE * rnd + e * EJ
                for i in range(EB):
                    slot = (B_MOE + i) % SPL
                    wh = WHI[:, slot, :].rearrange("p (k n) -> p k n", k=4)
                    wl = WLO[:, slot, :].rearrange("p (k n) -> p k n", k=4)
                    if i == 0:
                        pe.wait_ge(hte_lo, 9 * rnd + e + 1)
                    if i < IN_BLOCKS:
                        j = i // 4
                        if i % 4 == 0 and j >= 2:
                            pe.wait_ge(act_done, FG + J + (j - 1))
                        pe.wait_ge(lo_done, base + e * EB + (i + 1))
                        for k in range(2):
                            kk = 2 * (i % 4) + k
                            ins = split3([ps[:, 2 * (j % 2), :], ps[:, 2 * (j % 2) + 1, :]], HTE[:, 0, kk, :],
                                         HTE[:, 1, kk, :], [wh[:, 2 * k + n, :] for n in range(2)],
                                         [wl[:, 2 * k + n, :] for n in range(2)], kk == 0, kk == 7)
                    else:
                        m = i - IN_BLOCKS
                        if m == 0:
                            pe.wait_ge(y_lo, 9 * rnd + e + 1)
                        pe.wait_ge(act_lo, J + (m // 2 + 1))
                        pe.wait_ge(lo_done, base + e * EB + (i + 1))
                        for k in range(2):
                            kk = 2 * m + k
                            ins = split3([ps[:, 4, :], ps[:, 5, :]], ACTT[:, 0, kk, :], ACTT[:, 1, kk, :],
                                         [wh[:, 2 * k + n, :] for n in range(2)],
                                         [wl[:, 2 * k + n, :] for n in range(2)], kk == 0, kk == ED // P - 1)
                    ins.then_inc(used, 1)
                    if 5 <= i < 9:
                        if i == 5:
                            pe.wait_ge(y_lo, 9 * rnd + e + 1)
                            pe.wait_ge(gs_done, 9 * rnd + e + 1)
                        combine(9 * rnd + e, i - 5)
                    if i == 12:
                        pe.wait_ge(acc_done, (9 * rnd + e) * 4 + 5)
                        for t in range(XT):
                            pe.transpose(ps[:, 7, t * P:(t + 1) * P], ONEHOT[:, t, :], ID[:])
                        for t in range(XT):
                            ins = mm(ps[:, 7, 2 * P:2 * P + NE], ONEHOT[:, t, :], G9[:, t, :], t == 0, t == XT - 1)
                        ins.then_inc(ptt_ready, 1)
                    for j in range(EJ):
                        if i == 4 * j + 6:
                            pe.wait_ge(act_done, FG + J + (j + 1))
                            if j >= 1:
                                pe.wait_ge(act_lo, J + j)
                            for k in range(4):
                                ins = pe.transpose(ps[:, 6, k * P:(k + 1) * P], ACTN[:, j % 2, k * P:(k + 1) * P], ID[:])
                            ins.then_inc(tr_ready, 1)
                    if i == 32:
                        gather(9 * rnd + e + 2)
            pe.wait_ge(y_lo, 9 * rnd + 9)
            pe.wait_ge(gs_done, 9 * rnd + 9)
            for i in range(4):
                combine(9 * rnd + 8, i)

        experts(0)
        pe.wait_ge(flag_rdy, 1)
        more = pe.value_load(CNT[0:1, 0:1], min_val=0, max_val=1)
        with pe.If(more > 0):
            experts(1)
        pe.end_ifs()

    @block.vector
    def _(dve):
        at = [0]
        links = [0]

        def link(ins):
            links[0] += 1
            ins.then_inc(dch, 1)
            dve.wait_ge(dch, links[0])

        def lo_upto(n):
            for b in range(at[0], min(n, B_MOE)):
                dve.wait_ge(hi_done, b + 1)
                dve.tensor_tensor(WLO[:, b % SPL, :], WRAW[:, b % RAW, :], WHI[:, b % SPL, :].bitcast(F32),
                                  ALU.subtract).then_inc(lo_done, 1)
            at[0] = max(at[0], n)

        def rstd(ev, n, count, lk=link):
            lk(dve.tensor_scalar(MS[:, 0:n], SS[:, 0:n], 1.0 / count, EPS, ALU.mult, ALU.add))
            dve.sem_inc(ms_ready, 1)
            dve.wait_ge(std_ready, ev + 1)
            lk(dve.reciprocal(Y0[:, 0:n], STD[:, 0:n]))
            lk(dve.tensor_tensor(Y1[:, 0:n], Y0[:, 0:n], Y0[:, 0:n], ALU.mult))
            lk(dve.tensor_tensor(Y1[:, 0:n], Y1[:, 0:n], MS[:, 0:n], ALU.mult))
            lk(dve.tensor_scalar(Y1[:, 0:n], Y1[:, 0:n], -0.5, 1.5, ALU.mult, ALU.add))
            lk(dve.tensor_tensor(RSTD[:, 0:n], Y0[:, 0:n], Y1[:, 0:n], ALU.mult))

        def row(q, b):
            dve.wait_ge(ada_shift, q + 1)
            if q:
                dve.wait_ge(mod_stored, 16 * q)
            dve.wait_ge(bias_in, 16 * (q + 1))
            link(dve.tensor_tensor(MR, ps[0:2, 7, :], SH, ALU.add))
            dve.tensor_tensor(MR, MR, BI, ALU.add).then_inc(ada_row, 1)

        def norm(s, ev, u):
            for t in range(TILES):
                link(dve.tensor_tensor_reduce(XN[s][:, t, :], RES[:, t, :], RES[:, t, :], 1.0, 0.0, ALU.mult,
                                              ALU.add, SS[:, t:t + 1]))
            rstd(ev, 4, D)
            for t in range(TILES):
                dve.tensor_scalar(XN[s][:, t, :], RES[:, t, :], RSTD[:, t:t + 1], None,
                                  ALU.mult).then_inc(xn_ready, 1)
            lo_upto(u + SPL)
            dve.wait_ge(cols_tr, s + 1)
            link(dve.tensor_copy(COL[:], ps[:, 0, 0:40]))
            for st in range(2):
                ins = dve.scalar_tensor_tensor(out=ACOL[:, st, :], in0=COL[:, 16 * st + 8:16 * st + 16], scalar=1.0,
                                               in1=COL[:, 32:40], op0=ALU.add, op1=ALU.mult)
            link(ins)

            def low(k):
                dve.wait_ge(ht_hi, s * DK + k + 1)
                dve.tensor_tensor(HT[:, 1, k, :], TF[s][:, k % 2, :], HT[:, 0, k, :].bitcast(F32),
                                  ALU.subtract).then_inc(ht_lo, 1)

            for k in range(DK):
                dve.wait_ge(norm_tr, s * DK + k + 1)
                if k >= 2:
                    dve.wait_ge(ht_lo, s * DK + k - 1)
                for st in range(2):
                    ins = dve.tensor_scalar(TF[s][:, k % 2, 256 * st:256 * st + 256],
                                            ps[:, 4 + k % 4, 256 * st:256 * st + 256], ACOL[:, st, k:k + 1],
                                            COL[:, 16 * st + k:16 * st + k + 1], ALU.mult, ALU.add)
                ins.then_inc(tf_ready, 1)
                if k:
                    low(k - 1)
            low(DK - 1)

        def post(p, ev, tiles, sq_base, gates):
            gb, ngb, tmp, _ = POST[p]
            dve.wait_ge(gate_in, gates)
            for st in range(gb.shape[1]):
                link(dve.tensor_tensor(gb[:, st, :], gb[:, st, :], ngb, ALU.mult))
            dve.wait_ge(sq_done, sq_base + tiles)
            rstd(ev, tiles, D)
            for t in range(tiles):
                link(dve.scalar_tensor_tensor(out=tmp.rearrange("p (a b) -> p a b", a=2), in0=ps[:, t::4, :],
                                              scalar=RSTD[:, t:t + 1],
                                              in1=gb[:, t // 2, :].rearrange("p (a b) -> p a b", a=2),
                                              op0=ALU.mult, op1=ALU.mult))
                link(dve.tensor_tensor(RES[:, t, :], RES[:, t, :], tmp, ALU.add))
                dve.sem_inc(post_done, 1)

        def rotate(dst, src, tile, heads, rot, end=None):
            d5 = dst.rearrange("p (h a s d) -> p h a s d", a=2, s=2, d=16)
            s5 = src.rearrange("p (h a s d) -> p h a s d", a=2, s=2, d=16)
            r5 = rot.rearrange("p (h a s d) -> p h a s d", a=2, s=2, d=16)

            def tab(kind):
                v = ROPE[:, 64 * kind + 32 * tile:64 * kind + 32 * tile + 32].rearrange("p (a d) -> p a d", a=2)
                return v.unsqueeze(1).broadcast_to([P, heads, 2, 16])

            for s_ in range(2):
                dve.tensor_tensor(d5[:, :, :, s_, :], s5[:, :, :, s_, :], tab(0), ALU.mult)
            dve.tensor_tensor(r5[:, :, :, 0, :], s5[:, :, :, 1, :], tab(2), ALU.mult)
            link(dve.tensor_tensor(r5[:, :, :, 1, :], s5[:, :, :, 0, :], tab(1), ALU.mult))
            if end is None:
                link(dve.tensor_tensor(dst, dst, rot, ALU.add))
            else:
                gjd = "p (g j d) -> p g j d"
                link(dve.tensor_tensor(end.rearrange("p (j g d) -> p g j d", g=2, j=4), dst.rearrange(gjd, g=2, j=4),
                                       rot.rearrange(gjd, g=2, j=4), ALU.add))

        link(dve.memset(CST[:].bitcast(F32), 0.0))
        dve.wait_ge(cond_hi, 1)
        dve.tensor_tensor(CST[:, :, 32:34], ps[:, 7, 0:16].rearrange("p (s k) -> p k s", s=2),
                          CST[:, :, 0:2].bitcast(F32), ALU.subtract).then_inc(cond_lo, 1)
        lo_upto(SPL)
        for q in range(4):
            lo_upto(2 * q + 2 + SPL)
            row(q, 2 * q)
        dve.wait_ge(res_in, 64)
        dve.wait_ge(tab_in, 48)
        norm(0, 0, B_MIXIN)
        lo_upto(B_MIXIN + 4 + SPL)
        dve.wait_ge(used, B_MIXIN + 4)
        for t in range(XT):
            rotate(QROT, ps[:, 4 + t, :], t, 8, ROT0, Q_N[:, t, :])
        dve.sem_inc(q_x, 1)
        lo_upto(B_MIXIN + 5 + SPL)
        dve.wait_ge(used, B_MIXIN + 5)
        for t in range(XT):
            rotate(K_N[:, t, :], ps[:, t, 0:P], t, 2, ROT0[:, 0:P])
        dve.tensor_copy(V0[:, 0:2, :], ps[:, 0:2, P:2 * P]).then_inc(kv_x, 1)
        for u in range(8):
            dve.wait_ge(z_hi, u + 1)
            o = HT[:, 0, u % 4, 256 * (u // 4):256 * (u // 4) + 256]
            dve.tensor_tensor(HT[:, 1, u % 4, 256 * (u // 4):256 * (u // 4) + 256], ps[:, 6 + u % 2, 0:256],
                              o.bitcast(F32), ALU.subtract).then_inc(z_lo, 1)
        link(dve.tensor_scalar(SINK[:], SINK[:], -1.0, None, ALU.mult))
        qn = 4
        trs = 0
        for g in range(8):
            u, kv, t = ATT0_U[g], g % 2, g // 2
            nk = 512 if g < 4 else 256
            dve.wait_ge(scores, g + 1)
            link(dve.tensor_reduce(MX[:], ps[:, 0:4, 0:nk], AX_X, ALU.max))
            if g:
                dve.wait_ge(exps, g)
            link(dve.scalar_tensor_tensor(out=NEGM[:], in0=MX[:], scalar=-SCALE, in1=SINK[:, 4 * kv:4 * kv + 4],
                                          op0=ALU.mult, op1=ALU.min))
            dve.tensor_tensor(TS[:], NEGM[:], SINK[:, 4 * kv:4 * kv + 4], ALU.subtract).then_inc(negmax, 1)
            lo_upto(u + SPL)
            dve.wait_ge(exps, g + 1)
            link(dve.tensor_tensor(RL[:], SUMS[:], ES[:], ALU.add))
            link(dve.reciprocal(RL[:], RL[:]))
            for j in range(4):
                ins = dve.tensor_scalar(PR0[:, j, 0:nk], PR0[:, j, 0:nk], RL[:, j:j + 1], None, ALU.mult)
            ins.then_inc(prob_scaled, 1)
            lo_upto(u + 2 + SPL)
            row(qn, u)
            for c_ in range(1, nk // P, 2):
                dve.wait_ge(p_tr, trs + c_ + 1)
                dve.tensor_copy(PT0[:, c_, :], ps[:, 5, :]).then_inc(pt_odd, 1)
            trs += nk // P
            if ATT0_CHUNKS[g] == 2:
                lo_upto(u + 4 + SPL)
                row(qn + 1, u + 2)
            qn += ATT0_CHUNKS[g]
            dve.wait_ge(z_hi, 8 + g + 1)
            rows, cols = slice(HD * kv, HD * kv + HD), slice(t * P, t * P + P)
            dve.tensor_tensor(HT[rows, 1, 4:8, cols], ps[rows, 6, :].rearrange("p (j q) -> p j q", j=4),
                              HT[rows, 0, 4:8, cols].bitcast(F32), ALU.subtract).then_inc(z_lo, 1)
        lo_upto(B_MIXOUT + SPL)
        lo_upto(B_MIXOUT + 2 + SPL)
        lo_upto(B_FFNIN + SPL)
        post(0, 1, 4, 0, 48)
        norm(1, 2, B_FFNIN)
        for i in range(FG):
            lo_upto(B_FFNIN + 2 * i + 1 + SPL)
            lo_upto(B_FFNIN + 2 * i + 2 + SPL)
            dve.wait_ge(silu_done, i + 1)
            b0 = 4 * (i % 2)
            dve.tensor_tensor(ACTF[:, 2 * i:2 * i + 2, :], SILF, ps[:, b0 + 2:b0 + 4, :],
                              ALU.mult).then_inc(act_done, 1)
        for k in range(2 * FG):
            lo_upto(B_FFNOUT + k // 2 + SPL)
            dve.wait_ge(asp_hi, k + 1)
            dve.wait_ge(act_done, k // 2 + 1)
            dve.tensor_tensor(ASP[:, 1, k % 2, :], ACTF[:, k, :], ASP[:, 0, k % 2, :].bitcast(F32),
                              ALU.subtract).then_inc(asp_lo, 1)
        lo_upto(B_QKV + SPL)
        post(1, 3, 4, 4, 96)
        norm(2, 4, B_QKV)
        dve.wait_ge(tab_in, 64)
        for n in range(6):
            b0 = 4 * (n % 2)
            lo_upto(B_QKV + 2 * n + 1 + SPL)
            lo_upto(B_QKV + 2 * n + 2 + SPL)
            dve.wait_ge(used, B_QKV + 2 * n + 2)
            if n < 4:
                if n:
                    dve.wait_ge(nat_tr, n)
                for t in range(XT):
                    rotate(NAT[:, t, :], ps[:, b0 + t, :], t, 8, ROT1)
                dve.sem_inc(nat_x, 1)
            else:
                dve.tensor_copy(V1[:, 2:4, 512 * (n - 4):512 * (n - 4) + 512],
                                ps[:, b0 + 2:b0 + 4, :]).then_inc(v_odd, 1)
        dve.wait_ge(lam_in, 16)
        lv = T2[:, 0:256]
        link(dve.tensor_tensor_reduce(MODB[:, 1280:1344], lv[:, 0:64], lv[:, 64:128], 1.0, 0.0, ALU.mult, ALU.add,
                                      LAM[:, 0:1]))
        link(dve.tensor_tensor_reduce(MODB[:, 1344:1408], lv[:, 128:192], lv[:, 192:256], 1.0, 0.0, ALU.mult,
                                      ALU.add, LAM[:, 1:2]))
        dve.sem_inc(lam_dve, 1)
        dve.wait_ge(lam_exp, 1)
        link(dve.tensor_tensor(LAM[:, 1:2], LAM[:, 3:4], LAM[:, 2:3], ALU.subtract))
        link(dve.tensor_scalar(LAM[:, 0:1], LAM[:, 1:2], -LAM_INIT, None, ALU.add))
        dve.wait_ge(small_in, 32)
        link(dve.tensor_scalar(GSUB[:, 1:2], GSUB[:, 0:1], 1.0 - LAM_INIT, None, ALU.mult))
        dve.sem_inc(lam_dve, 1)
        for g in range(8):
            u, t, hp = ATT1_U[g], g // 4, g % 4
            dve.wait_ge(scores, 8 + g + 1)
            link(dve.tensor_reduce(MX[:], ps[:, 0:4, :], AX_X, ALU.max))
            if g:
                dve.wait_ge(exps, 8 + g)
            dve.tensor_scalar(NEGM[:], MX[:], -SCALE, None, ALU.mult).then_inc(negmax, 1)
            lo_upto(u + SPL)
            dve.wait_ge(exps, 8 + g + 1)
            link(dve.reciprocal(RL[:], SUMS[:]))
            link(dve.tensor_scalar(NRL[:], RL[:], LAM[:, 0:1], None, ALU.mult))
            for hh in range(2):
                ins = dve.tensor_scalar(P1[:, 2 * hh, :], P1[:, 2 * hh, :], RL[:, 2 * hh:2 * hh + 1], None, ALU.mult)
            link(ins)
            for hh in range(2):
                ins = dve.scalar_tensor_tensor(out=P1[:, 2 * hh, :], in0=P1[:, 2 * hh + 1, :],
                                               scalar=NRL[:, 2 * hh + 1:2 * hh + 2], in1=P1[:, 2 * hh, :],
                                               op0=ALU.mult, op1=ALU.add)
            ins.then_inc(prob_scaled, 1)
            lo_upto(u + 2 + SPL)
            row(16 + g, u)
            dve.wait_ge(p_tr, 24 + 2 * g + 2)
            dve.tensor_copy(PT1[:, 2:4, :], ps[:, 5, :].rearrange("p (c q) -> p c q", c=2)).then_inc(pt_odd, 1)
            dve.wait_ge(pv_done, 8 + g + 1)
            link(dve.tensor_copy(OA[:, t, 256 * hp:256 * hp + 256], ps[:, 6, 0:256]))
            dve.sem_inc(o_raw, 1)
            for hh in range(2):
                o = OA[:, t, 256 * hp + P * hh:256 * hp + P * hh + P]
                n_ = t * 8 + 2 * hp + hh
                ins = dve.tensor_tensor_reduce(T2[:, P * hh:P * hh + P], o, o, 1.0, 0.0,
                                               ALU.mult, ALU.add, SS[:, n_:n_ + 1])
            link(ins)
        rstd(5, 16, 2 * HD)
        for n_ in range(16):
            o = OA[:, n_ // 8, P * (n_ % 8):P * (n_ % 8) + P]
            ins = dve.tensor_scalar(o, o, RSTD[:, n_:n_ + 1], None, ALU.mult)
        ins.then_inc(o_norm, 1)
        lo_upto(B_DOUT + SPL)
        for b in range(4):
            dve.wait_ge(z_hi, 16 + b + 1)
            dve.scalar_tensor_tensor(out=ZT[:, 1, 2 * b:2 * b + 2, :],
                                     in0=ps[:, b, :].rearrange("p (h t) -> p h t", h=2), scalar=GSUB[:, 1:2],
                                     in1=ZT[:, 0, 2 * b:2 * b + 2, :].bitcast(F32), op0=ALU.mult,
                                     op1=ALU.subtract).then_inc(z_lo, 1)
        lo_upto(B_DOUT + 2 + SPL)
        post(2, 6, 2, 8, 128)
        dve.wait_ge(moe_in, 64)
        link(dve.scalar_tensor_tensor(out=SCB, in0=SCB, scalar=1.0, in1=NGB, op0=ALU.add, op1=ALU.mult))
        for t in range(XT):
            link(dve.tensor_tensor_reduce(HN[:, t, :], RES[:, t, :], RES[:, t, :], 1.0, 0.0, ALU.mult, ALU.add,
                                          SS[:, t:t + 1]))
        rstd(7, 2, D)
        for t in range(XT):
            link(dve.scalar_tensor_tensor(out=HN[:, t, :], in0=RES[:, t, :], scalar=RSTD[:, t:t + 1], in1=SCB,
                                          op0=ALU.mult, op1=ALU.mult))
            dve.tensor_tensor(HN[:, t, :], HN[:, t, :], SHB, ALU.add).then_inc(hn_done, 1)
        dve.wait_ge(logits_rdy, 1)
        L, EQ, CD, O1, L2, O2, AS = (LG[:, n, :, :] for n in range(7))
        M1, M2, I1, I2 = (LG[:, 7, :, 2 * n:2 * n + 1] for n in range(4))
        GT, GA, EB_ = LG[:, 8, :, 0:1], LG[:, 8, :, 1:2], LG[:, 8, :, 2:3]
        EX, DF = LG[:, 9, :, 0:1], LG[:, 9, :, 1:2]
        io8 = IOTA8.rearrange("p (t e) -> p t e", t=2)
        wide = [P, XT, NE]
        link(dve.tensor_copy(L, ps[:, 4, 0:16].rearrange("p (t e) -> p t e", t=2)))

        def first_max(lg, m, i_, oh):
            link(dve.tensor_reduce(m, lg, AX_X, ALU.max))
            link(dve.tensor_tensor(EQ, lg, m.broadcast_to(wide), ALU.is_equal))
            link(dve.tensor_tensor(CD, EQ, io8, ALU.mult))
            link(dve.tensor_reduce(i_, CD, AX_X, ALU.min))
            link(dve.tensor_tensor(oh, io8, i_.broadcast_to(wide), ALU.is_equal))

        first_max(L, M1, I1, O1)
        link(dve.scalar_tensor_tensor(out=L2, in0=O1, scalar=NEG, in1=L, op0=ALU.mult, op1=ALU.add))
        first_max(L2, M2, I2, O2)
        link(dve.tensor_tensor(AS, O1, O2, ALU.add))
        dve.sem_inc(assign_rdy, 1)
        link(dve.tensor_tensor(DF, M2, M1, ALU.subtract))
        dve.sem_inc(d_ready, 1)
        dve.wait_ge(e_ready, 1)
        link(dve.tensor_scalar(GT, EX, 1.0, None, ALU.add))
        link(dve.reciprocal(GA, GT))
        link(dve.tensor_tensor(EB_, GA, EX, ALU.mult))
        link(dve.tensor_tensor(EQ, O1, GA.broadcast_to(wide), ALU.mult))
        link(dve.tensor_tensor(CD, O2, EB_.broadcast_to(wide), ALU.mult))
        link(dve.tensor_tensor(G9[:], EQ, CD, ALU.add))
        link(dve.memset(PA[:], 0.0))
        dve.wait_ge(pos_rdy, 1)
        link(dve.tensor_copy(PA[:, 0:NE, 0, :], ps[:, 5, 0:16].rearrange("p (t e) -> p e t", t=2)))
        link(dve.tensor_copy(PA[:, 0:NE, 1, :], AS.rearrange("p t e -> p e t")))
        link(dve.tensor_reduce(GT[:, 0, :], ps[:, 5, 16:24], AX_X, ALU.max))
        link(dve.tensor_scalar(GT[:, 0, :], GT[:, 0, :], float(P), None, ALU.is_gt))
        link(dve.tensor_copy(CNT[0:1, 0:1], GT[0:1, 0, :]))
        dve.sem_inc(flag_rdy, 1)

        def experts(rnd):
            base = moe_base(rnd)
            n0 = 9 * rnd

            def onehot(src, n):
                dve.tensor_copy(CUR[:], src).then_inc(cur_done, 1)
                dve.wait_ge(cur_done, n)
                for t in range(XT):
                    ins = dve.tensor_scalar(ONEHOT[:, t, :], IOTA, CUR[:, 0, t:t + 1], CUR[:, 1, t:t + 1],
                                            ALU.is_equal, ALU.mult)
                ins.then_inc(onehot_rdy, 1)

            def hte(n):
                dve.wait_ge(hte_hi, n)
                dve.tensor_tensor(HTE[:, 1, :, :], ps[:, 2:4, :].rearrange("p b (k s) -> p (b k) s", k=4),
                                  HTE[:, 0, :, :].bitcast(F32), ALU.subtract).then_inc(hte_lo, 1)

            def ylo(n):
                dve.wait_ge(y_hi, n)
                dve.scalar_tensor_tensor(out=YS[:, 1, :].rearrange("p (a b) -> p a b", a=2), in0=ps[:, 4:6, :],
                                         scalar=GS[:, 0:1],
                                         in1=YS[:, 0, :].bitcast(F32).rearrange("p (a b) -> p a b", a=2),
                                         op0=ALU.mult, op1=ALU.subtract).then_inc(y_lo, 1)

            def accumulate(n, i):
                t, h = i // 2, i % 2
                dve.wait_ge(comb_rdy, n * 4 + (i + 1))
                dve.wait_ge(acc_done, n * 4 + (i + 1))
                o = YACC[:, t, 512 * h:512 * h + 512]
                dve.tensor_tensor(o, o, ps[:, 7, :], ALU.add).then_inc(acc_done, 1)

            if rnd:
                dve.wait_ge(gather_rdy, 9)
                dve.tensor_scalar(PA[:, :, 0, :], PA[:, :, 0, :], -float(P), None, ALU.add).then_inc(cur_done, 1)
                dve.wait_ge(cur_done, 10)
            else:
                dve.memset(YACC[:], 0.0).then_inc(acc_done, 1)
            dve.memset(PTR[:].bitcast(F32), 0.0)
            dve.memset(ps[:, 4:6, :], 0.0)
            dve.memset(GS[:], 0.0).then_inc(gs_done, 1)
            onehot(PA[:, 0, :, :], n0 + rnd + 1)
            hte(n0 + 1)
            with dve.Fori(0, NE) as e:
                J = EJ * NE * rnd + e * EJ
                for i in range(EB):
                    slot = (B_MOE + i) % SPL
                    dve.wait_ge(hi_done, base + e * EB + (i + 1))
                    dve.tensor_tensor(WLO[:, slot, :], WRAW[:, (B_MOE + i) % RAW, :], WHI[:, slot, :].bitcast(F32),
                                      ALU.subtract).then_inc(lo_done, 1)
                    if i == 2:
                        ylo(n0 + e + 1)
                    if 7 <= i < 11:
                        accumulate(n0 + e, i - 7)
                    if i == 15:
                        dve.wait_ge(pt_done, NE * rnd + e + 1)
                        dve.wait_ge(y_lo, n0 + e + 1)
                        dve.tensor_copy(GS[:], ps[:, 7, bass.ds(e + 2 * P, 1)]).then_inc(gs_done, 1)
                    if i == 21:
                        onehot(PA[:, bass.ds(e + 1, 1), :, :].rearrange("p o a t -> p (o a) t"), n0 + e + (rnd + 2))
                    for j in range(EJ):
                        if i == 4 * j + 6:
                            dve.wait_ge(silu_done, FG + J + (j + 1))
                            if j >= 2:
                                dve.wait_ge(tr_ready, J + (j - 1))
                            dve.tensor_tensor(ACTN[:, j % 2, :], SIL[:, j % 2, :], ps[:, 2 * (j % 2) + 1, :],
                                              ALU.mult).then_inc(act_done, 1)
                        if i == 4 * j + 9:
                            dve.wait_ge(act_hi, J + (j + 1))
                            dve.tensor_tensor(ACTT[:, 1, 4 * j:4 * j + 4, :],
                                              ps[:, 6, :].rearrange("p (k s) -> p k s", k=4),
                                              ACTT[:, 0, 4 * j:4 * j + 4, :].bitcast(F32),
                                              ALU.subtract).then_inc(act_lo, 1)
                    if i == 35:
                        hte(n0 + e + 2)
            ylo(n0 + 9)
            for i in range(4):
                accumulate(n0 + 8, i)
            dve.wait_ge(acc_done, (n0 + 9) * 4 + 1)

        experts(0)
        more = dve.value_load(CNT[0:1, 0:1], min_val=0, max_val=1)
        with dve.If(more > 0):
            experts(1)
        dve.end_ifs()

        fin = [0]

        def flink(ins):
            fin[0] += 1
            ins.then_inc(fin_chain, 1)
            dve.wait_ge(fin_chain, fin[0])

        gb, ngb, tmp, junk = POST[3]
        dve.wait_ge(gate_in, 160)
        flink(dve.tensor_tensor(gb[:, 0, :], gb[:, 0, :], ngb, ALU.mult))
        for t in range(XT):
            flink(dve.tensor_tensor_reduce(junk, YACC[:, t, :], YACC[:, t, :], 1.0, 0.0, ALU.mult, ALU.add,
                                           SS[:, t:t + 1]))
        rstd(8, 2, D, flink)
        for t in range(XT):
            flink(dve.scalar_tensor_tensor(out=tmp, in0=YACC[:, t, :], scalar=RSTD[:, t:t + 1], in1=gb[:, 0, :],
                                           op0=ALU.mult, op1=ALU.mult))
            flink(dve.tensor_tensor(RES[:, t, :], RES[:, t, :], tmp, ALU.add))
            dve.sem_inc(fin_rdy, 1)

    stack.close()


_INS = ["x", "c", "ctx", "c_ctx", "ada_w", "ada_b", "norm_g", "mix_in_w", "mix_out_w", "win_sink", "diff_qkv_w",
        "diff_out_w", "diff_lambda", "diff_subln_g", "ffn_in_w", "ffn_out_w", "router_w", "expert_in_w",
        "expert_out_w"]
_OUTS = [((1, 256, 1024), "float32")]


def kernel(**inputs):
    import numpy as _np
    import concourse.bacc as _bacc
    from concourse import mybir as _mybir
    from concourse.bass_utils import run_bass_kernel_spmd as _run

    nc = _bacc.Bacc("TRN2", target_bir_lowering=False, num_devices=1)
    arrays, args = {}, []
    for name in _INS + ["tables"]:
        a = constant_tables() if name == "tables" else _np.ascontiguousarray(inputs[name])
        arrays[f"in_{name}_dram"] = a
        args.append(nc.dram_tensor(f"in_{name}_dram", a.shape, _mybir.dt.from_np(a.dtype), kind="ExternalInput").ap())
    for i, (shape, dtype) in enumerate(_OUTS):
        dt = _mybir.dt.from_np(_np.dtype(dtype))
        args.append(nc.dram_tensor(f"out_{i}_dram", shape, dt, kind="ExternalOutput").ap())
    backbone(nc, *args)
    r = _run(nc, [arrays], core_ids=[0])
    got = tuple(r.results[0][f"out_{i}_dram"] for i in range(len(_OUTS)))
    return got[0]
```

```python
from contextlib import ExitStack
import math

import numpy as np

import concourse.bass as bass
from concourse import mybir

F32 = mybir.dt.float32
F32R = mybir.dt.float32r
I32 = mybir.dt.int32
ACT = mybir.ActivationFunctionType
ALU = mybir.AluOpType
AX_X = mybir.AxisListType.X

P = 128
D = 1024
DK = D // P
SEQ = 256
TILES = 4
XT = 2
EPS = 1e-6
NEG = -1e30
HD = 64
FFN = 2816
FG = FFN // 256
NE = 8
ED = 3584
EJ = ED // 512
SCALE = HD ** -0.5
LAM_INIT = 0.8 - 0.6 * math.exp(-0.3)

RAW = 6
SPL = 3
BLK = 2048

ADA_CH = 12
B_ADA0 = 0
B_MIXIN = 8
B_ATT0 = 13
B_MIXOUT = 37
B_FFNIN = 41
B_FFNOUT = B_FFNIN + 2 * FG
B_QKV = B_FFNOUT + FG
B_ATT1 = B_QKV + 12
B_DOUT = B_ATT1 + 16
B_MOE = B_DOUT + 4
IN_BLOCKS = 4 * EJ
OUT_BLOCKS = ED // 256
EB = IN_BLOCKS + OUT_BLOCKS
assert EB % RAW == 0 and EB % SPL == 0
ASP_AHEAD = 2
ATT0_CHUNKS = [2, 2, 2, 2, 1, 1, 1, 1]

T_ID, T_TRI, T_ROPE, T_DFT = 0, 128, 384, 576
T_MOE = T_DFT + 1280
T_ALL = T_MOE + 128 * 3 + 16


def constant_tables():
    t = np.zeros((P, T_ALL), np.float64)
    r = np.arange(P)
    t[:, T_ID:T_ID + P] = np.eye(P)
    t[:, T_TRI:T_TRI + P] = np.where(r[None, :] > r[:, None], NEG, 0)
    t[:, T_TRI + P:T_TRI + 2 * P] = np.where(r[None, :] < r[:, None], NEG, 0)
    inv = np.float32(10000.0) ** (-np.arange(0, 32, 2, dtype=np.float32) / np.float32(32))
    for tile in range(XT):
        tok = tile * P + r
        for axis, pos in enumerate((tok // 64, tok % 64)):
            ang = (pos[:, None].astype(np.float32) * inv[None, :]).astype(np.float64)
            at = T_ROPE + tile * 32 + axis * 16
            t[:, at:at + 16] = np.cos(ang)
            t[:, at + 64:at + 80] = np.sin(ang)
            t[:, at + 128:at + 144] = -np.sin(ang)
    lp = np.arange(SEQ)
    for c in range(2):
        ang = 2 * np.pi * (((c * P + r)[:, None] * lp[None, :]) % SEQ) / SEQ
        t[:, T_DFT + c * 512:T_DFT + c * 512 + 256] = np.cos(ang)
        t[:, T_DFT + c * 512 + 256:T_DFT + c * 512 + 512] = np.sin(ang)
    ang = 2 * np.pi * ((r[:, None] * r[None, :]) % P) / P
    norm = 1 / math.sqrt(SEQ * P)
    t[:, T_DFT + 1024:T_DFT + 1152] = np.cos(ang) * norm
    t[:, T_DFT + 1152:T_DFT + 1280] = -np.sin(ang) * norm
    t[:, T_MOE:T_MOE + P] = r[:, None] < r[None, :]
    t[:, T_MOE + P:T_MOE + 2 * P] = 1
    t[:, T_MOE + 2 * P:T_MOE + 3 * P] = r[None, :]
    t[:, T_MOE + 3 * P:] = np.tile(np.arange(8) - 8, 2)[None, :]
    return t.astype(np.float32)


def backbone(nc, x, c, ctx_in, c_ctx, ada_w, ada_b, norm_g, mix_in_w, mix_out_w, win_sink, diff_qkv_w,
             diff_out_w, diff_lambda, diff_subln_g, ffn_in_w, ffn_out_w, router_w, expert_in_w,
             expert_out_w, tables, out):
    stack = ExitStack()

    def sb(name, shape, dt=F32):
        return stack.enter_context(nc.sbuf_tensor(name, shape, dt))

    RES = sb("residual", [P, TILES, D])
    WRAW = sb("w_raw", [P, RAW, BLK])
    WHI = sb("w_hi", [P, SPL, BLK], F32R)
    WLO = sb("w_lo", [P, SPL, BLK], F32R)
    ID = sb("ident", [P, P])
    CST = sb("cond_stationary", [P, DK, P], F32R)
    MROW = sb("mod_rows", [40, 2, P])
    COL = sb("mod_cols", [P, 40])
    ACOL = sb("scale_cols", [P, 2, DK])
    SS = sb("sumsq", [P, 16])
    MS = sb("meansq", [P, 16])
    STD = sb("std", [P, 16])
    Y0 = sb("rstd0", [P, 16])
    Y1 = sb("rstd_tmp", [P, 16])
    RSTD = sb("rstd", [P, 16])
    SINK = sb("sink", [P, 8])
    MX = sb("row_max", [P, 4])
    NEGM = sb("neg_max", [P, 4])
    TS = sb("sink_shifted", [P, 4])
    ES = sb("sink_exp", [P, 4])
    SUMS = sb("row_sums", [P, 4])
    RL = sb("row_recip", [P, 4])
    NRL = sb("row_recip_lam", [P, 4])
    LAM = sb("lam", [P, 4])
    GSUB = sb("subln_col", [P, 2])
    CNT = sb("overflow", [1, 1], I32)

    RW = sb("router", [P, DK, NE])
    LG = sb("logits", [P, 10, XT, NE])
    G9 = sb("gates", [P, XT, NE])
    PA = sb("pos_assign", [P, NE + 1, 2, XT])
    CUR = sb("cur_pa", [P, 2, XT])
    GS = sb("gate_slot", [P, 1])

    def area(*specs):
        with ExitStack() as s:
            return [s.enter_context(nc.sbuf_tensor(n, sh, dt)) for n, sh, dt in specs]

    W0 = 8192
    HT, WORK, MODB, T2 = area(("h_t", [P, 2, DK, 512], F32R), ("work", [P, 12288], F32),
                              ("mod_buf", [P, 1536], F32), ("tables", [P, 512], F32))
    _, ASP = area(("pad_a", [P, W0 + 12288], F32), ("act_split", [P, 2, 2, 512], F32R))
    ZT, P1, PT1, ADAX = area(("z_t1", [P, 2, DK, 256], F32R), ("p1", [P, 4, 512], F32), ("pt1", [P, 4, 256], F32),
                             ("ada_rows", [P, 2, 512], F32))
    (HTE, YS, PTR, YACC, ONEHOT, SIL, TM) = area(
        ("h_te", [P, 2, DK, P], F32R), ("y_split", [P, 2, D], F32R), ("onehot_t", [P, 2 * P], F32R),
        ("y_acc", [P, XT, D], F32), ("onehot", [P, XT, P], F32), ("silu_g", [P, 2, 512], F32),
        ("moe_tables", [P, 400], F32))
    _, ACTT, ACTN, HN = area(("pad_b", [P, W0 + 4096], F32), ("act_t", [P, 2, ED // P, P], F32R),
                             ("act_n", [P, 2, 512], F32), ("h_nat", [P, XT, D], F32))
    _, HTF = area(("pad_c", [P, W0 + 4096], F32), ("h_tf", [P, DK, 256], F32))

    def act_split(part, k):
        return ASP[:, part, k, :] if k < 2 else HT[:, part, (k - 2) % 8, :]

    def work(off, *dims):
        n = int(np.prod(dims))
        v = WORK[:, off:off + n]
        if len(dims) == 1:
            return v
        names = "abcd"[:len(dims)]
        return v.rearrange(f"p ({' '.join(names)}) -> p {' '.join(names)}",
                           **{k: d for k, d in zip(names[1:], dims[1:])})

    F_N = work(0, TILES, 512)
    V0 = work(2048, TILES, P)
    QT0 = work(2560, 4, 512)
    KT0 = work(4608, 512)
    PR0 = work(5120, 4, 512)
    PT0 = work(7168, 4, 512)
    DFT = work(9216, 1280)
    AT0 = work(5120, 2, 512)
    K_N = work(6144, TILES, P)
    ROT0 = work(6656, 512)
    QROT = work(10496, 512)
    Q_N = work(7168, TILES, 512)
    ACTF = work(0, FFN // P, 512)
    SILF = work(11264, 2, 512)
    V1 = work(0, TILES, D)
    QT1 = work(4096, DK, 256)
    KT1 = work(6144, DK, 512)
    NAT = work(10240, TILES, 512)
    OA = work(10240, XT, D)
    ROT1 = MODB[:, 0:512]
    XN = {0: work(5120, TILES, D), 1: work(0, TILES, D), 2: work(4096, TILES, D)}
    TF = {0: work(0, 2, 512), 1: work(4096, 2, 512), 2: work(8192, 2, 512)}
    JUNK0 = work(1024, D)
    POST = {0: (work(5120, 2, D), work(7168, D), work(8192, D), work(9216, D)),
            1: (work(0, 2, D), work(2048, D), work(11264, D), work(3072, D)),
            2: (work(6144, 1, D), work(7168, D), work(8192, D), work(9216, D)),
            3: (work(0, 1, D), work(1024, D), work(2048, D), work(3072, D))}
    SCB, SHB, NGB = work(0, D), work(1024, D), work(2048, D)
    BI = MODB[0:2, 512:1024]

    def ada_rows(q):
        if q % 2 == 0:
            return MODB[0:2, 0:512], MODB[0:2, 1024:1536]
        if q < 16:
            return work(11008, 512)[0:2, :], work(11520, 512)[0:2, :]
        return ADAX[0:2, 0, :], ADAX[0:2, 1, :]

    TRI, ROPE = T2[:, 0:256], T2[:, 256:448]
    UPPER, ONES, IOTA, IOTA8 = TM[:, 0:P], TM[:, P:2 * P], TM[:, 2 * P:3 * P], TM[:, 3 * P:3 * P + 16]

    mod = nc.dram_tensor("mod_scratch", [2, 2, 6 * D], F32, kind="Internal").ap()
    ps = stack.enter_context(nc.psum_tensor("ps", [P, 8, 512], F32))

    def sem(name):
        return stack.enter_context(nc.semaphore(name))

    rows_in = [sem(f"rows_in{i}") for i in range(3)]
    mod_stored = [sem(f"mod_stored{i}") for i in range(2)]
    landed = [sem(f"landed{i}") for i in range(RAW)]
    (hi_done, lo_done, used, res_in, tab_in, crow_in, crow_silu, cond_tr, cond_hi, cond_lo, 
     ada_shift, ada_row, bias_in, cols_read, prod_done, rstd_ready, cols_tr, ms_ready, std_ready, xn_ready, norm_tr,
     tf_ready, ht_hi, ht_lo, dch, f_copied, q_ctx, kv_ctx, kv_x, q_x, qk_tr, qk_evac, dft1, at_ready, dft2,
     z_hi, z_lo, scores, negmax, exps, prob_scaled, p_tr, pt_even, pt_odd, pv_done, sq_done, gate_in,
     post_done, silu_done, act_done, asp_hi, asp_lo, asp_half, nat_ctx, nat_x, nat_tr, nat_evac, v_even,
     v_odd, small_in, lam_dve, lam_exp, o_raw, o_norm, o_tr, lam_in, hn_done, h_tr, h_evac, logits_rdy, d_ready, e_ready,
     assign_rdy, pos_rdy, flag_rdy, onehot_rdy, gather_rdy, hte_hi, hte_lo, tr_ready, act_hi, act_lo,
     y_hi, y_lo, ptt_ready, pt_done, gs_done, comb_rdy, acc_done, cur_done, fin_chain, out_done,
     fin_rdy, moe_in) = [sem(n) for n in (
        "hi_done lo_done used res_in tab_in crow_in crow_silu cond_tr cond_hi cond_lo "
        "ada_shift ada_row bias_in cols_read prod_done rstd_ready cols_tr ms_ready std_ready xn_ready norm_tr "
        "tf_ready ht_hi ht_lo dch f_copied q_ctx kv_ctx kv_x q_x qk_tr qk_evac dft1 at_ready dft2 "
        "z_hi z_lo scores negmax exps prob_scaled p_tr pt_even pt_odd pv_done sq_done gate_in "
        "post_done silu_done act_done asp_hi asp_lo asp_half nat_ctx nat_x nat_tr nat_evac v_even "
        "v_odd small_in lam_dve lam_exp o_raw o_norm o_tr lam_in hn_done h_tr h_evac logits_rdy d_ready e_ready "
        "assign_rdy pos_rdy flag_rdy onehot_rdy gather_rdy hte_hi hte_lo tr_ready act_hi act_lo "
        "y_hi y_lo ptt_ready pt_done gs_done comb_rdy acc_done cur_done fin_chain out_done "
        "fin_rdy moe_in").split()]

    def cols512(w, k0, c0):
        return [(w[k0 * P:(k0 + 4) * P, c0:c0 + 512].rearrange("(k p) n -> p k n", p=P), (4, 512), 0, P)]

    def rows256(w, k0):
        return [(w[k0 * P:(k0 + 2) * P, 0:D].rearrange("(k p) n -> p k n", p=P), (2, D), 0, P)]

    def ada_chunk(q):
        w = ada_w[q // ADA_CH]
        return [cols512(w, 4 * h, 512 * (q % ADA_CH)) for h in range(2)]

    blocks = []
    for q in range(4):
        blocks += ada_chunk(q)
    mw = mix_in_w[0]
    for n in range(2):
        blocks += [cols512(mw, 4 * h, 512 * n) for h in range(2)]
    blocks.append([(mw[:, 1024:1280].rearrange("(k p) n -> p k n", p=P), (8, 256), 0, P)])
    for q in range(4, 16):
        blocks += ada_chunk(q)
    for n in range(2):
        blocks += cols512(mix_out_w[0], 0, 512 * n),
        src = mix_out_w[0, 512:1024, 512 * n:512 * n + 512].rearrange("(g j d) n -> g d j n", g=2, j=4)
        blocks.append([(src[g], (4, 512), HD * g, HD) for g in range(2)])
    for i in range(FG):
        for h in range(2):
            blocks.append([(ffn_in_w[0, 512 * h:512 * h + 512, FFN * u + 256 * i:FFN * u + 256 * i + 256]
                            .rearrange("(k p) n -> p k n", p=P), (4, 2, 256, u), 0, P) for u in range(2)])
    for m in range(FG):
        blocks.append(rows256(ffn_out_w[0], 2 * m))
    for n in range(6):
        blocks += [cols512(diff_qkv_w[0], 4 * h, 512 * n) for h in range(2)]
    for q in range(16, 24):
        blocks += ada_chunk(q)
    for n in range(2):
        blocks += [cols512(diff_out_w[0], 4 * h, 512 * n) for h in range(2)]
    assert len(blocks) == B_MOE

    def slot_view(slot, dims, p0, pn):
        v = WRAW[p0:p0 + pn, slot, :]
        if len(dims) == 4:
            return v.rearrange("p (k u n) -> p k u n", k=dims[0], u=2)[:, :, dims[3], :]
        return v.rearrange("p (k n) -> p k n", k=dims[0])

    land_at, total = [], [0] * RAW
    for b, parts in enumerate(blocks):
        total[b % RAW] += 16 * len(parts)
        land_at.append(total[b % RAW])

    def moe_base(rnd):
        return B_MOE + NE * EB * rnd

    def moe_landed(rnd, x_, i):
        s = (B_MOE + i) % RAW
        firsts = [j for j in range(EB) if (B_MOE + j) % RAW == s]
        per = sum(16 * moe_parts(j) for j in firsts)
        upto = sum(16 * moe_parts(j) for j in firsts if j <= i)
        return total[s] + rnd * NE * per + x_ * per + upto

    def moe_parts(i):
        return 2 if i < IN_BLOCKS else 1

    ATT0_U = [B_ATT0 + 2 * sum(ATT0_CHUNKS[:g]) for g in range(9)]
    ATT1_U = [B_ATT1 + 2 * g for g in range(9)]

    def ada_end(q):
        if q < 4:
            return 2 * q + 2
        return (B_ATT0 + 2 * (q - 4) if q < 16 else B_ATT1 + 2 * (q - 16)) + 2

    def wait_stored(eng, n):
        eng.wait_ge(mod_stored[0], 16 * ((n + 1) // 2))
        eng.wait_ge(mod_stored[1], 16 * (n // 2))

    UNIT_BANK = {0: ((1, 2, 3, 0), (4, 5, 6, 7)), 1: ((1, 2, 3, 0), (4, 5, 6, 7)), 2: ((1, 2, 3, 0), (2, 3, 6, 7))}

    block = stack.enter_context(nc.Block())

    @block.sync
    def _(sp):
        sp.dma_start(MROW[0:8, 0, :], c[0].rearrange("(k p) -> k p", p=P)).then_inc(crow_in, 16)
        sp.dma_start(MROW[8:16, 0, :], c_ctx.rearrange("(k p) -> k p", p=P)).then_inc(crow_in, 16)
        sp.dma_start(ID[:], tables[:, T_ID:T_ID + P]).then_inc(crow_in, 16)
        for b, parts in enumerate(blocks):
            if b >= RAW:
                sp.wait_ge(lo_done, b - RAW + 1)
            for src, dims, p0, pn in parts:
                sp.dma_start(slot_view(b % RAW, dims, p0, pn), src).then_inc(landed[b % RAW], 16)
            if b == 4:
                for t in range(TILES):
                    src = (x if t < XT else ctx_in)[0, (t % 2) * P:(t % 2 + 1) * P, :]
                    sp.dma_start(RES[:, t, :], src).then_inc(res_in, 16)

        def experts(rnd):
            with sp.Fori(0, NE) as e:
                for i in range(EB):
                    slot = (B_MOE + i) % RAW
                    sp.wait_ge(lo_done, moe_base(rnd) + e * EB + (i - RAW + 1))
                    if i < IN_BLOCKS:
                        j, k0 = i // 4, 2 * (i % 4)
                        for u in range(2):
                            src = expert_in_w[0, e, k0 * P:(k0 + 2) * P, ED * u + 512 * j:ED * u + 512 * j + 512]
                            sp.dma_start(slot_view(slot, (2, 2, 512, u), 0, P),
                                         src.rearrange("(k p) n -> p k n", p=P)).then_inc(landed[slot], 16)
                    else:
                        k0 = 2 * (i - IN_BLOCKS)
                        src = expert_out_w[0, e, k0 * P:(k0 + 2) * P, :].rearrange("(k p) n -> p k n", p=P)
                        sp.dma_start(slot_view(slot, (2, D), 0, P), src).then_inc(landed[slot], 16)

        experts(0)
        sp.wait_ge(flag_rdy, 1)
        more = sp.value_load(CNT[0:1, 0:1], min_val=0, max_val=1)
        with sp.If(more > 0):
            experts(1)
        sp.end_ifs()
        for t in range(XT):
            sp.wait_ge(fin_rdy, t + 1)
            sp.dma_start(out[0, t * P:(t + 1) * P, :], RES[:, t, :]).then_inc(out_done, 16)
        sp.wait_ge(out_done, 16 * XT)

    @block.gpsimd
    def _(pool):
        def bias(q):
            if q:
                pool.wait_ge(ada_row, q)
            src = ada_b[q // ADA_CH:q // ADA_CH + 1, 512 * (q % ADA_CH):512 * (q % ADA_CH) + 512]
            pool.dma_start(BI, src.broadcast_to([2, 512])).then_inc(bias_in, 16)

        def store(q):
            pool.wait_ge(ada_row, q + 1)
            dst = mod[q // ADA_CH, :, 512 * (q % ADA_CH):512 * (q % ADA_CH) + 512]
            pool.dma_start(dst, ada_rows(q)[0]).then_inc(mod_stored[q % 2], 16)

        def mod_rows(s):
            layer, piece, gi, need = [(0, 0, 0, 4), (0, 3, 2, 16), (1, 0, 0, 16)][s]
            wait_stored(pool, need)
            if s == 2:
                pool.wait_ge(cols_tr, 1)
            for st in range(2):
                src = mod[layer, st, piece * D:(piece + 2) * D].rearrange("(k p) -> k p", p=P)
                pool.dma_start(MROW[16 * st:16 * st + 16, s % 2, :], src).then_inc(rows_in[s], 16)
            pool.dma_start(MROW[32:40, s % 2, :], norm_g[layer, gi].rearrange("(k p) -> k p", p=P)).then_inc(rows_in[s], 16)

        def gate_rows(p):
            layer, piece, gi = [(0, 2, 1), (0, 5, 3), (1, 2, 1), (1, 5, 3)][p]
            gb, ngb = POST[p][0], POST[p][1]
            for st in range(gb.shape[1]):
                src = mod[layer, st:st + 1, piece * D:(piece + 1) * D]
                pool.dma_start(gb[:, st, :], src.broadcast_to([P, D])).then_inc(gate_in, 16)
            pool.dma_start(ngb, norm_g[layer, gi:gi + 1, :].broadcast_to([P, D])).then_inc(gate_in, 16)

        bias(0)
        pool.dma_start(T2[:, 0:448], tables[:, T_TRI:T_TRI + 448]).then_inc(tab_in, 16)
        pool.dma_start(DFT, tables[:, T_DFT:T_DFT + 1280]).then_inc(tab_in, 16)
        pool.dma_start(SINK[:], win_sink.broadcast_to([P, 8])).then_inc(tab_in, 16)
        pool.dma_start(GSUB[:, 0:1], diff_subln_g.rearrange("a p -> p a")).then_inc(small_in, 16)
        pool.dma_start(RW[:], router_w[0].rearrange("(k p) e -> p k e", p=P)).then_inc(small_in, 16)
        for q in range(4):
            store(q)
            bias(q + 1)
        pool.wait_ge(cond_hi, 1)
        mod_rows(0)
        for q in range(4, 16):
            store(q)
            if q < 15:
                bias(q + 1)
        mod_rows(1)
        mod_rows(2)
        pool.wait_ge(pv_done, 8)
        gate_rows(0)
        pool.wait_ge(used, B_FFNOUT + 5)
        gate_rows(1)
        pool.wait_ge(used, B_QKV)
        pool.dma_start(ROPE, tables[:, T_ROPE:T_ROPE + 192]).then_inc(tab_in, 16)
        lam_row = diff_lambda.rearrange("a b d -> a (b d)")
        pool.dma_start(T2[:, 0:256], lam_row.broadcast_to([P, 256])).then_inc(lam_in, 16)
        bias(16)
        for q in range(16, 24):
            store(q)
            if q < 23:
                bias(q + 1)
        wait_stored(pool, 24)
        pool.wait_ge(pv_done, 16)
        gate_rows(2)
        pool.dma_start(SCB, mod[1, 0:1, 4 * D:5 * D].broadcast_to([P, D])).then_inc(moe_in, 16)
        pool.dma_start(SHB, mod[1, 0:1, 3 * D:4 * D].broadcast_to([P, D])).then_inc(moe_in, 16)
        pool.dma_start(NGB, norm_g[1, 2:3, :].broadcast_to([P, D])).then_inc(moe_in, 16)
        pool.wait_ge(post_done, 10)
        pool.dma_start(TM[:], tables[:, T_MOE:T_MOE + 400]).then_inc(moe_in, 16)
        pool.wait_ge(hn_done, 2)
        gate_rows(3)

    @block.scalar
    def _(act):
        at = [0]

        def hi_upto(n):
            for b in range(at[0], min(n, B_MOE)):
                act.wait_ge(landed[b % RAW], land_at[b])
                if b >= SPL:
                    act.wait_ge(used, b - SPL + 1)
                act.activation(WHI[:, b % SPL, :], WRAW[:, b % RAW, :], ACT.Copy).then_inc(hi_done, 1)
            at[0] = max(at[0], n)

        event, squared = [0], [0]

        def sqrt(c0, n):
            event[0] += 1
            act.wait_ge(ms_ready, event[0])
            act.activation(STD[:, c0:c0 + n], MS[:, c0:c0 + n], ACT.Sqrt).then_inc(std_ready, 1)

        def square(src, junk, col):
            if squared[0]:
                act.wait_ge(sq_done, squared[0])
            squared[0] += 1
            act.activation(junk, src, ACT.Square, accum_out=SS[:, col:col + 1]).then_inc(sq_done, 1)

        def shift(q):
            act.wait_ge(used, ada_end(q))
            if q >= 2:
                act.wait_ge(mod_stored[q % 2], 16 * (q // 2))
            hi, lo = ada_rows(q)
            act.activation(hi, ps[0:2, 7, :], ACT.Copy)
            act.activation(lo, ps[32:34, 7, :], ACT.Copy).then_inc(ada_shift, 1)

        def norm_hi(s, st):
            for u in range(4):
                n = 8 * s + 4 * st + u
                act.wait_ge(tf_ready, n + 1)
                act.activation(HT[:, 0, 2 * u:2 * u + 2, 256 * st:256 * st + 256],
                               TF[s][:, n % 2, :].rearrange("p (k t) -> p k t", k=2), ACT.Copy).then_inc(ht_hi, 1)

        def square_products(p, tiles):
            for t in tiles:
                square(ps[:, 2 * t:2 * t + 2, :], POST[p][3].rearrange("p (a b) -> p a b", a=2), t)

        def xn(s, event_n, tiles):
            act.wait_ge(rstd_ready, event_n)
            for t in tiles:
                act.activation(XN[s][:, t, :], RES[:, t, :], ACT.Copy, scale=RSTD[:, 4 + t:5 + t]).then_inc(xn_ready, 1)

        def boundary(p, first):
            s = p + 1
            for st in range(2):
                tiles = (2 * st, 2 * st + 1)
                if st == 0:
                    hi_upto(first + 1)
                act.wait_ge(prod_done, p + 1) if st == 0 else act.wait_ge(used, first)
                square_products(p, tiles)
                if st == 1:
                    norm_hi(s, 0)
                    hi_upto(first + SPL)
                sqrt(2 * st, 2)
                for t in tiles:
                    act.wait_ge(post_done, 4 * p + t + 1)
                    square(RES[:, t, :], POST[p][3], 4 + t)
                sqrt(4 + 2 * st, 2)
                xn(s, 2 * p + st + 2, tiles)
                if st == 0:
                    hi_upto(first + 2)
            norm_hi(s, 1)

        def act_hi_part(k):
            act.wait_ge(act_done, k // 2 + 1)
            if k >= 10:
                act.wait_ge(used, B_FFNOUT + (k - 8) // 2 + 1)
            elif k >= 2:
                act.wait_ge(used, B_FFNOUT)
            act.activation(act_split(0, k), ACTF[:, k, :], ACT.Copy).then_inc(asp_hi, 1)

        act.wait_ge(crow_in, 48)
        act.activation(MROW[0:16, 1, :], MROW[0:16, 0, :], ACT.Silu).then_inc(crow_silu, 1)
        act.wait_ge(cond_tr, 1)
        act.wait_ge(dch, 1)
        act.activation(CST[:, :, 0:2], ps[:, 7, 0:16].rearrange("p (s k) -> p k s", s=2),
                       ACT.Copy).then_inc(cond_hi, 1)
        hi_upto(SPL)
        for q in range(4):
            hi_upto(2 * q + 2 + SPL)
            shift(q)
            if q == 2:
                act.wait_ge(res_in, 64)
                for t in range(TILES):
                    square(RES[:, t, :], JUNK0, 4 + t)
        sqrt(4, 4)
        xn(0, 1, range(TILES))
        for st in range(2):
            norm_hi(0, st)
        hi_upto(B_MIXIN + 2 + SPL)
        act.wait_ge(used, B_MIXIN + 2)
        act.activation(F_N, ps[:, 0:4, :], ACT.Copy).then_inc(f_copied, 1)
        hi_upto(B_MIXIN + 4 + SPL)
        act.wait_ge(used, B_MIXIN + 4)
        for t in range(2, 4):
            ins = act.activation(Q_N[:, t, :].rearrange("p (j g d) -> p g j d", g=2, j=4),
                                 ps[:, 4 + t, :].rearrange("p (g j d) -> p g j d", g=2, j=4), ACT.Copy)
        ins.then_inc(q_ctx, 1)
        hi_upto(B_MIXIN + 5 + SPL)
        act.wait_ge(used, B_MIXIN + 5)
        act.activation(K_N[:, 2:4, :], ps[:, 2:4, 0:P], ACT.Copy)
        act.activation(V0[:, 2:4, :], ps[:, 2:4, P:2 * P], ACT.Copy).then_inc(kv_ctx, 1)
        for n in range(9):
            if n < 8:
                act.wait_ge(dft1, n + 1)
                if n >= 2:
                    act.wait_ge(dft2, n - 1)
                act.activation(AT0[:, n % 2, :], ps[:, 4 + n % 2, :], ACT.Copy).then_inc(at_ready, 1)
            if n >= 1:
                u = n - 1
                act.wait_ge(dft2, u + 1)
                act.activation(HT[:, 0, u % 4, 256 * (u // 4):256 * (u // 4) + 256], ps[:, 6 + u % 2, 0:256],
                               ACT.Copy).then_inc(z_hi, 1)
        act.wait_ge(qk_tr, 1)
        act.activation(KT0, ps[:, 0, :], ACT.Copy).then_inc(qk_evac, 1)
        for j in range(4):
            act.wait_ge(qk_tr, j + 2)
            act.activation(QT0[:, j, :], ps[:, (j + 1) % 4, :], ACT.Copy).then_inc(qk_evac, 1)
        def exps0(g):
            nk = 512 if g < 4 else 256
            act.wait_ge(negmax, g + 1)
            if g:
                act.wait_ge(p_tr, 4 * min(g, 4) + 2 * max(g - 4, 0))
            for j in range(4):
                act.activation(PR0[:, j, 0:nk], ps[:, j, 0:nk], ACT.Exp, bias=NEGM[:, j:j + 1], scale=SCALE,
                               accum_out=SUMS[:, j:j + 1])
            act.activation(ES[:], TS[:], ACT.Exp).then_inc(exps, 1)

        exps0(0)
        qn = 4
        for g in range(8):
            u = ATT0_U[g]
            nk = 512 if g < 4 else 256
            base = 4 * min(g, 4) + 2 * max(g - 4, 0)
            hi_upto(u + 2 + SPL)
            shift(qn)
            for c_ in range(0, nk // P, 2):
                act.wait_ge(p_tr, base + c_ + 1)
                act.activation(PT0[:, c_, :], ps[:, 4, :], ACT.Copy).then_inc(pt_even, 1)
            if ATT0_CHUNKS[g] == 2:
                hi_upto(u + 3 + SPL)
            if g < 7:
                exps0(g + 1)
            if ATT0_CHUNKS[g] == 2:
                hi_upto(u + 4 + SPL)
                shift(qn + 1)
            qn += ATT0_CHUNKS[g]
            act.wait_ge(pv_done, g + 1)
            kv, t = g % 2, g // 2
            act.activation(HT[HD * kv:HD * kv + HD, 0, 4:8, t * P:t * P + P],
                           ps[HD * kv:HD * kv + HD, 6, :].rearrange("p (j q) -> p j q", j=4),
                           ACT.Copy).then_inc(z_hi, 1)
        hi_upto(B_MIXOUT + 2 + SPL)
        boundary(0, B_FFNIN)
        for i in range(FG):
            if i == FG - 1:
                act_hi_part(0)
                act_hi_part(1)
            hi_upto(B_FFNIN + 2 * i + 1 + SPL)
            hi_upto(B_FFNIN + 2 * i + 2 + SPL)
            act.wait_ge(used, B_FFNIN + 2 * i + 2)
            if i:
                act.wait_ge(act_done, i)
            b0 = 4 * (i % 2)
            act.activation(SILF, ps[:, b0:b0 + 2, :], ACT.Silu).then_inc(silu_done, 1)
        for m in range(-ASP_AHEAD, FG - 2 + 1):
            hi_upto(B_FFNOUT + m + SPL)
            for k in range(2 * (m + ASP_AHEAD), 2 * (m + ASP_AHEAD) + 2):
                if 2 <= k < 2 * FG:
                    act_hi_part(k)
        boundary(1, B_QKV)
        def nat_evac_q(n):
            act.wait_ge(nat_tr, n + 1)
            b0 = 4 * (n % 2)
            if n < 2:
                act.activation(QT1[:, 4 * n:4 * n + 4, :],
                               ps[:, b0 + 2:b0 + 4, :].rearrange("p b (j t) -> p (b j) t", j=2),
                               ACT.Copy).then_inc(nat_evac, 1)
            else:
                act.activation(KT1[:, 4 * (n - 2):4 * (n - 2) + 4, :], ps[:, b0:b0 + 4, :],
                               ACT.Copy).then_inc(nat_evac, 1)

        for n in range(6):
            b0 = 4 * (n % 2)
            hi_upto(B_QKV + 2 * n + 1 + SPL)
            hi_upto(B_QKV + 2 * n + 2 + SPL)
            act.wait_ge(used, B_QKV + 2 * n + 2)
            if n in (2, 3):
                act.wait_ge(nat_tr, n)
                act.activation(NAT[:, 2:4, :], ps[:, b0 + 2:b0 + 4, :], ACT.Copy).then_inc(nat_ctx, 1)
            if n >= 4:
                act.activation(V1[:, 0:2, 512 * (n - 4):512 * (n - 4) + 512], ps[:, b0:b0 + 2, :],
                               ACT.Copy).then_inc(v_even, 1)
            if 1 <= n <= 4:
                nat_evac_q(n - 1)
        act.wait_ge(lam_dve, 1)
        act.activation(LAM[:, 2:4], LAM[:, 0:2], ACT.Exp).then_inc(lam_exp, 1)
        def exps1(g):
            act.wait_ge(negmax, 8 + g + 1)
            if g:
                act.wait_ge(p_tr, 24 + 2 * g)
            for j in range(4):
                ins = act.activation(P1[:, j, :], ps[:, j, :], ACT.Exp, bias=NEGM[:, j:j + 1], scale=SCALE,
                                     accum_out=SUMS[:, j:j + 1])
            ins.then_inc(exps, 1)

        exps1(0)
        for g in range(8):
            u, t, hp = ATT1_U[g], g // 4, g % 4
            hi_upto(u + 2 + SPL)
            shift(16 + g)
            act.wait_ge(p_tr, 24 + 2 * g + 1)
            act.wait_ge(pv_done, 8 + g)
            act.activation(PT1[:, 0:2, :], ps[:, 4, :].rearrange("p (c q) -> p c q", c=2),
                           ACT.Copy).then_inc(pt_even, 1)
            if g < 7:
                exps1(g + 1)
            act.wait_ge(pv_done, 8 + g + 1)
            act.activation(OA[:, t, 256 * hp:256 * hp + 256], ps[:, 6, 0:256], ACT.Copy)
            if g:
                act.wait_ge(o_raw, g)
            for hh in range(2):
                n_ = t * 8 + 2 * hp + hh
                ins = act.activation(T2[:, P * hh:P * hh + P], ps[:, 6, P * hh:P * hh + P], ACT.Square,
                                     accum_out=SS[:, n_:n_ + 1])
            ins.then_inc(o_raw, 1)
            if g == 5:
                sqrt(0, 8)
        sqrt(8, 8)
        act.wait_ge(lam_dve, 2)
        for b in range(4):
            act.wait_ge(o_tr, b + 1)
            act.activation(ZT[:, 0, 2 * b:2 * b + 2, :], ps[:, b, :].rearrange("p (h t) -> p h t", h=2), ACT.Copy,
                           scale=GSUB[:, 1:2]).then_inc(z_hi, 1)
        hi_upto(B_DOUT + 2 + SPL)
        for t in range(XT):
            act.wait_ge(prod_done, 3) if t == 0 else act.wait_ge(used, B_MOE)
            square_products(2, (t,))
            sqrt(t, 1)
        for t in range(XT):
            act.wait_ge(post_done, 9 + t)
            square(RES[:, t, :], POST[2][3], 4 + t)
        sqrt(4, 2)
        act.wait_ge(h_tr, 1)
        act.activation(HTF[:].rearrange("p (b j) t -> p b (j t)", b=4), ps[:, 0:4, :], ACT.Copy).then_inc(h_evac, 1)
        act.wait_ge(d_ready, 1)
        act.activation(LG[:, 9, :, 0:1], LG[:, 9, :, 1:2], ACT.Exp).then_inc(e_ready, 1)

        def experts(rnd):
            base = moe_base(rnd)

            def hte(e):
                act.wait_ge(gather_rdy, 9 * rnd + e + 1)
                act.activation(HTE[:, 0, :, :], ps[:, 2:4, :].rearrange("p b (k s) -> p (b k) s", k=4),
                               ACT.Copy).then_inc(hte_hi, 1)

            def yhi(n, end):
                act.wait_ge(used, end)
                act.wait_ge(gs_done, n)
                act.activation(YS[:, 0, :].rearrange("p (a b) -> p a b", a=2), ps[:, 4:6, :], ACT.Copy,
                               scale=GS[:, 0:1]).then_inc(y_hi, 1)

            hte(0)
            with act.Fori(0, NE) as e:
                J = EJ * NE * rnd + e * EJ
                for i in range(EB):
                    s = (B_MOE + i) % RAW
                    act.wait_ge(landed[s], moe_landed(rnd, e, i))
                    act.wait_ge(used, base + e * EB + (i - SPL + 1))
                    act.activation(WHI[:, (B_MOE + i) % SPL, :], WRAW[:, s, :], ACT.Copy).then_inc(hi_done, 1)
                    if i == 2:
                        yhi(9 * rnd + e + 1, base + e * EB)
                    if i == 15:
                        act.wait_ge(ptt_ready, NE * rnd + e + 1)
                        act.activation(PTR[:], ps[:, 7, 0:2 * P], ACT.Copy).then_inc(pt_done, 1)
                    for j in range(EJ):
                        if i == 4 * j + 6:
                            act.wait_ge(used, base + e * EB + (4 * j + 4))
                            if j >= 2:
                                act.wait_ge(act_done, FG + J + (j - 1))
                            act.activation(SIL[:, j % 2, :], ps[:, 2 * (j % 2), :], ACT.Silu).then_inc(silu_done, 1)
                        if i == 4 * j + 9:
                            act.wait_ge(tr_ready, J + (j + 1))
                            act.activation(ACTT[:, 0, 4 * j:4 * j + 4, :],
                                           ps[:, 6, :].rearrange("p (k s) -> p k s", k=4),
                                           ACT.Copy).then_inc(act_hi, 1)
                    if i == 35:
                        hte(e + 1)
            yhi(9 * rnd + 9, base + NE * EB)

        experts(0)
        act.wait_ge(flag_rdy, 1)
        more = act.value_load(CNT[0:1, 0:1], min_val=0, max_val=1)
        with act.If(more > 0):
            experts(1)
        act.end_ifs()
        sqrt(4, 2)

    @block.tensor
    def _(pe):
        def mm(out_, l, r, first, last):
            return pe.matmul(out_, l, r, start=first, stop=last, skip_group_check=True)

        def split3(outs, lh, ll, whs, wls, first, last):
            for n, o in enumerate(outs):
                mm(o, lh, whs[n], first, False)
                mm(o, lh, wls[n], False, False)
            for n, o in enumerate(outs):
                ins = mm(o, ll, whs[n], False, last)
            return ins

        def ada(q, b):
            if q:
                pe.wait_ge(ada_shift, q)
            for h in range(2):
                pe.wait_ge(lo_done, b + h + 1)
                for k in range(4):
                    for w in (WHI, WLO):
                        v = w[:, (b + h) % SPL, :].rearrange("p (k n) -> p k n", k=4)
                        ins = mm(ps[:, 7, :], CST[:, 4 * h + k, :], v[:, k, :], h == 0 and k == 0 and w is WHI,
                                 h == 1 and k == 3 and w is WLO)
                ins.then_inc(used, 1)

        def norm_tr_stage(s, st):
            pe.wait_ge(xn_ready, 4 * s + 2 * st + 2)
            if st == 0:
                pe.wait_ge(rows_in[s], 48)
                pe.transpose(ps[:, 0, 0:40], MROW[0:40, s % 2, :], ID[0:40, 0:40]).then_inc(cols_tr, 1)
            elif s == 0:
                pe.wait_ge(ada_shift, 4)
            for u in range(4):
                if st == 0 and u == 3:
                    pe.wait_ge(cols_read, s + 1)
                bank = UNIT_BANK[s][st][u]
                for k in range(2):
                    for t in range(2):
                        ins = pe.transpose(ps[:, bank, 256 * k + P * t:256 * k + P * t + P],
                                           XN[s][:, 2 * st + t, (2 * u + k) * P:(2 * u + k + 1) * P], ID[:])
                ins.then_inc(norm_tr, 1)

        def linear(b, src, streams, banks, before=None, done=None, between=None,
                   step=1):
            for i, tiles in enumerate(streams):
                if before:
                    before(i)
                for h in range(2):
                    pe.wait_ge(lo_done, b + h + 1)
                    wh = WHI[:, (b + h) % SPL, :].rearrange("p (k n) -> p k n", k=4)
                    wl = WLO[:, (b + h) % SPL, :].rearrange("p (k n) -> p k n", k=4)
                    for k in range(4):
                        kk = 4 * h + k
                        if between and i == 0 and kk == 5:
                            between()
                        for t in tiles:
                            ins = split3([ps[:, banks + step * t, :]], src[:, 0, kk, t * P:(t + 1) * P],
                                         src[:, 1, kk, t * P:(t + 1) * P], [wh[:, k, :]], [wl[:, k, :]],
                                         kk == 0, kk == 7)
                    if i == len(streams) - 1:
                        ins.then_inc(used, 1)
                    elif h == 1 and done:
                        ins.then_inc(prod_done, 1)

        pe.wait_ge(crow_silu, 1)
        pe.transpose(ps[:, 7, 0:16], MROW[0:16, 1, :], ID[0:16, 0:16]).then_inc(cond_tr, 1)
        pe.wait_ge(cond_lo, 1)
        for q in range(4):
            ada(q, 2 * q)
        def wait_ht(s):
            return lambda st: pe.wait_ge(ht_lo, 8 * s + 4 * st + 4)

        norm_tr_stage(0, 0)
        linear(B_MIXIN, HT, [(0, 1), (2, 3)], 0, before=wait_ht(0), between=lambda: norm_tr_stage(0, 1))
        linear(B_MIXIN + 2, HT, [range(4)], 4)
        pe.wait_ge(f_copied, 1)
        b = B_MIXIN + 4
        pe.wait_ge(lo_done, b + 1)
        wh = WHI[:, b % SPL, :].rearrange("p (k n) -> p k n", k=8)
        wl = WLO[:, b % SPL, :].rearrange("p (k n) -> p k n", k=8)
        for t in range(TILES):
            for k in range(DK):
                ins = split3([ps[:, t, 0:256]], HT[:, 0, k, t * P:(t + 1) * P], HT[:, 1, k, t * P:(t + 1) * P],
                             [wh[:, k, :]], [wl[:, k, :]], k == 0, k == 7)
        ins.then_inc(used, 1)
        pe.wait_ge(tab_in, 48)
        pe.wait_ge(q_x, 1)
        pe.wait_ge(q_ctx, 1)
        for n in range(9):
            if n < 8:
                st, gr = n // 4, n % 4
                if n >= 2:
                    pe.wait_ge(at_ready, n - 1)
                for tt in range(2):
                    ins = mm(ps[:, 4 + n % 2, :], F_N[:, 2 * st + tt, gr * P:(gr + 1) * P],
                             DFT[:, 512 * tt:512 * tt + 512], tt == 0, tt == 1)
                ins.then_inc(dft1, 1)
            if n >= 1:
                u = n - 1
                pe.wait_ge(at_ready, u + 1)
                if u >= 2:
                    pe.wait_ge(z_lo, u - 1)
                mm(ps[:, 6 + u % 2, 0:256], DFT[:, 1024:1152], AT0[:, u % 2, 0:256], True, False)
                mm(ps[:, 6 + u % 2, 0:256], DFT[:, 1152:1280], AT0[:, u % 2, 256:512], False,
                   True).then_inc(dft2, 1)
        pe.wait_ge(kv_ctx, 1)
        pe.wait_ge(kv_x, 1)
        for t in range(TILES):
            ins = pe.transpose(ps[:, 0, t * P:(t + 1) * P], K_N[:, t, :], ID[:])
        ins.then_inc(qk_tr, 1)
        for j in range(4):
            if j == 3:
                pe.wait_ge(qk_evac, 1)
            for t in range(TILES):
                ins = pe.transpose(ps[:, (j + 1) % 4, t * P:(t + 1) * P], Q_N[:, t, j * P:(j + 1) * P], ID[:])
            ins.then_inc(qk_tr, 1)

        def scores0(g):
            t, kv = g // 2, g % 2
            p0 = HD * kv
            if g == 0:
                pe.wait_ge(qk_evac, 5)
            else:
                pe.wait_ge(exps, g)
            for j in range(4):
                q_ = QT0[p0:p0 + HD, j, t * P:(t + 1) * P]
                if t < XT:
                    mm(ps[:, j, :], q_, KT0[p0:p0 + HD, :], True, False)
                    far = P * (1 - t)
                    ins = mm(ps[:, j, far:far + P], ID[:], TRI[:, P * t:P * t + P], False, True)
                else:
                    ins = mm(ps[:, j, 0:256], q_, KT0[p0:p0 + HD, 256:512], True, True)
            ins.then_inc(scores, 1)

        scores0(0)
        pe.wait_ge(z_lo, 8)
        qn = 4
        trs = 0
        for g in range(8):
            u = ATT0_U[g]
            t, kv = g // 2, g % 2
            ada(qn, u)
            if g < 7:
                scores0(g + 1)
            pe.wait_ge(prob_scaled, g + 1)
            nk = 4 if g < 4 else 2
            for c_ in range(nk):
                if trs + c_ >= 2:
                    n_before = (trs + c_) // 2
                    pe.wait_ge(pt_even if c_ % 2 == 0 else pt_odd, n_before)
                for j in range(4):
                    ins = pe.transpose(ps[:, 4 + c_ % 2, j * P:(j + 1) * P], PR0[:, j, c_ * P:(c_ + 1) * P], ID[:])
                ins.then_inc(p_tr, 1)
            trs += nk
            if ATT0_CHUNKS[g] == 2:
                ada(qn + 1, u + 2)
            qn += ATT0_CHUNKS[g]
            pe.wait_ge(z_lo, 8 + g)
            for c_ in range(nk):
                pe.wait_ge(pt_even if c_ % 2 == 0 else pt_odd, (trs - nk) // 2 + c_ // 2 + 1)
                tk = c_ if g < 4 else c_ + 2
                ins = mm(ps[HD * kv:HD * kv + HD, 6, :], V0[:, tk, HD * kv:HD * kv + HD], PT0[:, c_, :],
                         c_ == 0, c_ == nk - 1)
            ins.then_inc(pv_done, 1)
        pe.wait_ge(z_lo, 16)
        linear(B_MIXOUT, HT, [range(4)], 0, step=2)
        linear(B_MIXOUT + 2, HT, [(0, 1), (2, 3)], 1, done=True, step=2)
        norm_tr_stage(1, 0)
        for i in range(FG):
            if i >= 2:
                pe.wait_ge(act_done, i - 1)
            b0 = 4 * (i % 2)
            parts = ((0, 256), (256, 512)) if i == 0 else ((0, 512),)
            for part, (t0, t1) in enumerate(parts):
                if i == 0:
                    wait_ht(1)(part)
                for h in range(2):
                    b = B_FFNIN + 2 * i + h
                    pe.wait_ge(lo_done, b + 1)
                    wh = WHI[:, b % SPL, :].rearrange("p (k u n) -> p k u n", k=4, u=2)
                    wl = WLO[:, b % SPL, :].rearrange("p (k u n) -> p k u n", k=4, u=2)
                    for k in range(4):
                        kk = 4 * h + k
                        if i == 0 and part == 0 and kk == 5:
                            norm_tr_stage(1, 1)
                        for u in range(2):
                            for f in range(2):
                                o = ps[:, b0 + 2 * u + f, t0:t1]
                                mm(o, wh[:, k, u, f * P:(f + 1) * P], HT[:, 0, kk, t0:t1], kk == 0, False)
                                mm(o, wh[:, k, u, f * P:(f + 1) * P], HT[:, 1, kk, t0:t1], False, False)
                                ins = mm(o, wl[:, k, u, f * P:(f + 1) * P], HT[:, 0, kk, t0:t1], False, kk == 7)
                    if part == len(parts) - 1:
                        ins.then_inc(used, 1)

        def second_product(m, tiles):
            b = B_FFNOUT + m
            pe.wait_ge(lo_done, b + 1)
            wh = WHI[:, b % SPL, :].rearrange("p (k n) -> p k n", k=4)
            wl = WLO[:, b % SPL, :].rearrange("p (k n) -> p k n", k=4)
            for k in range(2):
                kk = 2 * m + k
                pe.wait_ge(asp_lo, kk + 1)
                for t in (2, 3, 0, 1) if kk == 0 else tiles:
                    if kk == 0 and t == 0:
                        pe.wait_ge(act_done, FG)
                    ins = split3([ps[:, 2 * t + n, :] for n in range(2)], act_split(0, kk)[:, t * P:(t + 1) * P],
                                 act_split(1, kk)[:, t * P:(t + 1) * P], [wh[:, 2 * k + n, :] for n in range(2)],
                                 [wl[:, 2 * k + n, :] for n in range(2)], kk == 0, kk == 2 * FG - 1)
            return ins

        for m in range(FG - 2):
            second_product(m, range(4)).then_inc(used, 1)
        for st in range(2):
            for m in (FG - 2, FG - 1):
                ins = second_product(m, (2 * st, 2 * st + 1))
                if st == 1:
                    ins.then_inc(used, 1)
            if st == 0:
                ins.then_inc(prod_done, 1)
        norm_tr_stage(2, 0)
        wait_ht(2)(0)

        def nat_transposes(n):
            b0 = 4 * (n % 2)
            if n < 2:
                pe.wait_ge(nat_x, n + 1)
                for j in range(4):
                    for t in range(XT):
                        ins = pe.transpose(ps[:, b0 + 2 + j // 2, (j % 2) * 256 + t * P:(j % 2) * 256 + t * P + P],
                                           NAT[:, t, j * P:(j + 1) * P], ID[:])
            else:
                pe.wait_ge(nat_x, n + 1)
                pe.wait_ge(nat_ctx, n - 1)
                for j in range(4):
                    for t in range(TILES):
                        ins = pe.transpose(ps[:, b0 + j, t * P:(t + 1) * P], NAT[:, t, j * P:(j + 1) * P], ID[:])
            ins.then_inc(nat_tr, 1)

        for n in range(6):
            if n >= 2:
                pe.wait_ge(nat_evac, n - 1)
            linear(B_QKV + 2 * n, HT, [range(2) if n < 2 else range(4)], 4 * (n % 2))
            if n == 0:
                norm_tr_stage(2, 1)
                wait_ht(2)(1)
            if 1 <= n <= 4:
                nat_transposes(n - 1)
        pe.wait_ge(v_even, 2)
        pe.wait_ge(v_odd, 2)

        def scores1(g):
            t, hp = g // 4, g % 4
            if g:
                pe.wait_ge(exps, 8 + g)
            else:
                pe.wait_ge(nat_evac, 4)
            for j in range(4):
                h, p0 = 2 * hp + j // 2, HD * (j % 2)
                ins = mm(ps[:, j, :], QT1[p0:p0 + HD, h, t * P:(t + 1) * P], KT1[p0:p0 + HD, h, :], True, True)
            ins.then_inc(scores, 1)

        scores1(0)
        for g in range(8):
            ada(16 + g, ATT1_U[g])
            if g < 7:
                scores1(g + 1)
            pe.wait_ge(prob_scaled, 8 + g + 1)
            for hb in range(2):
                if g:
                    pe.wait_ge(pt_even if hb == 0 else pt_odd, 12 + g)
                for cc in range(2):
                    for hh in range(2):
                        o = ps[:, 4 + hb, cc * 256 + hh * P:cc * 256 + hh * P + P]
                        ins = pe.transpose(o, P1[:, 2 * hh, (2 * hb + cc) * P:(2 * hb + cc + 1) * P], ID[:])
                ins.then_inc(p_tr, 1)
            if g:
                pe.wait_ge(o_raw, g)
            pe.wait_ge(pt_even, 12 + g + 1)
            pe.wait_ge(pt_odd, 12 + g + 1)
            for hh in range(2):
                h = 2 * (g % 4) + hh
                for c_ in range(4):
                    ins = mm(ps[:, 6, hh * P:(hh + 1) * P], PT1[:, c_, hh * P:(hh + 1) * P],
                             V1[:, c_, h * P:(h + 1) * P], c_ == 0, c_ == 3)
            ins.then_inc(pv_done, 1)
        pe.wait_ge(o_norm, 2)
        for b_ in range(4):
            for hh in range(2):
                for t in range(XT):
                    h = 2 * b_ + hh
                    ins = pe.transpose(ps[:, b_, hh * 256 + t * P:hh * 256 + t * P + P],
                                       OA[:, t, h * P:(h + 1) * P], ID[:])
            ins.then_inc(o_tr, 1)
        pe.wait_ge(z_lo, 20)
        linear(B_DOUT, ZT, [range(2)], 0, step=2)
        linear(B_DOUT + 2, ZT, [(0,), (1,)], 1, done=True, step=2)
        pe.wait_ge(hn_done, 2)
        for k in range(DK):
            for t in range(XT):
                ins = pe.transpose(ps[:, k // 2, (k % 2) * 256 + t * P:(k % 2) * 256 + t * P + P],
                                   HN[:, t, k * P:(k + 1) * P], ID[:])
        ins.then_inc(h_tr, 1)
        pe.wait_ge(h_evac, 1)
        pe.wait_ge(small_in, 32)
        for t in range(XT):
            for k in range(DK):
                ins = mm(ps[:, 4, t * NE:(t + 1) * NE], HTF[:, k, t * P:(t + 1) * P], RW[:, k, :], k == 0, k == DK - 1)
        ins.then_inc(logits_rdy, 1)
        pe.wait_ge(assign_rdy, 1)
        pe.wait_ge(moe_in, 64)
        A0, A1 = LG[:, 6, 0, :], LG[:, 6, 1, :]
        mm(ps[:, 5, 0:8], UPPER, A0, True, True)
        mm(ps[:, 5, 8:16], ONES, A0, True, False)
        mm(ps[:, 5, 8:16], UPPER, A1, False, True)
        mm(ps[:, 5, 16:24], ONES, A0, True, False)
        mm(ps[:, 5, 16:24], ONES, A1, False, True).then_inc(pos_rdy, 1)

        def experts(rnd):
            base = moe_base(rnd)

            def gather(n):
                pe.wait_ge(onehot_rdy, n)
                for k in range(DK):
                    for t in range(XT):
                        ins = mm(ps[:, 2 + k // 4, (k % 4) * P:(k % 4 + 1) * P], HN[:, t, k * P:(k + 1) * P],
                                 ONEHOT[:, t, :], t == 0, t == XT - 1)
                ins.then_inc(gather_rdy, 1)

            def combine(n, i):
                t, h = i // 2, i % 2
                pe.wait_ge(acc_done, n * 4 + (i + 1))
                for q in range(2):
                    ins = mm(ps[:, 7, :], PTR[:, t * P:(t + 1) * P], YS[:, q, 512 * h:512 * h + 512], q == 0, q == 1)
                ins.then_inc(comb_rdy, 1)

            gather(9 * rnd + 1)
            with pe.Fori(0, NE) as e:
                J = EJ * NE * rnd + e * EJ
                for i in range(EB):
                    slot = (B_MOE + i) % SPL
                    wh = WHI[:, slot, :].rearrange("p (k n) -> p k n", k=4)
                    wl = WLO[:, slot, :].rearrange("p (k n) -> p k n", k=4)
                    if i == 0:
                        pe.wait_ge(hte_lo, 9 * rnd + e + 1)
                    if i < IN_BLOCKS:
                        j = i // 4
                        if i % 4 == 0 and j >= 2:
                            pe.wait_ge(act_done, FG + J + (j - 1))
                        pe.wait_ge(lo_done, base + e * EB + (i + 1))
                        for k in range(2):
                            kk = 2 * (i % 4) + k
                            ins = split3([ps[:, 2 * (j % 2), :], ps[:, 2 * (j % 2) + 1, :]], HTE[:, 0, kk, :],
                                         HTE[:, 1, kk, :], [wh[:, 2 * k + n, :] for n in range(2)],
                                         [wl[:, 2 * k + n, :] for n in range(2)], kk == 0, kk == 7)
                    else:
                        m = i - IN_BLOCKS
                        if m == 0:
                            pe.wait_ge(y_lo, 9 * rnd + e + 1)
                        pe.wait_ge(act_lo, J + (m // 2 + 1))
                        pe.wait_ge(lo_done, base + e * EB + (i + 1))
                        for k in range(2):
                            kk = 2 * m + k
                            ins = split3([ps[:, 4, :], ps[:, 5, :]], ACTT[:, 0, kk, :], ACTT[:, 1, kk, :],
                                         [wh[:, 2 * k + n, :] for n in range(2)],
                                         [wl[:, 2 * k + n, :] for n in range(2)], kk == 0, kk == ED // P - 1)
                    ins.then_inc(used, 1)
                    if 5 <= i < 9:
                        if i == 5:
                            pe.wait_ge(y_lo, 9 * rnd + e + 1)
                            pe.wait_ge(gs_done, 9 * rnd + e + 1)
                        combine(9 * rnd + e, i - 5)
                    if i == 12:
                        pe.wait_ge(acc_done, (9 * rnd + e) * 4 + 5)
                        for t in range(XT):
                            pe.transpose(ps[:, 7, t * P:(t + 1) * P], ONEHOT[:, t, :], ID[:])
                        for t in range(XT):
                            ins = mm(ps[:, 7, 2 * P:2 * P + NE], ONEHOT[:, t, :], G9[:, t, :], t == 0, t == XT - 1)
                        ins.then_inc(ptt_ready, 1)
                    for j in range(EJ):
                        if i == 4 * j + 6:
                            pe.wait_ge(act_done, FG + J + (j + 1))
                            if j >= 1:
                                pe.wait_ge(act_lo, J + j)
                            for k in range(4):
                                ins = pe.transpose(ps[:, 6, k * P:(k + 1) * P], ACTN[:, j % 2, k * P:(k + 1) * P], ID[:])
                            ins.then_inc(tr_ready, 1)
                    if i == 32:
                        gather(9 * rnd + e + 2)
            pe.wait_ge(y_lo, 9 * rnd + 9)
            pe.wait_ge(gs_done, 9 * rnd + 9)
            for i in range(4):
                combine(9 * rnd + 8, i)

        experts(0)
        pe.wait_ge(flag_rdy, 1)
        more = pe.value_load(CNT[0:1, 0:1], min_val=0, max_val=1)
        with pe.If(more > 0):
            experts(1)
        pe.end_ifs()

    @block.vector
    def _(dve):
        at = [0]
        links = [0]

        def link(ins):
            links[0] += 1
            ins.then_inc(dch, 1)
            dve.wait_ge(dch, links[0])

        def lo_upto(n):
            for b in range(at[0], min(n, B_MOE)):
                dve.wait_ge(hi_done, b + 1)
                dve.tensor_tensor(WLO[:, b % SPL, :], WRAW[:, b % RAW, :], WHI[:, b % SPL, :].bitcast(F32),
                                  ALU.subtract).then_inc(lo_done, 1)
            at[0] = max(at[0], n)

        event, squared, rstds = [0], [0], [0]

        def rstd(c0, n, count, lk=link):
            ms, std, y0, y1 = (v[:, c0:c0 + n] for v in (MS, STD, Y0, Y1))
            lk(dve.tensor_scalar(ms, SS[:, c0:c0 + n], 1.0 / count, EPS, ALU.mult, ALU.add))
            dve.sem_inc(ms_ready, 1)
            event[0] += 1
            dve.wait_ge(std_ready, event[0])
            lk(dve.reciprocal(y0, std))
            lk(dve.tensor_tensor(y1, y0, y0, ALU.mult))
            lk(dve.tensor_tensor(y1, y1, ms, ALU.mult))
            lk(dve.tensor_scalar(y1, y1, -0.5, 1.5, ALU.mult, ALU.add))
            lk(dve.tensor_tensor(RSTD[:, c0:c0 + n], y0, y1, ALU.mult))

        def wait_squares(n):
            squared[0] += n
            dve.wait_ge(sq_done, squared[0])

        def row(q):
            hi, lo = ada_rows(q)
            dve.wait_ge(ada_shift, q + 1)
            dve.wait_ge(bias_in, 16 * (q + 1))
            link(dve.tensor_tensor(hi, hi, lo, ALU.add))
            dve.tensor_tensor(hi, hi, BI, ALU.add).then_inc(ada_row, 1)

        def modulate(s, st):
            if st == 0:
                dve.wait_ge(cols_tr, s + 1)
                link(dve.tensor_copy(COL[:], ps[:, 0, 0:40]))
                dve.sem_inc(cols_read, 1)
                for i in range(2):
                    ins = dve.scalar_tensor_tensor(out=ACOL[:, i, :], in0=COL[:, 16 * i + 8:16 * i + 16], scalar=1.0,
                                                   in1=COL[:, 32:40], op0=ALU.add, op1=ALU.mult)
                link(ins)

            def low(u):
                n = 8 * s + 4 * st + u
                dve.wait_ge(ht_hi, n + 1)
                cols = slice(256 * st, 256 * st + 256)
                dve.tensor_tensor(HT[:, 1, 2 * u:2 * u + 2, cols], TF[s][:, n % 2, :].rearrange("p (k t) -> p k t", k=2),
                                  HT[:, 0, 2 * u:2 * u + 2, cols].bitcast(F32), ALU.subtract).then_inc(ht_lo, 1)

            for u in range(4):
                n = 8 * s + 4 * st + u
                dve.wait_ge(norm_tr, n + 1)
                if n % 8 >= 2:
                    dve.wait_ge(ht_lo, n - 1)
                for k in range(2):
                    ins = dve.tensor_scalar(TF[s][:, n % 2, 256 * k:256 * k + 256],
                                            ps[:, UNIT_BANK[s][st][u], 256 * k:256 * k + 256],
                                            ACOL[:, st, 2 * u + k:2 * u + k + 1],
                                            COL[:, 16 * st + 2 * u + k:16 * st + 2 * u + k + 1], ALU.mult, ALU.add)
                ins.then_inc(tf_ready, 1)
                if u:
                    low(u - 1)
            low(3)

        def gates(p, count):
            gb, ngb = POST[p][0], POST[p][1]
            dve.wait_ge(gate_in, count)
            for st in range(gb.shape[1]):
                link(dve.tensor_tensor(gb[:, st, :], gb[:, st, :], ngb, ALU.mult))

        def update(p, t):
            gb, _, tmp, _ = POST[p]
            link(dve.scalar_tensor_tensor(out=tmp.rearrange("p (a b) -> p a b", a=2), in0=ps[:, 2 * t:2 * t + 2, :],
                                          scalar=RSTD[:, t:t + 1], in1=gb[:, t // 2, :].rearrange("p (a b) -> p a b", a=2),
                                          op0=ALU.mult, op1=ALU.mult))
            link(dve.tensor_tensor(RES[:, t, :], RES[:, t, :], tmp, ALU.add))
            dve.sem_inc(post_done, 1)

        def boundary(p, first, count):
            s = p + 1
            lo_upto(first + 1)
            gates(p, count)
            for st in range(2):
                wait_squares(2)
                rstd(2 * st, 2, D)
                for t in (2 * st, 2 * st + 1):
                    update(p, t)
                wait_squares(2)
                rstd(4 + 2 * st, 2, D)
                dve.sem_inc(rstd_ready, 1)
                if st == 0:
                    lo_upto(first + 2)
                modulate(s, st)
                if st == 0:
                    lo_upto(first + SPL)

        def act_lo_part(k):
            dve.wait_ge(asp_hi, k + 1)
            dve.wait_ge(act_done, k // 2 + 1)
            dve.tensor_tensor(act_split(1, k), ACTF[:, k, :], act_split(0, k).bitcast(F32),
                              ALU.subtract).then_inc(asp_lo, 1)

        def rotate(dst, src, tile, heads, rot, end=None):
            d5 = dst.rearrange("p (h a s d) -> p h a s d", a=2, s=2, d=16)
            s5 = src.rearrange("p (h a s d) -> p h a s d", a=2, s=2, d=16)
            r5 = rot.rearrange("p (h a s d) -> p h a s d", a=2, s=2, d=16)

            def tab(kind):
                v = ROPE[:, 64 * kind + 32 * tile:64 * kind + 32 * tile + 32].rearrange("p (a d) -> p a d", a=2)
                return v.unsqueeze(1).broadcast_to([P, heads, 2, 16])

            for s_ in range(2):
                dve.tensor_tensor(d5[:, :, :, s_, :], s5[:, :, :, s_, :], tab(0), ALU.mult)
            dve.tensor_tensor(r5[:, :, :, 0, :], s5[:, :, :, 1, :], tab(2), ALU.mult)
            link(dve.tensor_tensor(r5[:, :, :, 1, :], s5[:, :, :, 0, :], tab(1), ALU.mult))
            if end is None:
                link(dve.tensor_tensor(dst, dst, rot, ALU.add))
            else:
                gjd = "p (g j d) -> p g j d"
                link(dve.tensor_tensor(end.rearrange("p (j g d) -> p g j d", g=2, j=4), dst.rearrange(gjd, g=2, j=4),
                                       rot.rearrange(gjd, g=2, j=4), ALU.add))

        link(dve.memset(CST[:].bitcast(F32), 0.0))
        dve.wait_ge(cond_hi, 1)
        dve.tensor_tensor(CST[:, :, 32:34], ps[:, 7, 0:16].rearrange("p (s k) -> p k s", s=2),
                          CST[:, :, 0:2].bitcast(F32), ALU.subtract).then_inc(cond_lo, 1)
        lo_upto(SPL)
        for q in range(4):
            lo_upto(2 * q + 2 + SPL)
            row(q)
        wait_squares(4)
        rstd(4, 4, D)
        dve.sem_inc(rstd_ready, 1)
        for st in range(2):
            modulate(0, st)
        dve.wait_ge(tab_in, 48)
        lo_upto(B_MIXIN + 4 + SPL)
        dve.wait_ge(used, B_MIXIN + 4)
        for t in range(XT):
            rotate(QROT, ps[:, 4 + t, :], t, 8, ROT0, Q_N[:, t, :])
        dve.sem_inc(q_x, 1)
        lo_upto(B_MIXIN + 5 + SPL)
        dve.wait_ge(used, B_MIXIN + 5)
        for t in range(XT):
            rotate(K_N[:, t, :], ps[:, t, 0:P], t, 2, ROT0[:, 0:P])
        dve.tensor_copy(V0[:, 0:2, :], ps[:, 0:2, P:2 * P]).then_inc(kv_x, 1)
        for u in range(8):
            dve.wait_ge(z_hi, u + 1)
            o = HT[:, 0, u % 4, 256 * (u // 4):256 * (u // 4) + 256]
            dve.tensor_tensor(HT[:, 1, u % 4, 256 * (u // 4):256 * (u // 4) + 256], ps[:, 6 + u % 2, 0:256],
                              o.bitcast(F32), ALU.subtract).then_inc(z_lo, 1)
        link(dve.tensor_scalar(SINK[:], SINK[:], -1.0, None, ALU.mult))
        def maxima0(g):
            kv, nk = g % 2, 512 if g < 4 else 256
            dve.wait_ge(scores, g + 1)
            link(dve.tensor_reduce(MX[:], ps[:, 0:4, 0:nk], AX_X, ALU.max))
            link(dve.scalar_tensor_tensor(out=NEGM[:], in0=MX[:], scalar=-SCALE, in1=SINK[:, 4 * kv:4 * kv + 4],
                                          op0=ALU.mult, op1=ALU.min))
            dve.tensor_tensor(TS[:], NEGM[:], SINK[:, 4 * kv:4 * kv + 4], ALU.subtract).then_inc(negmax, 1)

        maxima0(0)
        qn = 4
        trs = 0
        for g in range(8):
            u, kv, t = ATT0_U[g], g % 2, g // 2
            nk = 512 if g < 4 else 256
            lo_upto(u + SPL)
            dve.wait_ge(exps, g + 1)
            link(dve.tensor_tensor(RL[:], SUMS[:], ES[:], ALU.add))
            link(dve.reciprocal(RL[:], RL[:]))
            for j in range(4):
                ins = dve.tensor_scalar(PR0[:, j, 0:nk], PR0[:, j, 0:nk], RL[:, j:j + 1], None, ALU.mult)
            ins.then_inc(prob_scaled, 1)
            lo_upto(u + 2 + SPL)
            row(qn)
            if g < 7:
                maxima0(g + 1)
            for c_ in range(1, nk // P, 2):
                dve.wait_ge(p_tr, trs + c_ + 1)
                dve.tensor_copy(PT0[:, c_, :], ps[:, 5, :]).then_inc(pt_odd, 1)
            trs += nk // P
            if ATT0_CHUNKS[g] == 2:
                lo_upto(u + 4 + SPL)
                row(qn + 1)
            qn += ATT0_CHUNKS[g]
            dve.wait_ge(z_hi, 8 + g + 1)
            rows, cols = slice(HD * kv, HD * kv + HD), slice(t * P, t * P + P)
            dve.tensor_tensor(HT[rows, 1, 4:8, cols], ps[rows, 6, :].rearrange("p (j q) -> p j q", j=4),
                              HT[rows, 0, 4:8, cols].bitcast(F32), ALU.subtract).then_inc(z_lo, 1)
        lo_upto(B_MIXOUT + 2 + SPL)
        boundary(0, B_FFNIN, 48)
        for i in range(FG):
            if i == FG - 1:
                act_lo_part(0)
                act_lo_part(1)
            lo_upto(B_FFNIN + 2 * i + 1 + SPL)
            lo_upto(B_FFNIN + 2 * i + 2 + SPL)
            dve.wait_ge(silu_done, i + 1)
            b0 = 4 * (i % 2)
            dve.tensor_tensor(ACTF[:, 2 * i:2 * i + 2, :], SILF, ps[:, b0 + 2:b0 + 4, :],
                              ALU.mult).then_inc(act_done, 1)
        for m in range(-ASP_AHEAD, FG - 2 + 1):
            lo_upto(B_FFNOUT + m + SPL)
            for k in range(2 * (m + ASP_AHEAD), 2 * (m + ASP_AHEAD) + 2):
                if 2 <= k < 2 * FG:
                    act_lo_part(k)
        boundary(1, B_QKV, 96)
        dve.wait_ge(tab_in, 64)
        for n in range(6):
            b0 = 4 * (n % 2)
            lo_upto(B_QKV + 2 * n + 1 + SPL)
            lo_upto(B_QKV + 2 * n + 2 + SPL)
            dve.wait_ge(used, B_QKV + 2 * n + 2)
            if n < 4:
                if n:
                    dve.wait_ge(nat_tr, n)
                for t in range(XT):
                    rotate(NAT[:, t, :], ps[:, b0 + t, :], t, 8, ROT1)
                dve.sem_inc(nat_x, 1)
            else:
                dve.tensor_copy(V1[:, 2:4, 512 * (n - 4):512 * (n - 4) + 512],
                                ps[:, b0 + 2:b0 + 4, :]).then_inc(v_odd, 1)
        dve.wait_ge(lam_in, 16)
        lv = T2[:, 0:256]
        link(dve.tensor_tensor_reduce(MODB[:, 1280:1344], lv[:, 0:64], lv[:, 64:128], 1.0, 0.0, ALU.mult, ALU.add,
                                      LAM[:, 0:1]))
        link(dve.tensor_tensor_reduce(MODB[:, 1344:1408], lv[:, 128:192], lv[:, 192:256], 1.0, 0.0, ALU.mult,
                                      ALU.add, LAM[:, 1:2]))
        dve.sem_inc(lam_dve, 1)
        dve.wait_ge(lam_exp, 1)
        link(dve.tensor_tensor(LAM[:, 1:2], LAM[:, 3:4], LAM[:, 2:3], ALU.subtract))
        link(dve.tensor_scalar(LAM[:, 0:1], LAM[:, 1:2], -LAM_INIT, None, ALU.add))
        dve.wait_ge(small_in, 32)
        link(dve.tensor_scalar(GSUB[:, 1:2], GSUB[:, 0:1], 1.0 - LAM_INIT, None, ALU.mult))
        dve.sem_inc(lam_dve, 1)
        def maxima1(g):
            dve.wait_ge(scores, 8 + g + 1)
            link(dve.tensor_reduce(MX[:], ps[:, 0:4, :], AX_X, ALU.max))
            dve.tensor_scalar(NEGM[:], MX[:], -SCALE, None, ALU.mult).then_inc(negmax, 1)

        def sub_norm(t):
            rstd(8 * t, 8, 2 * HD)
            o = OA[:, t, :].rearrange("p (h d) -> p h d", h=8)
            r = RSTD[:, 8 * t:8 * t + 8].unsqueeze(2).broadcast_to([P, 8, P])
            dve.tensor_tensor(o, o, r, ALU.mult).then_inc(o_norm, 1)

        maxima1(0)
        for g in range(8):
            u = ATT1_U[g]
            lo_upto(u + SPL)
            dve.wait_ge(exps, 8 + g + 1)
            link(dve.reciprocal(RL[:], SUMS[:]))
            link(dve.tensor_scalar(NRL[:], RL[:], LAM[:, 0:1], None, ALU.mult))
            for hh in range(2):
                ins = dve.tensor_scalar(P1[:, 2 * hh, :], P1[:, 2 * hh, :], RL[:, 2 * hh:2 * hh + 1], None, ALU.mult)
            link(ins)
            for hh in range(2):
                ins = dve.scalar_tensor_tensor(out=P1[:, 2 * hh, :], in0=P1[:, 2 * hh + 1, :],
                                               scalar=NRL[:, 2 * hh + 1:2 * hh + 2], in1=P1[:, 2 * hh, :],
                                               op0=ALU.mult, op1=ALU.add)
            ins.then_inc(prob_scaled, 1)
            lo_upto(u + 2 + SPL)
            row(16 + g)
            if g < 7:
                maxima1(g + 1)
            dve.wait_ge(p_tr, 24 + 2 * g + 2)
            dve.tensor_copy(PT1[:, 2:4, :], ps[:, 5, :].rearrange("p (c q) -> p c q", c=2)).then_inc(pt_odd, 1)
            if g == 5:
                dve.wait_ge(o_raw, 4)
                sub_norm(0)
        dve.wait_ge(o_raw, 8)
        sub_norm(1)
        lo_upto(B_DOUT + SPL)
        for b in range(4):
            dve.wait_ge(z_hi, 16 + b + 1)
            dve.scalar_tensor_tensor(out=ZT[:, 1, 2 * b:2 * b + 2, :],
                                     in0=ps[:, b, :].rearrange("p (h t) -> p h t", h=2), scalar=GSUB[:, 1:2],
                                     in1=ZT[:, 0, 2 * b:2 * b + 2, :].bitcast(F32), op0=ALU.mult,
                                     op1=ALU.subtract).then_inc(z_lo, 1)
        lo_upto(B_DOUT + 2 + SPL)
        gates(2, 128)
        for t in range(XT):
            wait_squares(1)
            rstd(t, 1, D)
            update(2, t)
        dve.wait_ge(moe_in, 64)
        link(dve.scalar_tensor_tensor(out=SCB, in0=SCB, scalar=1.0, in1=NGB, op0=ALU.add, op1=ALU.mult))
        wait_squares(2)
        rstd(4, 2, D)
        for t in range(XT):
            link(dve.scalar_tensor_tensor(out=HN[:, t, :], in0=RES[:, t, :], scalar=RSTD[:, 4 + t:5 + t], in1=SCB,
                                          op0=ALU.mult, op1=ALU.mult))
            dve.tensor_tensor(HN[:, t, :], HN[:, t, :], SHB, ALU.add).then_inc(hn_done, 1)
        dve.wait_ge(logits_rdy, 1)
        L, EQ, CD, O1, L2, O2, AS = (LG[:, n, :, :] for n in range(7))
        M1, M2, I1, I2 = (LG[:, 7, :, 2 * n:2 * n + 1] for n in range(4))
        GT, GA, EB_ = LG[:, 8, :, 0:1], LG[:, 8, :, 1:2], LG[:, 8, :, 2:3]
        EX, DF = LG[:, 9, :, 0:1], LG[:, 9, :, 1:2]
        io8 = IOTA8.rearrange("p (t e) -> p t e", t=2)
        wide = [P, XT, NE]
        link(dve.tensor_copy(L, ps[:, 4, 0:16].rearrange("p (t e) -> p t e", t=2)))

        def first_max(lg, m, i_, oh):
            link(dve.tensor_reduce(m, lg, AX_X, ALU.max))
            link(dve.tensor_tensor(EQ, lg, m.broadcast_to(wide), ALU.is_equal))
            link(dve.tensor_tensor(CD, EQ, io8, ALU.mult))
            link(dve.tensor_reduce(i_, CD, AX_X, ALU.min))
            link(dve.tensor_tensor(oh, io8, i_.broadcast_to(wide), ALU.is_equal))

        first_max(L, M1, I1, O1)
        link(dve.scalar_tensor_tensor(out=L2, in0=O1, scalar=NEG, in1=L, op0=ALU.mult, op1=ALU.add))
        first_max(L2, M2, I2, O2)
        link(dve.tensor_tensor(AS, O1, O2, ALU.add))
        dve.sem_inc(assign_rdy, 1)
        link(dve.tensor_tensor(DF, M2, M1, ALU.subtract))
        dve.sem_inc(d_ready, 1)
        dve.wait_ge(e_ready, 1)
        link(dve.tensor_scalar(GT, EX, 1.0, None, ALU.add))
        link(dve.reciprocal(GA, GT))
        link(dve.tensor_tensor(EB_, GA, EX, ALU.mult))
        link(dve.tensor_tensor(EQ, O1, GA.broadcast_to(wide), ALU.mult))
        link(dve.tensor_tensor(CD, O2, EB_.broadcast_to(wide), ALU.mult))
        link(dve.tensor_tensor(G9[:], EQ, CD, ALU.add))
        link(dve.memset(PA[:], 0.0))
        dve.wait_ge(pos_rdy, 1)
        link(dve.tensor_copy(PA[:, 0:NE, 0, :], ps[:, 5, 0:16].rearrange("p (t e) -> p e t", t=2)))
        link(dve.tensor_copy(PA[:, 0:NE, 1, :], AS.rearrange("p t e -> p e t")))
        link(dve.tensor_reduce(GT[:, 0, :], ps[:, 5, 16:24], AX_X, ALU.max))
        link(dve.tensor_scalar(GT[:, 0, :], GT[:, 0, :], float(P), None, ALU.is_gt))
        link(dve.tensor_copy(CNT[0:1, 0:1], GT[0:1, 0, :]))
        dve.sem_inc(flag_rdy, 1)

        def experts(rnd):
            base = moe_base(rnd)
            n0 = 9 * rnd

            def onehot(src, n):
                dve.tensor_copy(CUR[:], src).then_inc(cur_done, 1)
                dve.wait_ge(cur_done, n)
                for t in range(XT):
                    ins = dve.tensor_scalar(ONEHOT[:, t, :], IOTA, CUR[:, 0, t:t + 1], CUR[:, 1, t:t + 1],
                                            ALU.is_equal, ALU.mult)
                ins.then_inc(onehot_rdy, 1)

            def hte(n):
                dve.wait_ge(hte_hi, n)
                dve.tensor_tensor(HTE[:, 1, :, :], ps[:, 2:4, :].rearrange("p b (k s) -> p (b k) s", k=4),
                                  HTE[:, 0, :, :].bitcast(F32), ALU.subtract).then_inc(hte_lo, 1)

            def ylo(n):
                dve.wait_ge(y_hi, n)
                dve.scalar_tensor_tensor(out=YS[:, 1, :].rearrange("p (a b) -> p a b", a=2), in0=ps[:, 4:6, :],
                                         scalar=GS[:, 0:1],
                                         in1=YS[:, 0, :].bitcast(F32).rearrange("p (a b) -> p a b", a=2),
                                         op0=ALU.mult, op1=ALU.subtract).then_inc(y_lo, 1)

            def accumulate(n, i):
                t, h = i // 2, i % 2
                dve.wait_ge(comb_rdy, n * 4 + (i + 1))
                dve.wait_ge(acc_done, n * 4 + (i + 1))
                o = YACC[:, t, 512 * h:512 * h + 512]
                dve.tensor_tensor(o, o, ps[:, 7, :], ALU.add).then_inc(acc_done, 1)

            if rnd:
                dve.wait_ge(gather_rdy, 9)
                dve.tensor_scalar(PA[:, :, 0, :], PA[:, :, 0, :], -float(P), None, ALU.add).then_inc(cur_done, 1)
                dve.wait_ge(cur_done, 10)
            else:
                dve.memset(YACC[:], 0.0).then_inc(acc_done, 1)
            dve.memset(PTR[:].bitcast(F32), 0.0)
            dve.memset(ps[:, 4:6, :], 0.0)
            dve.memset(GS[:], 0.0).then_inc(gs_done, 1)
            onehot(PA[:, 0, :, :], n0 + rnd + 1)
            hte(n0 + 1)
            with dve.Fori(0, NE) as e:
                J = EJ * NE * rnd + e * EJ
                for i in range(EB):
                    slot = (B_MOE + i) % SPL
                    dve.wait_ge(hi_done, base + e * EB + (i + 1))
                    dve.tensor_tensor(WLO[:, slot, :], WRAW[:, (B_MOE + i) % RAW, :], WHI[:, slot, :].bitcast(F32),
                                      ALU.subtract).then_inc(lo_done, 1)
                    if i == 2:
                        ylo(n0 + e + 1)
                    if 7 <= i < 11:
                        accumulate(n0 + e, i - 7)
                    if i == 15:
                        dve.wait_ge(pt_done, NE * rnd + e + 1)
                        dve.wait_ge(y_lo, n0 + e + 1)
                        dve.tensor_copy(GS[:], ps[:, 7, bass.ds(e + 2 * P, 1)]).then_inc(gs_done, 1)
                    if i == 21:
                        onehot(PA[:, bass.ds(e + 1, 1), :, :].rearrange("p o a t -> p (o a) t"), n0 + e + (rnd + 2))
                    for j in range(EJ):
                        if i == 4 * j + 6:
                            dve.wait_ge(silu_done, FG + J + (j + 1))
                            if j >= 2:
                                dve.wait_ge(tr_ready, J + (j - 1))
                            dve.tensor_tensor(ACTN[:, j % 2, :], SIL[:, j % 2, :], ps[:, 2 * (j % 2) + 1, :],
                                              ALU.mult).then_inc(act_done, 1)
                        if i == 4 * j + 9:
                            dve.wait_ge(act_hi, J + (j + 1))
                            dve.tensor_tensor(ACTT[:, 1, 4 * j:4 * j + 4, :],
                                              ps[:, 6, :].rearrange("p (k s) -> p k s", k=4),
                                              ACTT[:, 0, 4 * j:4 * j + 4, :].bitcast(F32),
                                              ALU.subtract).then_inc(act_lo, 1)
                    if i == 35:
                        hte(n0 + e + 2)
            ylo(n0 + 9)
            for i in range(4):
                accumulate(n0 + 8, i)
            dve.wait_ge(acc_done, (n0 + 9) * 4 + 1)

        experts(0)
        more = dve.value_load(CNT[0:1, 0:1], min_val=0, max_val=1)
        with dve.If(more > 0):
            experts(1)
        dve.end_ifs()

        fin = [0]

        def flink(ins):
            fin[0] += 1
            ins.then_inc(fin_chain, 1)
            dve.wait_ge(fin_chain, fin[0])

        gb, ngb, tmp, junk = POST[3]
        dve.wait_ge(gate_in, 160)
        flink(dve.tensor_tensor(gb[:, 0, :], gb[:, 0, :], ngb, ALU.mult))
        for t in range(XT):
            flink(dve.tensor_tensor_reduce(junk, YACC[:, t, :], YACC[:, t, :], 1.0, 0.0, ALU.mult, ALU.add,
                                           SS[:, 4 + t:5 + t]))
        rstd(4, 2, D, flink)
        for t in range(XT):
            flink(dve.scalar_tensor_tensor(out=tmp, in0=YACC[:, t, :], scalar=RSTD[:, 4 + t:5 + t], in1=gb[:, 0, :],
                                           op0=ALU.mult, op1=ALU.mult))
            flink(dve.tensor_tensor(RES[:, t, :], RES[:, t, :], tmp, ALU.add))
            dve.sem_inc(fin_rdy, 1)

    stack.close()


_INS = ["x", "c", "ctx", "c_ctx", "ada_w", "ada_b", "norm_g", "mix_in_w", "mix_out_w", "win_sink", "diff_qkv_w",
        "diff_out_w", "diff_lambda", "diff_subln_g", "ffn_in_w", "ffn_out_w", "router_w", "expert_in_w",
        "expert_out_w"]
_OUTS = [((1, 256, 1024), "float32")]


def kernel(**inputs):
    import numpy as _np
    import concourse.bacc as _bacc
    from concourse import mybir as _mybir
    from concourse.bass_utils import run_bass_kernel_spmd as _run

    nc = _bacc.Bacc("TRN2", target_bir_lowering=False, num_devices=1)
    arrays, args = {}, []
    for name in _INS + ["tables"]:
        a = constant_tables() if name == "tables" else _np.ascontiguousarray(inputs[name])
        arrays[f"in_{name}_dram"] = a
        args.append(nc.dram_tensor(f"in_{name}_dram", a.shape, _mybir.dt.from_np(a.dtype), kind="ExternalInput").ap())
    for i, (shape, dtype) in enumerate(_OUTS):
        dt = _mybir.dt.from_np(_np.dtype(dtype))
        args.append(nc.dram_tensor(f"out_{i}_dram", shape, dt, kind="ExternalOutput").ap())
    backbone(nc, *args)
    r = _run(nc, [arrays], core_ids=[0])
    got = tuple(r.results[0][f"out_{i}_dram"] for i in range(len(_OUTS)))
    return got[0]
```

```python
from contextlib import ExitStack
import math

import numpy as np

import concourse.bass as bass
from concourse import mybir

F32 = mybir.dt.float32
F32R = mybir.dt.float32r
I32 = mybir.dt.int32
ACT = mybir.ActivationFunctionType
ALU = mybir.AluOpType
AX_X = mybir.AxisListType.X

P = 128
D = 1024
DK = D // P
SEQ = 256
TILES = 4
XT = 2
EPS = 1e-6
NEG = -1e30
HD = 64
FFN = 2816
FG = FFN // 256
NE = 8
ED = 3584
EJ = ED // 512
SCALE = HD ** -0.5
LAM_INIT = 0.8 - 0.6 * math.exp(-0.3)

RAW = 6
SPL = 3
BLK = 2048

ADA_CH = 12
B_ADA0 = 0
B_MIXIN = 8
B_ATT0 = 13
B_MIXOUT = 37
B_FFNIN = 41
B_FFNOUT = B_FFNIN + 2 * FG
B_QKV = B_FFNOUT + FG
B_ATT1 = B_QKV + 12
B_DOUT = B_ATT1 + 16
B_MOE = B_DOUT + 4
IN_BLOCKS = 4 * EJ
OUT_BLOCKS = ED // 256
EB = IN_BLOCKS + OUT_BLOCKS
assert EB % RAW == 0 and EB % SPL == 0
SPLIT_AHEAD = 2
ATT0_CHUNKS = [2, 2, 2, 2, 1, 1, 1, 1]

T_ID, T_TRI, T_ROPE, T_DFT = 0, 128, 384, 576
T_MOE = T_DFT + 1280
T_ALL = T_MOE + 128 * 3 + 16


def constant_tables():
    t = np.zeros((P, T_ALL), np.float64)
    r = np.arange(P)
    t[:, T_ID:T_ID + P] = np.eye(P)
    t[:, T_TRI:T_TRI + P] = np.where(r[None, :] > r[:, None], NEG, 0)
    t[:, T_TRI + P:T_TRI + 2 * P] = np.where(r[None, :] < r[:, None], NEG, 0)
    inv = np.float32(10000.0) ** (-np.arange(0, 32, 2, dtype=np.float32) / np.float32(32))
    for tile in range(XT):
        tok = tile * P + r
        for axis, pos in enumerate((tok // 64, tok % 64)):
            ang = (pos[:, None].astype(np.float32) * inv[None, :]).astype(np.float64)
            at = T_ROPE + tile * 32 + axis * 16
            t[:, at:at + 16] = np.cos(ang)
            t[:, at + 64:at + 80] = np.sin(ang)
            t[:, at + 128:at + 144] = -np.sin(ang)
    lp = np.arange(SEQ)
    for c in range(2):
        ang = 2 * np.pi * (((c * P + r)[:, None] * lp[None, :]) % SEQ) / SEQ
        t[:, T_DFT + c * 512:T_DFT + c * 512 + 256] = np.cos(ang)
        t[:, T_DFT + c * 512 + 256:T_DFT + c * 512 + 512] = np.sin(ang)
    ang = 2 * np.pi * ((r[:, None] * r[None, :]) % P) / P
    norm = 1 / math.sqrt(SEQ * P)
    t[:, T_DFT + 1024:T_DFT + 1152] = np.cos(ang) * norm
    t[:, T_DFT + 1152:T_DFT + 1280] = -np.sin(ang) * norm
    t[:, T_MOE:T_MOE + P] = r[:, None] < r[None, :]
    t[:, T_MOE + P:T_MOE + 2 * P] = 1
    t[:, T_MOE + 2 * P:T_MOE + 3 * P] = r[None, :]
    t[:, T_MOE + 3 * P:] = np.tile(np.arange(8) - 8, 2)[None, :]
    return t.astype(np.float32)


def backbone(nc, x, c, ctx_in, c_ctx, ada_w, ada_b, norm_g, mix_in_w, mix_out_w, win_sink, diff_qkv_w,
             diff_out_w, diff_lambda, diff_subln_g, ffn_in_w, ffn_out_w, router_w, expert_in_w,
             expert_out_w, tables, out):
    stack = ExitStack()

    def sb(name, shape, dt=F32):
        return stack.enter_context(nc.sbuf_tensor(name, shape, dt))

    RES = sb("residual", [P, TILES, D])
    WRAW = sb("w_raw", [P, RAW, BLK])
    WHI = sb("w_hi", [P, SPL, BLK], F32R)
    WLO = sb("w_lo", [P, SPL, BLK], F32R)
    ID = sb("ident", [P, P])
    CST = sb("cond_stationary", [P, DK, P], F32R)
    MROW = sb("mod_rows", [40, 2, P])
    COL = sb("mod_cols", [P, 40])
    ACOL = sb("scale_cols", [P, 2, DK])
    SS = sb("sumsq", [P, 16])
    MS = sb("meansq", [P, 16])
    STD = sb("std", [P, 16])
    Y0 = sb("rstd0", [P, 16])
    Y1 = sb("rstd_tmp", [P, 16])
    RSTD = sb("rstd", [P, 16])
    SINK = sb("sink", [P, 8])
    MX = sb("row_max", [P, 4])
    NEGM = sb("neg_max", [P, 4])
    TS = sb("sink_shifted", [P, 4])
    ES = sb("sink_exp", [P, 4])
    SUMS = sb("row_sums", [P, 4])
    RL = sb("row_recip", [P, 4])
    NRL = sb("row_recip_lam", [P, 4])
    LAM = sb("lam", [P, 4])
    GSUB = sb("subln_col", [P, 2])
    CNT = sb("overflow", [1, 1], I32)

    RW = sb("router", [P, DK, NE])
    LG = sb("logits", [P, 10, XT, NE])
    G9 = sb("gates", [P, XT, NE])
    PA = sb("pos_assign", [P, NE + 1, 2, XT])
    CUR = sb("cur_pa", [P, 2, XT])
    GS = sb("gate_slot", [P, 1])

    def area(*specs):
        with ExitStack() as s:
            return [s.enter_context(nc.sbuf_tensor(n, sh, dt)) for n, sh, dt in specs]

    W0 = 8192
    HT, WORK, MODB, T2 = area(("h_t", [P, 2, DK, 512], F32R), ("work", [P, 12288], F32),
                              ("mod_buf", [P, 1536], F32), ("tables", [P, 512], F32))
    _, ASP = area(("pad_a", [P, W0 + 12288], F32), ("act_split", [P, 2, 2, 512], F32R))
    ZT, P1, PT1, ADAX = area(("z_t1", [P, 2, DK, 256], F32R), ("p1", [P, 4, 512], F32), ("pt1", [P, 4, 256], F32),
                             ("ada_rows", [P, 2, 512], F32))
    (HTE, YS, PTR, YACC, ONEHOT, SIL, TM) = area(
        ("h_te", [P, 2, DK, P], F32R), ("y_split", [P, 2, D], F32R), ("onehot_t", [P, 2 * P], F32R),
        ("y_acc", [P, XT, D], F32), ("onehot", [P, XT, P], F32), ("silu_g", [P, 2, 512], F32),
        ("moe_tables", [P, 400], F32))
    _, ACTT, ACTN, HN = area(("pad_b", [P, W0 + 4096], F32), ("act_t", [P, 2, ED // P, P], F32R),
                             ("act_n", [P, 2, 512], F32), ("h_nat", [P, XT, D], F32))
    _, HTF = area(("pad_c", [P, W0 + 4096], F32), ("h_tf", [P, DK, 256], F32))

    def act_split(part, k):
        return ASP[:, part, k, :] if k < 2 else HT[:, part, (k - 2) % 8, :]

    def work(off, *dims):
        n = int(np.prod(dims))
        v = WORK[:, off:off + n]
        if len(dims) == 1:
            return v
        names = "abcd"[:len(dims)]
        return v.rearrange(f"p ({' '.join(names)}) -> p {' '.join(names)}",
                           **{k: d for k, d in zip(names[1:], dims[1:])})

    F_N = work(0, TILES, 512)
    V0 = work(2048, TILES, P)
    QT0 = work(2560, 4, 512)
    KT0 = work(4608, 512)
    PR0 = work(5120, 4, 512)
    PT0 = work(7168, 4, 512)
    DFT = work(9216, 1280)
    AT0 = work(5120, 2, 512)
    K_N = work(6144, TILES, P)
    ROT0 = work(6656, 512)
    QROT = work(10496, 512)
    Q_N = work(7168, TILES, 512)
    ACTF = work(0, FFN // P, 512)
    SILF = work(11264, 2, 512)
    V1 = work(0, TILES, D)
    QT1 = work(4096, DK, 256)
    KT1 = work(6144, DK, 512)
    NAT = work(10240, TILES, 512)
    OA = work(10240, XT, D)
    ROT1 = MODB[:, 0:512]
    XN = {0: work(5120, TILES, D), 1: work(0, TILES, D), 2: work(4096, TILES, D)}
    TF = {0: work(0, 2, 512), 1: work(4096, 2, 512), 2: work(8192, 2, 512)}
    JUNK0 = work(1024, D)
    POST = {0: (work(5120, 2, D), work(7168, D), work(8192, D), work(9216, D)),
            1: (work(0, 2, D), work(2048, D), work(11264, D), work(3072, D)),
            2: (work(6144, 1, D), work(7168, D), work(8192, D), work(9216, D)),
            3: (work(0, 1, D), work(1024, D), work(2048, D), work(3072, D))}
    SCB, SHB, NGB = work(0, D), work(1024, D), work(2048, D)
    BI, BI0 = MODB[0:2, 512:1024], work(2048, 2048)[0:2, :]

    def ada_rows(q):
        if q % 2 == 0:
            return MODB[0:2, 0:512], MODB[0:2, 1024:1536]
        if q < 16:
            return work(11008, 512)[0:2, :], work(11520, 512)[0:2, :]
        return ADAX[0:2, 0, :], ADAX[0:2, 1, :]

    TRI, ROPE = T2[:, 0:256], T2[:, 256:448]
    UPPER, ONES, IOTA, IOTA8 = TM[:, 0:P], TM[:, P:2 * P], TM[:, 2 * P:3 * P], TM[:, 3 * P:3 * P + 16]

    mod = nc.dram_tensor("mod_scratch", [2, 2, 6 * D], F32, kind="Internal").ap()
    ps = stack.enter_context(nc.psum_tensor("ps", [P, 8, 512], F32))

    def sem(name):
        return stack.enter_context(nc.semaphore(name))

    rows_in = [sem(f"rows_in{i}") for i in range(3)]
    mod_stored = [sem(f"mod_stored{i}") for i in range(2)]
    landed = [sem(f"landed{i}") for i in range(RAW)]
    hi_done = sem("hi_done")
    lo_done = sem("lo_done")
    used = sem("used")
    res_in = sem("res_in")
    tab_in = sem("tab_in")
    rope_in = sem("rope_in")
    crow_in = sem("crow_in")
    small_in = sem("small_in")
    bias0_in = sem("bias0_in")
    bias_in = sem("bias_in")
    gate_in = sem("gate_in")
    lam_in = sem("lam_in")
    moe_in = sem("moe_in")
    tm_in = sem("tm_in")
    out_done = sem("out_done")
    crow_silu = sem("crow_silu")
    cond_tr = sem("cond_tr")
    cond_hi = sem("cond_hi")
    cond_lo = sem("cond_lo")
    ada_shift = sem("ada_shift")
    pool_chain = sem("pool_chain")
    ada_row = sem("ada_row")
    row_tr = sem("row_tr")
    cols_tr = sem("cols_tr")
    cols_read = sem("cols_read")
    sq_done = sem("sq_done")
    ms_ready = sem("ms_ready")
    std_ready = sem("std_ready")
    rstd_ready = sem("rstd_ready")
    xn_ready = sem("xn_ready")
    norm_tr = sem("norm_tr")
    tf_ready = sem("tf_ready")
    ht_hi = sem("ht_hi")
    ht_lo = sem("ht_lo")
    prod_done = sem("prod_done")
    post_done = sem("post_done")
    dve_chain = sem("dve_chain")
    f_copied = sem("f_copied")
    q_ctx = sem("q_ctx")
    q_x = sem("q_x")
    kv_ctx = sem("kv_ctx")
    kv_x = sem("kv_x")
    qk_tr = sem("qk_tr")
    qk_evac = sem("qk_evac")
    dft1 = sem("dft1")
    at_ready = sem("at_ready")
    dft2 = sem("dft2")
    z_hi = sem("z_hi")
    z_lo = sem("z_lo")
    scores = sem("scores")
    negmax = sem("negmax")
    exps = sem("exps")
    prob_scaled = sem("prob_scaled")
    p_tr = sem("p_tr")
    pt_even = sem("pt_even")
    pt_odd = sem("pt_odd")
    pv_done = sem("pv_done")
    silu_done = sem("silu_done")
    act_done = sem("act_done")
    hidden_hi = sem("hidden_hi")
    hidden_lo = sem("hidden_lo")
    nat_x = sem("nat_x")
    nat_ctx = sem("nat_ctx")
    nat_tr = sem("nat_tr")
    nat_evac = sem("nat_evac")
    v_even = sem("v_even")
    v_odd = sem("v_odd")
    lam_dve = sem("lam_dve")
    lam_exp = sem("lam_exp")
    o_raw = sem("o_raw")
    o_norm = sem("o_norm")
    o_tr = sem("o_tr")
    hn_done = sem("hn_done")
    h_tr = sem("h_tr")
    h_evac = sem("h_evac")
    logits_rdy = sem("logits_rdy")
    assign_rdy = sem("assign_rdy")
    d_ready = sem("d_ready")
    e_ready = sem("e_ready")
    pos_rdy = sem("pos_rdy")
    flag_rdy = sem("flag_rdy")
    cur_done = sem("cur_done")
    onehot_rdy = sem("onehot_rdy")
    gather_rdy = sem("gather_rdy")
    hte_hi = sem("hte_hi")
    hte_lo = sem("hte_lo")
    tr_ready = sem("tr_ready")
    act_hi = sem("act_hi")
    act_lo = sem("act_lo")
    ptt_ready = sem("ptt_ready")
    pt_done = sem("pt_done")
    gs_done = sem("gs_done")
    y_hi = sem("y_hi")
    y_lo = sem("y_lo")
    comb_rdy = sem("comb_rdy")
    acc_done = sem("acc_done")
    fin_chain = sem("fin_chain")
    fin_rdy = sem("fin_rdy")

    def cols512(w, k0, c0):
        return [(w[k0 * P:(k0 + 4) * P, c0:c0 + 512].rearrange("(k p) n -> p k n", p=P), (4, 512), 0, P)]

    def rows256(w, k0):
        return [(w[k0 * P:(k0 + 2) * P, 0:D].rearrange("(k p) n -> p k n", p=P), (2, D), 0, P)]

    def ada_chunk(q):
        w = ada_w[q // ADA_CH]
        return [cols512(w, 4 * h, 512 * (q % ADA_CH)) for h in range(2)]

    blocks = []
    for q in range(4):
        blocks += ada_chunk(q)
    mw = mix_in_w[0]
    for n in range(2):
        blocks += [cols512(mw, 4 * h, 512 * n) for h in range(2)]
    blocks.append([(mw[:, 1024:1280].rearrange("(k p) n -> p k n", p=P), (8, 256), 0, P)])
    for q in range(4, 16):
        blocks += ada_chunk(q)
    for n in range(2):
        blocks += cols512(mix_out_w[0], 0, 512 * n),
        src = mix_out_w[0, 512:1024, 512 * n:512 * n + 512].rearrange("(g j d) n -> g d j n", g=2, j=4)
        blocks.append([(src[g], (4, 512), HD * g, HD) for g in range(2)])
    for i in range(FG):
        for h in range(2):
            blocks.append([(ffn_in_w[0, 512 * h:512 * h + 512, FFN * u + 256 * i:FFN * u + 256 * i + 256]
                            .rearrange("(k p) n -> p k n", p=P), (4, 2, 256, u), 0, P) for u in range(2)])
    for m in range(FG):
        blocks.append(rows256(ffn_out_w[0], 2 * m))
    for n in range(6):
        blocks += [cols512(diff_qkv_w[0], 4 * h, 512 * n) for h in range(2)]
    for q in range(16, 24):
        blocks += ada_chunk(q)
    for n in range(2):
        blocks += [cols512(diff_out_w[0], 4 * h, 512 * n) for h in range(2)]
    assert len(blocks) == B_MOE

    def slot_view(slot, dims, p0, pn):
        v = WRAW[p0:p0 + pn, slot, :]
        if len(dims) == 4:
            return v.rearrange("p (k u n) -> p k u n", k=dims[0], u=2)[:, :, dims[3], :]
        return v.rearrange("p (k n) -> p k n", k=dims[0])

    land_at, total = [], [0] * RAW
    for b, parts in enumerate(blocks):
        total[b % RAW] += 16 * len(parts)
        land_at.append(total[b % RAW])

    def moe_base(rnd):
        return B_MOE + NE * EB * rnd

    def moe_landed(rnd, x_, i):
        s = (B_MOE + i) % RAW
        firsts = [j for j in range(EB) if (B_MOE + j) % RAW == s]
        per = sum(16 * moe_parts(j) for j in firsts)
        upto = sum(16 * moe_parts(j) for j in firsts if j <= i)
        return total[s] + rnd * NE * per + x_ * per + upto

    def moe_parts(i):
        return 2 if i < IN_BLOCKS else 1

    land_at += [moe_landed(0, 0, i) for i in range(SPL)]

    ATT0_U = [B_ATT0 + 2 * sum(ATT0_CHUNKS[:g]) for g in range(9)]
    ATT1_U = [B_ATT1 + 2 * g for g in range(9)]

    def ada_end(q):
        if q < 4:
            return 2 * q + 2
        return (B_ATT0 + 2 * (q - 4) if q < 16 else B_ATT1 + 2 * (q - 16)) + 2

    def wait_stored(eng, n):
        eng.wait_ge(mod_stored[0], 16 * ((n - 3) // 2))
        eng.wait_ge(mod_stored[1], 16 * ((n - 4) // 2))

    UNIT_BANK = {0: ((0, 1, 2, 3), (4, 5, 6, 7)), 1: ((0, 1, 2, 3), (4, 5, 6, 7)), 2: ((0, 1, 2, 3), (2, 3, 6, 7))}

    block = stack.enter_context(nc.Block())

    @block.sync
    def _(sp):
        sp.dma_start(MROW[0:8, 0, :], c[0].rearrange("(k p) -> k p", p=P)).then_inc(crow_in, 16)
        sp.dma_start(MROW[8:16, 0, :], c_ctx.rearrange("(k p) -> k p", p=P)).then_inc(crow_in, 16)
        sp.dma_start(BI0, ada_b[0:1, 0:2048].broadcast_to([2, 2048])).then_inc(bias0_in, 16)
        sp.dma_start(ID[:], tables[:, T_ID:T_ID + P]).then_inc(crow_in, 16)
        for b, parts in enumerate(blocks):
            if b == 5:
                sp.dma_start(T2[:, 0:448], tables[:, T_TRI:T_TRI + 448]).then_inc(tab_in, 16)
                sp.dma_start(SINK[:], win_sink.broadcast_to([P, 8])).then_inc(tab_in, 16)
            if b == 8:
                sp.dma_start(DFT, tables[:, T_DFT:T_DFT + 1280]).then_inc(tab_in, 16)
                sp.dma_start(GSUB[:, 0:1], diff_subln_g.rearrange("a p -> p a")).then_inc(small_in, 16)
                sp.dma_start(RW[:], router_w[0].rearrange("(k p) e -> p k e", p=P)).then_inc(small_in, 16)
            if b >= RAW:
                sp.wait_ge(lo_done, b - RAW + 1)
            for src, dims, p0, pn in parts:
                sp.dma_start(slot_view(b % RAW, dims, p0, pn), src).then_inc(landed[b % RAW], 16)
            if b == 3:
                for t in range(TILES):
                    src = (x if t < XT else ctx_in)[0, (t % 2) * P:(t % 2 + 1) * P, :]
                    sp.dma_start(RES[:, t, :], src).then_inc(res_in, 16)

        def experts(rnd):
            with sp.Fori(0, NE) as e:
                for i in range(EB):
                    slot = (B_MOE + i) % RAW
                    sp.wait_ge(lo_done, moe_base(rnd) + e * EB + (i - RAW + 1))
                    if i < IN_BLOCKS:
                        j, k0 = i // 4, 2 * (i % 4)
                        for u in range(2):
                            src = expert_in_w[0, e, k0 * P:(k0 + 2) * P, ED * u + 512 * j:ED * u + 512 * j + 512]
                            sp.dma_start(slot_view(slot, (2, 2, 512, u), 0, P),
                                         src.rearrange("(k p) n -> p k n", p=P)).then_inc(landed[slot], 16)
                    else:
                        k0 = 2 * (i - IN_BLOCKS)
                        src = expert_out_w[0, e, k0 * P:(k0 + 2) * P, :].rearrange("(k p) n -> p k n", p=P)
                        sp.dma_start(slot_view(slot, (2, D), 0, P), src).then_inc(landed[slot], 16)

        experts(0)
        sp.wait_ge(flag_rdy, 1)
        more = sp.value_load(CNT[0:1, 0:1], min_val=0, max_val=1)
        with sp.If(more > 0):
            experts(1)
        sp.end_ifs()
        for t in range(XT):
            sp.wait_ge(fin_rdy, t + 1)
            sp.dma_start(out[0, t * P:(t + 1) * P, :], RES[:, t, :]).then_inc(out_done, 16)
        sp.wait_ge(out_done, 16 * XT)

    @block.gpsimd
    def _(pool):
        def bias(q):
            if q > 4:
                pool.wait_ge(ada_row, q)
            src = ada_b[q // ADA_CH:q // ADA_CH + 1, 512 * (q % ADA_CH):512 * (q % ADA_CH) + 512]
            pool.dma_start(BI, src.broadcast_to([2, 512])).then_inc(bias_in, 16)

        links = [0]

        def row(q):
            hi, lo = ada_rows(q)
            pool.wait_ge(ada_shift, q + 1)
            pool.wait_ge(bias0_in, 16) if q < 4 else pool.wait_ge(bias_in, 16 * (q - 3))
            links[0] += 1
            pool.tensor_tensor(hi, hi, lo, ALU.add).then_inc(pool_chain, 1)
            pool.wait_ge(pool_chain, links[0])
            bias_row = BI0[:, 512 * q:512 * q + 512] if q < 4 else BI
            pool.tensor_tensor(hi, hi, bias_row, ALU.add).then_inc(ada_row, 1)

        def store(q):
            pool.wait_ge(ada_row, q + 1)
            dst = mod[q // ADA_CH, :, 512 * (q % ADA_CH):512 * (q % ADA_CH) + 512]
            pool.dma_start(dst, ada_rows(q)[0]).then_inc(mod_stored[q % 2], 16)

        def mod_rows(s):
            layer, piece, gi = [None, (0, 3, 2), (1, 0, 0)][s]
            if s == 2:
                pool.wait_ge(cols_tr, 1)
            src = norm_g[layer, gi].rearrange("(k p) -> k p", p=P)
            pool.dma_start(MROW[32:40, s % 2, :], src).then_inc(rows_in[s], 16)
            wait_stored(pool, 16)
            for st in range(2):
                src = mod[layer, st, piece * D:(piece + 2) * D].rearrange("(k p) -> k p", p=P)
                pool.dma_start(MROW[16 * st:16 * st + 16, s % 2, :], src).then_inc(rows_in[s], 16)

        def gate_rows(p):
            layer, piece, gi = [(0, 2, 1), (0, 5, 3), (1, 2, 1), (1, 5, 3)][p]
            gb, ngb = POST[p][0], POST[p][1]
            for st in range(gb.shape[1]):
                src = mod[layer, st:st + 1, piece * D:(piece + 1) * D]
                pool.dma_start(gb[:, st, :], src.broadcast_to([P, D])).then_inc(gate_in, 16)
            pool.dma_start(ngb, norm_g[layer, gi:gi + 1, :].broadcast_to([P, D])).then_inc(gate_in, 16)

        bias(4)
        pool.dma_start(MROW[32:40, 0, :], norm_g[0, 0].rearrange("(k p) -> k p", p=P)).then_inc(rows_in[0], 16)
        for q in range(4):
            row(q)
        for q in range(4, 16):
            row(q)
            store(q)
            if q < 15:
                bias(q + 1)
        mod_rows(1)
        mod_rows(2)
        pool.wait_ge(pv_done, 8)
        gate_rows(0)
        pool.wait_ge(used, B_FFNOUT + 5)
        gate_rows(1)
        pool.wait_ge(used, B_QKV)
        pool.dma_start(ROPE, tables[:, T_ROPE:T_ROPE + 192]).then_inc(rope_in, 16)
        lam_row = diff_lambda.rearrange("a b d -> a (b d)")
        pool.dma_start(T2[:, 0:256], lam_row.broadcast_to([P, 256])).then_inc(lam_in, 16)
        bias(16)
        for q in range(16, 24):
            row(q)
            store(q)
            if q < 23:
                bias(q + 1)
        wait_stored(pool, 24)
        pool.wait_ge(pv_done, 16)
        gate_rows(2)
        pool.dma_start(SCB, mod[1, 0:1, 4 * D:5 * D].broadcast_to([P, D])).then_inc(moe_in, 16)
        pool.dma_start(SHB, mod[1, 0:1, 3 * D:4 * D].broadcast_to([P, D])).then_inc(moe_in, 16)
        pool.dma_start(NGB, norm_g[1, 2:3, :].broadcast_to([P, D])).then_inc(moe_in, 16)
        pool.dma_start(TM[:], tables[:, T_MOE:T_MOE + 400]).then_inc(tm_in, 16)
        pool.wait_ge(hn_done, 2)
        gate_rows(3)

    @block.scalar
    def _(act):
        at = [0]

        def hi_upto(n):
            for b in range(at[0], min(n, B_MOE + SPL)):
                act.wait_ge(landed[b % RAW], land_at[b])
                if b >= SPL:
                    act.wait_ge(used, b - SPL + 1)
                act.activation(WHI[:, b % SPL, :], WRAW[:, b % RAW, :], ACT.Copy).then_inc(hi_done, 1)
            at[0] = max(at[0], n)

        event, squared = [0], [0]

        def sqrt(c0, n):
            event[0] += 1
            act.wait_ge(ms_ready, event[0])
            act.activation(STD[:, c0:c0 + n], MS[:, c0:c0 + n], ACT.Sqrt).then_inc(std_ready, 1)

        def square(src, junk, col):
            if squared[0]:
                act.wait_ge(sq_done, squared[0])
            squared[0] += 1
            act.activation(junk, src, ACT.Square, accum_out=SS[:, col:col + 1]).then_inc(sq_done, 1)

        def shift(q):
            act.wait_ge(used, ada_end(q))
            if 2 <= q < 6:
                act.wait_ge(row_tr, q - 1)
            elif q >= 6:
                act.wait_ge(mod_stored[q % 2], 16 * ((q - 4) // 2))
            hi, lo = ada_rows(q)
            act.activation(hi, ps[0:2, 7, :], ACT.Copy)
            act.activation(lo, ps[32:34, 7, :], ACT.Copy).then_inc(ada_shift, 1)

        def norm_hi(s, st):
            for u in range(4):
                n = 8 * s + 4 * st + u
                act.wait_ge(tf_ready, n + 1)
                act.activation(HT[:, 0, 2 * u:2 * u + 2, 256 * st:256 * st + 256],
                               TF[s][:, n % 2, :].rearrange("p (k t) -> p k t", k=2), ACT.Copy).then_inc(ht_hi, 1)

        def square_products(p, tiles):
            for t in tiles:
                square(ps[:, 2 * t:2 * t + 2, :], POST[p][3].rearrange("p (a b) -> p a b", a=2), t)

        def xn(s, event_n, tiles):
            act.wait_ge(rstd_ready, event_n)
            for t in tiles:
                act.activation(XN[s][:, t, :], RES[:, t, :], ACT.Copy, scale=RSTD[:, 4 + t:5 + t]).then_inc(xn_ready, 1)

        def boundary(p, first):
            s = p + 1
            for st in range(2):
                tiles = (2 * st, 2 * st + 1)
                if st == 0:
                    hi_upto(first + 1)
                act.wait_ge(prod_done, p + 1) if st == 0 else act.wait_ge(used, first)
                square_products(p, tiles)
                if st == 1:
                    norm_hi(s, 0)
                    hi_upto(first + SPL)
                sqrt(2 * st, 2)
                if st == 0:
                    hi_upto(first + 2)
                for t in tiles:
                    act.wait_ge(post_done, 4 * p + t + 1)
                    square(RES[:, t, :], POST[p][3], 4 + t)
                sqrt(4 + 2 * st, 2)
                xn(s, 2 * p + st + 2, tiles[:1])
            norm_hi(s, 1)

        def act_hi_part(k):
            act.wait_ge(act_done, k // 2 + 1)
            if k >= 10:
                act.wait_ge(used, B_FFNOUT + (k - 8) // 2 + 1)
            elif k >= 2:
                act.wait_ge(used, B_FFNOUT)
            act.activation(act_split(0, k), ACTF[:, k, :], ACT.Copy).then_inc(hidden_hi, 1)

        act.wait_ge(crow_in, 48)
        act.activation(MROW[0:16, 1, :], MROW[0:16, 0, :], ACT.Silu).then_inc(crow_silu, 1)
        act.wait_ge(cond_tr, 1)
        act.wait_ge(dve_chain, 1)
        act.activation(CST[:, :, 0:2], ps[:, 7, 0:16].rearrange("p (s k) -> p k s", s=2),
                       ACT.Copy).then_inc(cond_hi, 1)
        hi_upto(SPL)
        for q in range(4):
            hi_upto(2 * q + 1 + SPL)
            shift(q)
            hi_upto(2 * q + 2 + SPL)
            if q == 1:
                act.wait_ge(res_in, 64)
                for t in range(TILES):
                    square(RES[:, t, :], JUNK0, 4 + t)
                sqrt(4, 4)
            if q == 2:
                xn(0, 1, range(TILES))
        for st in range(2):
            norm_hi(0, st)
        hi_upto(B_MIXIN + 2 + SPL)
        act.wait_ge(used, B_MIXIN + 2)
        act.activation(F_N, ps[:, 0:4, :], ACT.Copy).then_inc(f_copied, 1)
        hi_upto(B_MIXIN + 4 + SPL)
        act.wait_ge(used, B_MIXIN + 4)
        for t in range(2, 4):
            ins = act.activation(Q_N[:, t, :].rearrange("p (j g d) -> p g j d", g=2, j=4),
                                 ps[:, 4 + t, :].rearrange("p (g j d) -> p g j d", g=2, j=4), ACT.Copy)
        ins.then_inc(q_ctx, 1)
        hi_upto(B_MIXIN + 5 + SPL)
        act.wait_ge(used, B_MIXIN + 5)
        act.activation(K_N[:, 2:4, :], ps[:, 2:4, 0:P], ACT.Copy)
        act.activation(V0[:, 2:4, :], ps[:, 2:4, P:2 * P], ACT.Copy).then_inc(kv_ctx, 1)
        for n in range(9):
            if n < 8:
                act.wait_ge(dft1, n + 1)
                if n >= 2:
                    act.wait_ge(dft2, n - 1)
                act.activation(AT0[:, n % 2, :], ps[:, 4 + n % 2, :], ACT.Copy).then_inc(at_ready, 1)
            if n >= 1:
                u = n - 1
                act.wait_ge(dft2, u + 1)
                act.activation(HT[:, 0, u % 4, 256 * (u // 4):256 * (u // 4) + 256], ps[:, 6 + u % 2, 0:256],
                               ACT.Copy).then_inc(z_hi, 1)
        act.wait_ge(qk_tr, 1)
        act.activation(KT0, ps[:, 0, :], ACT.Copy).then_inc(qk_evac, 1)
        for j in range(4):
            act.wait_ge(qk_tr, j + 2)
            act.activation(QT0[:, j, :], ps[:, (j + 1) % 4, :], ACT.Copy).then_inc(qk_evac, 1)
        def exps0(g):
            nk = 512 if g < 4 else 256
            act.wait_ge(negmax, g + 1)
            if g:
                act.wait_ge(p_tr, 4 * min(g, 4) + 2 * max(g - 4, 0))
            for j in range(4):
                act.activation(PR0[:, j, 0:nk], ps[:, j, 0:nk], ACT.Exp, bias=NEGM[:, j:j + 1], scale=SCALE,
                               accum_out=SUMS[:, j:j + 1])
            act.activation(ES[:], TS[:], ACT.Exp).then_inc(exps, 1)

        exps0(0)
        qn = 4
        for g in range(8):
            u = ATT0_U[g]
            nk = 512 if g < 4 else 256
            base = 4 * min(g, 4) + 2 * max(g - 4, 0)
            hi_upto(u + 1 + SPL)
            shift(qn)
            hi_upto(u + 2 + SPL)
            for c_ in range(nk // P):
                act.wait_ge(p_tr, base + c_ + 1)
                act.activation(PT0[:, c_, :], ps[:, 4 + c_ % 2, :],
                               ACT.Copy).then_inc(pt_even if c_ % 2 == 0 else pt_odd, 1)
            if ATT0_CHUNKS[g] == 2:
                hi_upto(u + 3 + SPL)
                shift(qn + 1)
            if g < 7:
                exps0(g + 1)
            if ATT0_CHUNKS[g] == 2:
                hi_upto(u + 4 + SPL)
            qn += ATT0_CHUNKS[g]
            act.wait_ge(pv_done, g + 1)
            kv, t = g % 2, g // 2
            act.activation(HT[HD * kv:HD * kv + HD, 0, 4:8, t * P:t * P + P],
                           ps[HD * kv:HD * kv + HD, 6, :].rearrange("p (j q) -> p j q", j=4),
                           ACT.Copy).then_inc(z_hi, 1)
        hi_upto(B_MIXOUT + 2 + SPL)
        boundary(0, B_FFNIN)
        for i in range(FG):
            if i == FG - 1:
                act_hi_part(0)
                act_hi_part(1)
            hi_upto(B_FFNIN + 2 * i + 1 + SPL)
            if i < FG - 1:
                hi_upto(B_FFNIN + 2 * i + 2 + SPL)
            act.wait_ge(used, B_FFNIN + 2 * i + 2)
            if i:
                act.wait_ge(act_done, i)
            b0 = 4 * (i % 2)
            act.activation(SILF, ps[:, b0:b0 + 2, :], ACT.Silu).then_inc(silu_done, 1)
        for m in range(-SPLIT_AHEAD, FG - 2 + 1):
            hi_upto(B_FFNOUT + m + SPL)
            for k in range(2 * (m + SPLIT_AHEAD), 2 * (m + SPLIT_AHEAD) + 2):
                if 2 <= k < 2 * FG:
                    act_hi_part(k)
        boundary(1, B_QKV)
        def nat_evac_q(n):
            act.wait_ge(nat_tr, n + 1)
            b0 = 4 * (n % 2)
            if n < 2:
                act.activation(QT1[:, 4 * n:4 * n + 4, :],
                               ps[:, b0 + 2:b0 + 4, :].rearrange("p b (j t) -> p (b j) t", j=2),
                               ACT.Copy).then_inc(nat_evac, 1)
            else:
                act.activation(KT1[:, 4 * (n - 2):4 * (n - 2) + 4, :], ps[:, b0:b0 + 4, :],
                               ACT.Copy).then_inc(nat_evac, 1)

        for n in range(6):
            b0 = 4 * (n % 2)
            hi_upto(B_QKV + 2 * n + 1 + SPL)
            if 1 <= n <= 4:
                nat_evac_q(n - 1)
            hi_upto(B_QKV + 2 * n + 2 + SPL)
            act.wait_ge(used, B_QKV + 2 * n + 2)
            if n in (2, 3):
                act.wait_ge(nat_tr, n)
                act.activation(NAT[:, 2:4, :], ps[:, b0 + 2:b0 + 4, :], ACT.Copy).then_inc(nat_ctx, 1)
            if n >= 4:
                act.activation(V1[:, 0:2, 512 * (n - 4):512 * (n - 4) + 512], ps[:, b0:b0 + 2, :],
                               ACT.Copy).then_inc(v_even, 1)
        act.wait_ge(lam_dve, 1)
        act.activation(LAM[:, 2:4], LAM[:, 0:2], ACT.Exp).then_inc(lam_exp, 1)
        def exps1(g):
            act.wait_ge(negmax, 8 + g + 1)
            if g:
                act.wait_ge(p_tr, 24 + 2 * g)
            for j in range(4):
                ins = act.activation(P1[:, j, :], ps[:, j, :], ACT.Exp, bias=NEGM[:, j:j + 1], scale=SCALE,
                                     accum_out=SUMS[:, j:j + 1])
            ins.then_inc(exps, 1)

        exps1(0)
        for g in range(8):
            u, t, hp = ATT1_U[g], g // 4, g % 4
            hi_upto(u + 1 + SPL)
            shift(16 + g)
            hi_upto(u + 2 + SPL)
            act.wait_ge(p_tr, 24 + 2 * g + 1)
            act.wait_ge(pv_done, 8 + g)
            act.activation(PT1[:, 0:2, :], ps[:, 4, :].rearrange("p (c q) -> p c q", c=2),
                           ACT.Copy).then_inc(pt_even, 1)
            act.wait_ge(p_tr, 24 + 2 * g + 2)
            act.activation(PT1[:, 2:4, :], ps[:, 5, :].rearrange("p (c q) -> p c q", c=2),
                           ACT.Copy).then_inc(pt_odd, 1)
            if g < 7:
                exps1(g + 1)
            act.wait_ge(pv_done, 8 + g + 1)
            act.activation(OA[:, t, 256 * hp:256 * hp + 256], ps[:, 6, 0:256], ACT.Copy)
            if g:
                act.wait_ge(o_raw, g)
            for hh in range(2):
                n_ = t * 8 + 2 * hp + hh
                ins = act.activation(T2[:, P * hh:P * hh + P], ps[:, 6, P * hh:P * hh + P], ACT.Square,
                                     accum_out=SS[:, n_:n_ + 1])
            ins.then_inc(o_raw, 1)
            if g == 5:
                sqrt(0, 8)
        sqrt(8, 8)
        act.wait_ge(lam_dve, 2)
        for b in range(4):
            act.wait_ge(o_tr, b + 1)
            act.activation(ZT[:, 0, 2 * b:2 * b + 2, :], ps[:, b, :].rearrange("p (h t) -> p h t", h=2), ACT.Copy,
                           scale=GSUB[:, 1:2]).then_inc(z_hi, 1)
        hi_upto(B_DOUT + 2 + SPL)
        for t in range(XT):
            act.wait_ge(prod_done, 3) if t == 0 else act.wait_ge(used, B_MOE)
            square_products(2, (t,))
            sqrt(t, 1)
        for t in range(XT):
            act.wait_ge(post_done, 9 + t)
            square(RES[:, t, :], POST[2][3], 4 + t)
        sqrt(4, 2)
        hi_upto(B_MOE + SPL)
        for b in range(4):
            act.wait_ge(h_tr, b + 1)
            act.activation(HTF[:, 4 * (b % 2):4 * (b % 2) + 4, P * (b // 2):P * (b // 2) + P],
                           ps[:, b, :].rearrange("p (k t) -> p k t", k=4), ACT.Copy).then_inc(h_evac, 1)
        act.wait_ge(d_ready, 1)
        act.activation(LG[:, 9, :, 0:1], LG[:, 9, :, 1:2], ACT.Exp).then_inc(e_ready, 1)

        def experts(rnd):
            base = moe_base(rnd)

            def hte(e):
                act.wait_ge(gather_rdy, 9 * rnd + e + 1)
                act.activation(HTE[:, 0, :, :], ps[:, 2:4, :].rearrange("p b (k s) -> p (b k) s", k=4),
                               ACT.Copy).then_inc(hte_hi, 1)

            def yhi(n, end):
                act.wait_ge(used, end)
                act.wait_ge(gs_done, n)
                act.activation(YS[:, 0, :].rearrange("p (a b) -> p a b", a=2), ps[:, 4:6, :], ACT.Copy,
                               scale=GS[:, 0:1]).then_inc(y_hi, 1)

            def split(e, i):
                s = (B_MOE + i) % RAW
                act.wait_ge(landed[s], moe_landed(rnd, e, i))
                act.wait_ge(used, base + e * EB + (i - SPL + 1))
                act.activation(WHI[:, (B_MOE + i) % SPL, :], WRAW[:, s, :], ACT.Copy).then_inc(hi_done, 1)

            def rest(e, i):
                J = EJ * NE * rnd + e * EJ
                if i == 1:
                    hte(e)
                if i == 2:
                    yhi(9 * rnd + e + 1, base + e * EB)
                if i == 15:
                    act.wait_ge(ptt_ready, NE * rnd + e + 1)
                    act.activation(PTR[:], ps[:, 7, 0:2 * P], ACT.Copy).then_inc(pt_done, 1)
                for j in range(EJ):
                    if i == 4 * j + 6:
                        act.wait_ge(used, base + e * EB + (4 * j + 4))
                        if j >= 2:
                            act.wait_ge(act_done, FG + J + (j - 1))
                        act.activation(SIL[:, j % 2, :], ps[:, 2 * (j % 2), :], ACT.Silu).then_inc(silu_done, 1)
                    if i == 4 * j + 9:
                        act.wait_ge(tr_ready, J + (j + 1))
                        act.activation(ACTT[:, 0, 4 * j:4 * j + 4, :],
                                       ps[:, 6, :].rearrange("p (k s) -> p k s", k=4),
                                       ACT.Copy).then_inc(act_hi, 1)

            def blocks_of(e, first, last):
                for i in range(first, last):
                    split(e, i)
                    rest(e, i)

            for i in range(SPL):
                if rnd:
                    split(0, i)
                rest(0, i)
            with act.Fori(0, NE - 1) as e:
                blocks_of(e, SPL, EB)
                blocks_of(e + 1, 0, SPL)
            blocks_of(NE - 1, SPL, EB)
            yhi(9 * rnd + 9, base + NE * EB)

        experts(0)
        act.wait_ge(flag_rdy, 1)
        more = act.value_load(CNT[0:1, 0:1], min_val=0, max_val=1)
        with act.If(more > 0):
            experts(1)
        act.end_ifs()
        sqrt(4, 2)

    @block.tensor
    def _(pe):
        def mm(out_, l, r, first, last):
            return pe.matmul(out_, l, r, start=first, stop=last, skip_group_check=True)

        def split3(outs, lh, ll, whs, wls, first, last):
            for n, o in enumerate(outs):
                mm(o, lh, whs[n], first, False)
                mm(o, lh, wls[n], False, False)
            for n, o in enumerate(outs):
                ins = mm(o, ll, whs[n], False, last)
            return ins

        def ada(q, b):
            if q:
                pe.wait_ge(ada_shift, q)
            for h in range(2):
                pe.wait_ge(lo_done, b + h + 1)
                for k in range(4):
                    for w in (WHI, WLO):
                        v = w[:, (b + h) % SPL, :].rearrange("p (k n) -> p k n", k=4)
                        ins = mm(ps[:, 7, :], CST[:, 4 * h + k, :], v[:, k, :], h == 0 and k == 0 and w is WHI,
                                 h == 1 and k == 3 and w is WLO)
                ins.then_inc(used, 1)

        def norm_tr_stage(s, st):
            pe.wait_ge(xn_ready, 4 * s + 2 * st + 2)
            if st == 0 and s:
                pe.wait_ge(rows_in[s], 48)
                pe.transpose(ps[:, 3, 0:40], MROW[0:40, s % 2, :], ID[0:40, 0:40]).then_inc(cols_tr, 1)
            elif s == 0:
                pe.wait_ge(ada_shift, 4)
                pe.wait_ge(cols_read, 1)
            for u in range(4):
                if st == 0 and u == 3 and s:
                    pe.wait_ge(cols_read, s + 1)
                bank = UNIT_BANK[s][st][u]
                for k in range(2):
                    for t in range(2):
                        ins = pe.transpose(ps[:, bank, 256 * k + P * t:256 * k + P * t + P],
                                           XN[s][:, 2 * st + t, (2 * u + k) * P:(2 * u + k + 1) * P], ID[:])
                ins.then_inc(norm_tr, 1)

        def linear(b, src, streams, banks, before=None, done=None, between=None,
                   at=5, step=1):
            for i, tiles in enumerate(streams):
                for h in range(2):
                    pe.wait_ge(lo_done, b + h + 1)
                    wh = WHI[:, (b + h) % SPL, :].rearrange("p (k n) -> p k n", k=4)
                    wl = WLO[:, (b + h) % SPL, :].rearrange("p (k n) -> p k n", k=4)
                    for k in range(4):
                        kk = 4 * h + k
                        if between and i == 0 and kk == at:
                            between()
                        if before:
                            before(i, kk)
                        for t in tiles:
                            ins = split3([ps[:, banks + step * t, :]], src[:, 0, kk, t * P:(t + 1) * P],
                                         src[:, 1, kk, t * P:(t + 1) * P], [wh[:, k, :]], [wl[:, k, :]],
                                         kk == 0, kk == 7)
                    if i == len(streams) - 1:
                        ins.then_inc(used, 1)
                    elif h == 1 and done:
                        ins.then_inc(prod_done, 1)

        pe.wait_ge(crow_silu, 1)
        pe.transpose(ps[:, 7, 0:16], MROW[0:16, 1, :], ID[0:16, 0:16]).then_inc(cond_tr, 1)
        pe.wait_ge(cond_lo, 1)

        def row_transposes(q):
            pe.wait_ge(ada_row, q + 1)
            for j in range(4):
                at = 2 * (4 * q + j)
                ins = pe.transpose(ps[:, 6, at:at + 2], ada_rows(q)[0][:, j * P:(j + 1) * P], ID[0:2, 0:2])
            ins.then_inc(row_tr, 1)

        for q in range(4):
            ada(q, 2 * q)
            if q:
                row_transposes(q - 1)
        pe.wait_ge(rows_in[0], 16)
        pe.transpose(ps[:, 5, 0:8], MROW[32:40, 0, :], ID[32:40, 32:40]).then_inc(cols_tr, 1)
        row_transposes(3)
        def wait_ht(s):
            return lambda st, kk: pe.wait_ge(ht_lo, 8 * s + 4 * st + kk // 2 + 1)

        norm_tr_stage(0, 0)
        linear(B_MIXIN, HT, [(0, 1), (2, 3)], 0, before=wait_ht(0), between=lambda: norm_tr_stage(0, 1),
               at=2)
        linear(B_MIXIN + 2, HT, [range(4)], 4)
        pe.wait_ge(f_copied, 1)
        b = B_MIXIN + 4
        pe.wait_ge(lo_done, b + 1)
        wh = WHI[:, b % SPL, :].rearrange("p (k n) -> p k n", k=8)
        wl = WLO[:, b % SPL, :].rearrange("p (k n) -> p k n", k=8)
        for t in range(TILES):
            for k in range(DK):
                ins = split3([ps[:, t, 0:256]], HT[:, 0, k, t * P:(t + 1) * P], HT[:, 1, k, t * P:(t + 1) * P],
                             [wh[:, k, :]], [wl[:, k, :]], k == 0, k == 7)
        ins.then_inc(used, 1)
        pe.wait_ge(tab_in, 48)
        pe.wait_ge(q_x, 1)
        pe.wait_ge(q_ctx, 1)
        for n in range(9):
            if n < 8:
                st, gr = n // 4, n % 4
                if n >= 2:
                    pe.wait_ge(at_ready, n - 1)
                for tt in range(2):
                    ins = mm(ps[:, 4 + n % 2, :], F_N[:, 2 * st + tt, gr * P:(gr + 1) * P],
                             DFT[:, 512 * tt:512 * tt + 512], tt == 0, tt == 1)
                ins.then_inc(dft1, 1)
            if n >= 1:
                u = n - 1
                pe.wait_ge(at_ready, u + 1)
                if u >= 2:
                    pe.wait_ge(z_lo, u - 1)
                mm(ps[:, 6 + u % 2, 0:256], DFT[:, 1024:1152], AT0[:, u % 2, 0:256], True, False)
                mm(ps[:, 6 + u % 2, 0:256], DFT[:, 1152:1280], AT0[:, u % 2, 256:512], False,
                   True).then_inc(dft2, 1)
        pe.wait_ge(kv_ctx, 1)
        pe.wait_ge(kv_x, 1)
        for t in range(TILES):
            ins = pe.transpose(ps[:, 0, t * P:(t + 1) * P], K_N[:, t, :], ID[:])
        ins.then_inc(qk_tr, 1)
        for j in range(4):
            if j == 3:
                pe.wait_ge(qk_evac, 1)
            for t in range(TILES):
                ins = pe.transpose(ps[:, (j + 1) % 4, t * P:(t + 1) * P], Q_N[:, t, j * P:(j + 1) * P], ID[:])
            ins.then_inc(qk_tr, 1)

        def scores0(g):
            t, kv = g // 2, g % 2
            p0 = HD * kv
            if g == 0:
                pe.wait_ge(qk_evac, 5)
            else:
                pe.wait_ge(exps, g)
            for j in range(4):
                q_ = QT0[p0:p0 + HD, j, t * P:(t + 1) * P]
                if t < XT:
                    mm(ps[:, j, :], q_, KT0[p0:p0 + HD, :], True, False)
                    far = P * (1 - t)
                    ins = mm(ps[:, j, far:far + P], ID[:], TRI[:, P * t:P * t + P], False, True)
                else:
                    ins = mm(ps[:, j, 0:256], q_, KT0[p0:p0 + HD, 256:512], True, True)
            ins.then_inc(scores, 1)

        scores0(0)
        pe.wait_ge(z_lo, 8)
        qn = 4
        trs = 0
        for g in range(8):
            u = ATT0_U[g]
            t, kv = g // 2, g % 2
            ada(qn, u)
            if g < 7:
                scores0(g + 1)
            pe.wait_ge(prob_scaled, g + 1)
            nk = 4 if g < 4 else 2
            for c_ in range(nk):
                if trs + c_ >= 2:
                    n_before = (trs + c_) // 2
                    pe.wait_ge(pt_even if c_ % 2 == 0 else pt_odd, n_before)
                for j in range(4):
                    ins = pe.transpose(ps[:, 4 + c_ % 2, j * P:(j + 1) * P], PR0[:, j, c_ * P:(c_ + 1) * P], ID[:])
                ins.then_inc(p_tr, 1)
            trs += nk
            if ATT0_CHUNKS[g] == 2:
                ada(qn + 1, u + 2)
            qn += ATT0_CHUNKS[g]
            pe.wait_ge(z_lo, 8 + g)
            for c_ in range(nk):
                pe.wait_ge(pt_even if c_ % 2 == 0 else pt_odd, (trs - nk) // 2 + c_ // 2 + 1)
                tk = c_ if g < 4 else c_ + 2
                ins = mm(ps[HD * kv:HD * kv + HD, 6, :], V0[:, tk, HD * kv:HD * kv + HD], PT0[:, c_, :],
                         c_ == 0, c_ == nk - 1)
            ins.then_inc(pv_done, 1)
        pe.wait_ge(z_lo, 16)
        linear(B_MIXOUT, HT, [range(4)], 0, step=2)
        linear(B_MIXOUT + 2, HT, [(0, 1), (2, 3)], 1, done=True, step=2)
        norm_tr_stage(1, 0)
        for i in range(FG):
            if i >= 2:
                pe.wait_ge(act_done, i - 1)
            b0 = 4 * (i % 2)
            parts = ((0, 256), (256, 512)) if i == 0 else ((0, 512),)
            for part, (t0, t1) in enumerate(parts):
                if part == 1:
                    norm_tr_stage(1, 1)
                for h in range(2):
                    b = B_FFNIN + 2 * i + h
                    pe.wait_ge(lo_done, b + 1)
                    wh = WHI[:, b % SPL, :].rearrange("p (k u n) -> p k u n", k=4, u=2)
                    wl = WLO[:, b % SPL, :].rearrange("p (k u n) -> p k u n", k=4, u=2)
                    for k in range(4):
                        kk = 4 * h + k
                        if i == 0:
                            wait_ht(1)(part, max(kk, 4) if part == 0 else kk)
                        for u in range(2):
                            for f in range(2):
                                o = ps[:, b0 + 2 * u + f, t0:t1]
                                mm(o, wh[:, k, u, f * P:(f + 1) * P], HT[:, 0, kk, t0:t1], kk == 0, False)
                                mm(o, wh[:, k, u, f * P:(f + 1) * P], HT[:, 1, kk, t0:t1], False, False)
                                ins = mm(o, wl[:, k, u, f * P:(f + 1) * P], HT[:, 0, kk, t0:t1], False, kk == 7)
                    if part == len(parts) - 1:
                        ins.then_inc(used, 1)

        def second_product(m, tiles):
            b = B_FFNOUT + m
            pe.wait_ge(lo_done, b + 1)
            wh = WHI[:, b % SPL, :].rearrange("p (k n) -> p k n", k=4)
            wl = WLO[:, b % SPL, :].rearrange("p (k n) -> p k n", k=4)
            for k in range(2):
                kk = 2 * m + k
                pe.wait_ge(hidden_lo, kk + 1)
                for t in (2, 3, 0, 1) if kk == 0 else tiles:
                    if kk == 0 and t == 0:
                        pe.wait_ge(act_done, FG)
                    ins = split3([ps[:, 2 * t + n, :] for n in range(2)], act_split(0, kk)[:, t * P:(t + 1) * P],
                                 act_split(1, kk)[:, t * P:(t + 1) * P], [wh[:, 2 * k + n, :] for n in range(2)],
                                 [wl[:, 2 * k + n, :] for n in range(2)], kk == 0, kk == 2 * FG - 1)
            return ins

        for m in range(FG - 2):
            second_product(m, range(4)).then_inc(used, 1)
        for st in range(2):
            for m in (FG - 2, FG - 1):
                ins = second_product(m, (2 * st, 2 * st + 1))
                if st == 1:
                    ins.then_inc(used, 1)
            if st == 0:
                ins.then_inc(prod_done, 1)
        norm_tr_stage(2, 0)

        def nat_transposes(n):
            b0 = 4 * (n % 2)
            if n < 2:
                pe.wait_ge(nat_x, n + 1)
                wait_ht(2)(1, DK - 1)
                for j in range(4):
                    for t in range(XT):
                        ins = pe.transpose(ps[:, b0 + 2 + j // 2, (j % 2) * 256 + t * P:(j % 2) * 256 + t * P + P],
                                           NAT[:, t, j * P:(j + 1) * P], ID[:])
            else:
                pe.wait_ge(nat_x, n + 1)
                pe.wait_ge(nat_ctx, n - 1)
                for j in range(4):
                    for t in range(TILES):
                        ins = pe.transpose(ps[:, b0 + j, t * P:(t + 1) * P], NAT[:, t, j * P:(j + 1) * P], ID[:])
            ins.then_inc(nat_tr, 1)

        for n in range(6):
            if n >= 2:
                pe.wait_ge(nat_evac, n - 1)
            if n == 1:
                pe.wait_ge(post_done, 2 * TILES)
            between = {1: lambda: norm_tr_stage(2, 1), 2: lambda: nat_transposes(1), 3: lambda: nat_transposes(2),
                       4: lambda: nat_transposes(3)}.get(n)
            linear(B_QKV + 2 * n, HT, [range(2) if n < 2 else range(4)], 4 * (n % 2), between=between,
                   at=2 if n == 1 else 5, before=wait_ht(2) if n == 0 else None)
            if n == 1:
                nat_transposes(0)

        def scores1(g):
            t, hp = g // 4, g % 4
            if g:
                pe.wait_ge(exps, 8 + g)
            else:
                pe.wait_ge(nat_evac, 4)
            for j in range(4):
                h, p0 = 2 * hp + j // 2, HD * (j % 2)
                ins = mm(ps[:, j, :], QT1[p0:p0 + HD, h, t * P:(t + 1) * P], KT1[p0:p0 + HD, h, :], True, True)
            ins.then_inc(scores, 1)

        pe.wait_ge(v_even, 1)
        pe.wait_ge(v_odd, 1)
        scores1(0)
        pe.wait_ge(v_even, 2)
        pe.wait_ge(v_odd, 2)
        for g in range(8):
            ada(16 + g, ATT1_U[g])
            if g < 7:
                scores1(g + 1)
            pe.wait_ge(prob_scaled, 8 + g + 1)
            for hb in range(2):
                if g:
                    pe.wait_ge(pt_even if hb == 0 else pt_odd, 12 + g)
                for cc in range(2):
                    for hh in range(2):
                        o = ps[:, 4 + hb, cc * 256 + hh * P:cc * 256 + hh * P + P]
                        ins = pe.transpose(o, P1[:, 2 * hh, (2 * hb + cc) * P:(2 * hb + cc + 1) * P], ID[:])
                ins.then_inc(p_tr, 1)
            if g:
                pe.wait_ge(o_raw, g)
            pe.wait_ge(pt_even, 12 + g + 1)
            pe.wait_ge(pt_odd, 12 + g + 1)
            for hh in range(2):
                h = 2 * (g % 4) + hh
                for c_ in range(4):
                    ins = mm(ps[:, 6, hh * P:(hh + 1) * P], PT1[:, c_, hh * P:(hh + 1) * P],
                             V1[:, c_, h * P:(h + 1) * P], c_ == 0, c_ == 3)
            ins.then_inc(pv_done, 1)
        pe.wait_ge(o_norm, 2)
        for b_ in range(4):
            for hh in range(2):
                for t in range(XT):
                    h = 2 * b_ + hh
                    ins = pe.transpose(ps[:, b_, hh * 256 + t * P:hh * 256 + t * P + P],
                                       OA[:, t, h * P:(h + 1) * P], ID[:])
            ins.then_inc(o_tr, 1)
        pe.wait_ge(z_lo, 20)
        linear(B_DOUT, ZT, [range(2)], 0, step=2)
        linear(B_DOUT + 2, ZT, [(0,), (1,)], 1, done=True, step=2)
        pe.wait_ge(small_in, 32)
        for t in range(XT):
            pe.wait_ge(hn_done, t + 1)
            for k in range(DK):
                ins = pe.transpose(ps[:, 2 * t + k // 4, (k % 4) * P:(k % 4 + 1) * P],
                                   HN[:, t, k * P:(k + 1) * P], ID[:])
                if k % 4 == 3:
                    ins.then_inc(h_tr, 1)
            for k in range(DK):
                pe.wait_ge(h_evac, 2 * t + k // 4 + 1)
                ins = mm(ps[:, 4, t * NE:(t + 1) * NE], HTF[:, k, t * P:(t + 1) * P], RW[:, k, :], k == 0, k == DK - 1)
        ins.then_inc(logits_rdy, 1)
        pe.wait_ge(assign_rdy, 1)
        pe.wait_ge(tm_in, 16)
        A0, A1 = LG[:, 6, 0, :], LG[:, 6, 1, :]
        mm(ps[:, 5, 0:8], UPPER, A0, True, True)
        mm(ps[:, 5, 8:16], ONES, A0, True, False)
        mm(ps[:, 5, 8:16], UPPER, A1, False, True)
        mm(ps[:, 5, 16:24], ONES, A0, True, False)
        mm(ps[:, 5, 16:24], ONES, A1, False, True).then_inc(pos_rdy, 1)

        def experts(rnd):
            base = moe_base(rnd)

            def gather(n):
                pe.wait_ge(onehot_rdy, n)
                for k in range(DK):
                    for t in range(XT):
                        ins = mm(ps[:, 2 + k // 4, (k % 4) * P:(k % 4 + 1) * P], HN[:, t, k * P:(k + 1) * P],
                                 ONEHOT[:, t, :], t == 0, t == XT - 1)
                ins.then_inc(gather_rdy, 1)

            def combine(n, i, bank=7):
                t, h = i // 2, i % 2
                if bank == 7:
                    pe.wait_ge(acc_done, n * 4 + (i + 1))
                for q in range(2):
                    ins = mm(ps[:, bank, :], PTR[:, t * P:(t + 1) * P], YS[:, q, 512 * h:512 * h + 512], q == 0, q == 1)
                ins.then_inc(comb_rdy, 1)

            gather(9 * rnd + 1)
            with pe.Fori(0, NE) as e:
                J = EJ * NE * rnd + e * EJ
                for i in range(EB):
                    slot = (B_MOE + i) % SPL
                    wh = WHI[:, slot, :].rearrange("p (k n) -> p k n", k=4)
                    wl = WLO[:, slot, :].rearrange("p (k n) -> p k n", k=4)
                    if i == 0:
                        pe.wait_ge(hte_lo, NE * rnd + e + 1)
                    if i < IN_BLOCKS:
                        j = i // 4
                        if i % 4 == 0 and j >= 2:
                            pe.wait_ge(act_done, FG + J + (j - 1))
                        pe.wait_ge(lo_done, base + e * EB + (i + 1))
                        for k in range(2):
                            kk = 2 * (i % 4) + k
                            ins = split3([ps[:, 2 * (j % 2), :], ps[:, 2 * (j % 2) + 1, :]], HTE[:, 0, kk, :],
                                         HTE[:, 1, kk, :], [wh[:, 2 * k + n, :] for n in range(2)],
                                         [wl[:, 2 * k + n, :] for n in range(2)], kk == 0, kk == 7)
                    else:
                        m = i - IN_BLOCKS
                        if m == 0:
                            pe.wait_ge(y_lo, 9 * rnd + e + 1)
                        pe.wait_ge(act_lo, J + (m // 2 + 1))
                        pe.wait_ge(lo_done, base + e * EB + (i + 1))
                        for k in range(2):
                            kk = 2 * m + k
                            ins = split3([ps[:, 4, :], ps[:, 5, :]], ACTT[:, 0, kk, :], ACTT[:, 1, kk, :],
                                         [wh[:, 2 * k + n, :] for n in range(2)],
                                         [wl[:, 2 * k + n, :] for n in range(2)], kk == 0, kk == ED // P - 1)
                    ins.then_inc(used, 1)
                    if 5 <= i < 9:
                        if i == 5:
                            pe.wait_ge(y_lo, 9 * rnd + e + 1)
                            pe.wait_ge(gs_done, 9 * rnd + e + 1)
                        combine(9 * rnd + e, i - 5)
                    if i == 12:
                        pe.wait_ge(acc_done, (9 * rnd + e) * 4 + 5)
                        for t in range(XT):
                            pe.transpose(ps[:, 7, t * P:(t + 1) * P], ONEHOT[:, t, :], ID[:])
                        for t in range(XT):
                            ins = mm(ps[:, 7, 2 * P:2 * P + NE], ONEHOT[:, t, :], G9[:, t, :], t == 0, t == XT - 1)
                        ins.then_inc(ptt_ready, 1)
                    for j in range(EJ):
                        if i == 4 * j + 6:
                            pe.wait_ge(act_done, FG + J + (j + 1))
                            if j >= 1:
                                pe.wait_ge(act_lo, J + j)
                            for k in range(4):
                                ins = pe.transpose(ps[:, 6, k * P:(k + 1) * P], ACTN[:, j % 2, k * P:(k + 1) * P], ID[:])
                            ins.then_inc(tr_ready, 1)
                    if i == 32:
                        gather(9 * rnd + e + 2)
            pe.wait_ge(y_lo, 9 * rnd + 9)
            pe.wait_ge(gs_done, 9 * rnd + 9)
            for i in range(4):
                combine(9 * rnd + 8, i, bank=i)

        experts(0)
        pe.wait_ge(flag_rdy, 1)
        more = pe.value_load(CNT[0:1, 0:1], min_val=0, max_val=1)
        with pe.If(more > 0):
            experts(1)
        pe.end_ifs()

    @block.vector
    def _(dve):
        at = [0]
        links = [0]

        def link(ins):
            links[0] += 1
            ins.then_inc(dve_chain, 1)
            dve.wait_ge(dve_chain, links[0])

        def lo_upto(n):
            for b in range(at[0], min(n, B_MOE + SPL)):
                dve.wait_ge(hi_done, b + 1)
                dve.tensor_tensor(WLO[:, b % SPL, :], WRAW[:, b % RAW, :], WHI[:, b % SPL, :].bitcast(F32),
                                  ALU.subtract).then_inc(lo_done, 1)
            at[0] = max(at[0], n)

        event, squared, rstds = [0], [0], [0]

        def rstd(c0, n, count, lk=link):
            ms, std, y0, y1 = (v[:, c0:c0 + n] for v in (MS, STD, Y0, Y1))
            lk(dve.tensor_scalar(ms, SS[:, c0:c0 + n], 1.0 / count, EPS, ALU.mult, ALU.add))
            dve.sem_inc(ms_ready, 1)
            event[0] += 1
            dve.wait_ge(std_ready, event[0])
            lk(dve.reciprocal(y0, std))
            lk(dve.tensor_tensor(y1, y0, y0, ALU.mult))
            lk(dve.tensor_tensor(y1, y1, ms, ALU.mult))
            lk(dve.tensor_scalar(y1, y1, -0.5, 1.5, ALU.mult, ALU.add))
            lk(dve.tensor_tensor(RSTD[:, c0:c0 + n], y0, y1, ALU.mult))

        def wait_squares(n):
            squared[0] += n
            dve.wait_ge(sq_done, squared[0])

        def modulate(s, st):
            if st == 0:
                if s == 0:
                    dve.wait_ge(row_tr, 4)
                    link(dve.tensor_copy(COL[:, 0:32].rearrange("p (s m) -> p s m", s=2),
                                         ps[:, 6, 0:32].rearrange("p (m s) -> p s m", s=2)))
                    dve.wait_ge(cols_tr, 1)
                    link(dve.tensor_copy(COL[:, 32:40], ps[:, 5, 0:8]))
                else:
                    dve.wait_ge(cols_tr, s + 1)
                    link(dve.tensor_copy(COL[:], ps[:, 3, 0:40]))
                dve.sem_inc(cols_read, 1)
                for i in range(2):
                    ins = dve.scalar_tensor_tensor(out=ACOL[:, i, :], in0=COL[:, 16 * i + 8:16 * i + 16], scalar=1.0,
                                                   in1=COL[:, 32:40], op0=ALU.add, op1=ALU.mult)
                link(ins)

            def low(u):
                n = 8 * s + 4 * st + u
                dve.wait_ge(ht_hi, n + 1)
                cols = slice(256 * st, 256 * st + 256)
                dve.tensor_tensor(HT[:, 1, 2 * u:2 * u + 2, cols], TF[s][:, n % 2, :].rearrange("p (k t) -> p k t", k=2),
                                  HT[:, 0, 2 * u:2 * u + 2, cols].bitcast(F32), ALU.subtract).then_inc(ht_lo, 1)

            for u in range(4):
                n = 8 * s + 4 * st + u
                dve.wait_ge(norm_tr, n + 1)
                if n % 8 >= 2:
                    dve.wait_ge(ht_lo, n - 1)
                for k in range(2):
                    ins = dve.tensor_scalar(TF[s][:, n % 2, 256 * k:256 * k + 256],
                                            ps[:, UNIT_BANK[s][st][u], 256 * k:256 * k + 256],
                                            ACOL[:, st, 2 * u + k:2 * u + k + 1],
                                            COL[:, 16 * st + 2 * u + k:16 * st + 2 * u + k + 1], ALU.mult, ALU.add)
                ins.then_inc(tf_ready, 1)
                if u:
                    low(u - 1)
            low(3)

        def gates(p, count):
            gb, ngb = POST[p][0], POST[p][1]
            dve.wait_ge(gate_in, count)
            for st in range(gb.shape[1]):
                link(dve.tensor_tensor(gb[:, st, :], gb[:, st, :], ngb, ALU.mult))

        def update(p, t):
            gb, _, tmp, _ = POST[p]
            link(dve.scalar_tensor_tensor(out=tmp.rearrange("p (a b) -> p a b", a=2), in0=ps[:, 2 * t:2 * t + 2, :],
                                          scalar=RSTD[:, t:t + 1],
                                          in1=gb[:, t // 2, :].rearrange("p (a b) -> p a b", a=2),
                                          op0=ALU.mult, op1=ALU.mult))
            link(dve.tensor_tensor(RES[:, t, :], RES[:, t, :], tmp, ALU.add))
            dve.sem_inc(post_done, 1)

        def boundary(p, first, count):
            s = p + 1
            lo_upto(first + 1)
            gates(p, count)
            for st in range(2):
                wait_squares(2)
                rstd(2 * st, 2, D)
                for t in (2 * st, 2 * st + 1):
                    update(p, t)
                if st == 0:
                    lo_upto(first + 2)
                wait_squares(2)
                rstd(4 + 2 * st, 2, D)
                dve.sem_inc(rstd_ready, 1)
                t = 2 * st + 1
                dve.tensor_scalar(XN[s][:, t, :], RES[:, t, :], RSTD[:, 4 + t:5 + t], None,
                                  ALU.mult).then_inc(xn_ready, 1)
                modulate(s, st)
                if st == 0:
                    lo_upto(first + SPL)

        def act_lo_part(k):
            dve.wait_ge(hidden_hi, k + 1)
            dve.wait_ge(act_done, k // 2 + 1)
            dve.tensor_tensor(act_split(1, k), ACTF[:, k, :], act_split(0, k).bitcast(F32),
                              ALU.subtract).then_inc(hidden_lo, 1)

        def rotate(dst, src, tile, heads, rot, end=None):
            d5 = dst.rearrange("p (h a s d) -> p h a s d", a=2, s=2, d=16)
            s5 = src.rearrange("p (h a s d) -> p h a s d", a=2, s=2, d=16)
            r5 = rot.rearrange("p (h a s d) -> p h a s d", a=2, s=2, d=16)

            def tab(kind):
                v = ROPE[:, 64 * kind + 32 * tile:64 * kind + 32 * tile + 32].rearrange("p (a d) -> p a d", a=2)
                return v.unsqueeze(1).broadcast_to([P, heads, 2, 16])

            for s_ in range(2):
                dve.tensor_tensor(d5[:, :, :, s_, :], s5[:, :, :, s_, :], tab(0), ALU.mult)
            dve.tensor_tensor(r5[:, :, :, 0, :], s5[:, :, :, 1, :], tab(2), ALU.mult)
            link(dve.tensor_tensor(r5[:, :, :, 1, :], s5[:, :, :, 0, :], tab(1), ALU.mult))
            if end is None:
                link(dve.tensor_tensor(dst, dst, rot, ALU.add))
            else:
                gjd = "p (g j d) -> p g j d"
                link(dve.tensor_tensor(end.rearrange("p (j g d) -> p g j d", g=2, j=4), dst.rearrange(gjd, g=2, j=4),
                                       rot.rearrange(gjd, g=2, j=4), ALU.add))

        link(dve.memset(CST[:].bitcast(F32), 0.0))
        dve.wait_ge(cond_hi, 1)
        dve.tensor_tensor(CST[:, :, 32:34], ps[:, 7, 0:16].rearrange("p (s k) -> p k s", s=2),
                          CST[:, :, 0:2].bitcast(F32), ALU.subtract).then_inc(cond_lo, 1)
        lo_upto(SPL)
        for q in range(4):
            lo_upto(2 * q + 2 + SPL)
            if q == 1:
                wait_squares(4)
                rstd(4, 4, D)
                dve.sem_inc(rstd_ready, 1)
        for st in range(2):
            modulate(0, st)
        dve.wait_ge(tab_in, 48)
        lo_upto(B_MIXIN + 4 + SPL)
        dve.wait_ge(used, B_MIXIN + 4)
        for t in range(XT):
            rotate(QROT, ps[:, 4 + t, :], t, 8, ROT0, Q_N[:, t, :])
        dve.sem_inc(q_x, 1)
        lo_upto(B_MIXIN + 5 + SPL)
        dve.wait_ge(used, B_MIXIN + 5)
        for t in range(XT):
            rotate(K_N[:, t, :], ps[:, t, 0:P], t, 2, ROT0[:, 0:P])
        dve.tensor_copy(V0[:, 0:2, :], ps[:, 0:2, P:2 * P]).then_inc(kv_x, 1)
        for u in range(8):
            dve.wait_ge(z_hi, u + 1)
            o = HT[:, 0, u % 4, 256 * (u // 4):256 * (u // 4) + 256]
            dve.tensor_tensor(HT[:, 1, u % 4, 256 * (u // 4):256 * (u // 4) + 256], ps[:, 6 + u % 2, 0:256],
                              o.bitcast(F32), ALU.subtract).then_inc(z_lo, 1)
        link(dve.tensor_scalar(SINK[:], SINK[:], -1.0, None, ALU.mult))
        def maxima0(g):
            kv, nk = g % 2, 512 if g < 4 else 256
            dve.wait_ge(scores, g + 1)
            link(dve.tensor_reduce(MX[:], ps[:, 0:4, 0:nk], AX_X, ALU.max))
            link(dve.scalar_tensor_tensor(out=NEGM[:], in0=MX[:], scalar=-SCALE, in1=SINK[:, 4 * kv:4 * kv + 4],
                                          op0=ALU.mult, op1=ALU.min))
            dve.tensor_tensor(TS[:], NEGM[:], SINK[:, 4 * kv:4 * kv + 4], ALU.subtract).then_inc(negmax, 1)

        maxima0(0)
        for g in range(8):
            u, kv, t = ATT0_U[g], g % 2, g // 2
            nk = 512 if g < 4 else 256
            lo_upto(u + SPL)
            dve.wait_ge(exps, g + 1)
            link(dve.tensor_tensor(RL[:], SUMS[:], ES[:], ALU.add))
            link(dve.reciprocal(RL[:], RL[:]))
            for j in range(4):
                ins = dve.tensor_scalar(PR0[:, j, 0:nk], PR0[:, j, 0:nk], RL[:, j:j + 1], None, ALU.mult)
            ins.then_inc(prob_scaled, 1)
            lo_upto(u + 2 + SPL)
            if g < 7:
                maxima0(g + 1)
            if ATT0_CHUNKS[g] == 2:
                lo_upto(u + 4 + SPL)
            dve.wait_ge(z_hi, 8 + g + 1)
            rows, cols = slice(HD * kv, HD * kv + HD), slice(t * P, t * P + P)
            dve.tensor_tensor(HT[rows, 1, 4:8, cols], ps[rows, 6, :].rearrange("p (j q) -> p j q", j=4),
                              HT[rows, 0, 4:8, cols].bitcast(F32), ALU.subtract).then_inc(z_lo, 1)
        lo_upto(B_MIXOUT + 2 + SPL)
        boundary(0, B_FFNIN, 48)
        for i in range(FG):
            if i == FG - 1:
                act_lo_part(0)
                act_lo_part(1)
            lo_upto(B_FFNIN + 2 * i + 1 + SPL)
            if i < FG - 1:
                lo_upto(B_FFNIN + 2 * i + 2 + SPL)
            dve.wait_ge(silu_done, i + 1)
            b0 = 4 * (i % 2)
            dve.tensor_tensor(ACTF[:, 2 * i:2 * i + 2, :], SILF, ps[:, b0 + 2:b0 + 4, :],
                              ALU.mult).then_inc(act_done, 1)
        for m in range(-SPLIT_AHEAD, FG - 2 + 1):
            lo_upto(B_FFNOUT + m + SPL)
            for k in range(2 * (m + SPLIT_AHEAD), 2 * (m + SPLIT_AHEAD) + 2):
                if 2 <= k < 2 * FG:
                    act_lo_part(k)
        boundary(1, B_QKV, 96)
        dve.wait_ge(rope_in, 16)
        for n in range(6):
            b0 = 4 * (n % 2)
            lo_upto(B_QKV + 2 * n + 1 + SPL)
            lo_upto(B_QKV + 2 * n + 2 + SPL)
            dve.wait_ge(used, B_QKV + 2 * n + 2)
            if n < 4:
                if n:
                    dve.wait_ge(nat_tr, n)
                for t in range(XT):
                    rotate(NAT[:, t, :], ps[:, b0 + t, :], t, 8, ROT1)
                dve.sem_inc(nat_x, 1)
            else:
                dve.tensor_copy(V1[:, 2:4, 512 * (n - 4):512 * (n - 4) + 512],
                                ps[:, b0 + 2:b0 + 4, :]).then_inc(v_odd, 1)
        dve.wait_ge(lam_in, 16)
        lv = T2[:, 0:256]
        link(dve.tensor_tensor_reduce(MODB[:, 1280:1344], lv[:, 0:64], lv[:, 64:128], 1.0, 0.0, ALU.mult, ALU.add,
                                      LAM[:, 0:1]))
        link(dve.tensor_tensor_reduce(MODB[:, 1344:1408], lv[:, 128:192], lv[:, 192:256], 1.0, 0.0, ALU.mult,
                                      ALU.add, LAM[:, 1:2]))
        dve.sem_inc(lam_dve, 1)
        dve.wait_ge(lam_exp, 1)
        link(dve.tensor_tensor(LAM[:, 1:2], LAM[:, 3:4], LAM[:, 2:3], ALU.subtract))
        link(dve.tensor_scalar(LAM[:, 0:1], LAM[:, 1:2], -LAM_INIT, None, ALU.add))
        dve.wait_ge(small_in, 32)
        link(dve.tensor_scalar(GSUB[:, 1:2], GSUB[:, 0:1], 1.0 - LAM_INIT, None, ALU.mult))
        dve.sem_inc(lam_dve, 1)
        def maxima1(g):
            dve.wait_ge(scores, 8 + g + 1)
            link(dve.tensor_reduce(MX[:], ps[:, 0:4, :], AX_X, ALU.max))
            dve.tensor_scalar(NEGM[:], MX[:], -SCALE, None, ALU.mult).then_inc(negmax, 1)

        def sub_norm(t):
            rstd(8 * t, 8, 2 * HD)
            o = OA[:, t, :].rearrange("p (h d) -> p h d", h=8)
            r = RSTD[:, 8 * t:8 * t + 8].unsqueeze(2).broadcast_to([P, 8, P])
            dve.tensor_tensor(o, o, r, ALU.mult).then_inc(o_norm, 1)

        maxima1(0)
        for g in range(8):
            u = ATT1_U[g]
            lo_upto(u + SPL)
            dve.wait_ge(exps, 8 + g + 1)
            link(dve.reciprocal(RL[:], SUMS[:]))
            link(dve.tensor_scalar(NRL[:], RL[:], LAM[:, 0:1], None, ALU.mult))
            for hh in range(2):
                ins = dve.tensor_scalar(P1[:, 2 * hh, :], P1[:, 2 * hh, :], RL[:, 2 * hh:2 * hh + 1], None, ALU.mult)
            link(ins)
            for hh in range(2):
                ins = dve.scalar_tensor_tensor(out=P1[:, 2 * hh, :], in0=P1[:, 2 * hh + 1, :],
                                               scalar=NRL[:, 2 * hh + 1:2 * hh + 2], in1=P1[:, 2 * hh, :],
                                               op0=ALU.mult, op1=ALU.add)
            ins.then_inc(prob_scaled, 1)
            lo_upto(u + 2 + SPL)
            if g < 7:
                maxima1(g + 1)
            if g == 5:
                dve.wait_ge(o_raw, 4)
                sub_norm(0)
        dve.wait_ge(o_raw, 8)
        sub_norm(1)
        lo_upto(B_DOUT + SPL)
        for b in range(4):
            dve.wait_ge(z_hi, 16 + b + 1)
            dve.scalar_tensor_tensor(out=ZT[:, 1, 2 * b:2 * b + 2, :],
                                     in0=ps[:, b, :].rearrange("p (h t) -> p h t", h=2), scalar=GSUB[:, 1:2],
                                     in1=ZT[:, 0, 2 * b:2 * b + 2, :].bitcast(F32), op0=ALU.mult,
                                     op1=ALU.subtract).then_inc(z_lo, 1)
        lo_upto(B_DOUT + 2 + SPL)
        gates(2, 128)
        dve.wait_ge(moe_in, 48)
        link(dve.scalar_tensor_tensor(out=SCB, in0=SCB, scalar=1.0, in1=NGB, op0=ALU.add, op1=ALU.mult))
        for t in range(XT):
            wait_squares(1)
            rstd(t, 1, D)
            update(2, t)
        wait_squares(2)
        rstd(4, 2, D)
        for t in range(XT):
            link(dve.scalar_tensor_tensor(out=HN[:, t, :], in0=RES[:, t, :], scalar=RSTD[:, 4 + t:5 + t], in1=SCB,
                                          op0=ALU.mult, op1=ALU.mult))
            dve.tensor_tensor(HN[:, t, :], HN[:, t, :], SHB, ALU.add).then_inc(hn_done, 1)
        lo_upto(B_MOE + SPL)
        dve.wait_ge(logits_rdy, 1)
        dve.wait_ge(tm_in, 16)
        L, EQ, CD, O1, L2, O2, AS = (LG[:, n, :, :] for n in range(7))
        M1, M2, I1, I2 = (LG[:, 7, :, 2 * n:2 * n + 1] for n in range(4))
        GT, GA, GB = LG[:, 8, :, 0:1], LG[:, 8, :, 1:2], LG[:, 8, :, 2:3]
        EX, DF = LG[:, 9, :, 0:1], LG[:, 9, :, 1:2]
        io8 = IOTA8.rearrange("p (t e) -> p t e", t=2)
        wide = [P, XT, NE]
        link(dve.tensor_copy(L, ps[:, 4, 0:16].rearrange("p (t e) -> p t e", t=2)))

        def first_max(lg, m, i_, oh):
            link(dve.tensor_reduce(m, lg, AX_X, ALU.max))
            link(dve.tensor_tensor(EQ, lg, m.broadcast_to(wide), ALU.is_equal))
            link(dve.tensor_tensor(CD, EQ, io8, ALU.mult))
            link(dve.tensor_reduce(i_, CD, AX_X, ALU.min))
            link(dve.tensor_tensor(oh, io8, i_.broadcast_to(wide), ALU.is_equal))

        first_max(L, M1, I1, O1)
        link(dve.scalar_tensor_tensor(out=L2, in0=O1, scalar=NEG, in1=L, op0=ALU.mult, op1=ALU.add))
        first_max(L2, M2, I2, O2)
        link(dve.tensor_tensor(AS, O1, O2, ALU.add))
        dve.sem_inc(assign_rdy, 1)
        link(dve.tensor_tensor(DF, M2, M1, ALU.subtract))
        dve.sem_inc(d_ready, 1)
        dve.wait_ge(e_ready, 1)
        link(dve.tensor_scalar(GT, EX, 1.0, None, ALU.add))
        link(dve.reciprocal(GA, GT))
        link(dve.tensor_tensor(GB, GA, EX, ALU.mult))
        link(dve.tensor_tensor(EQ, O1, GA.broadcast_to(wide), ALU.mult))
        link(dve.tensor_tensor(CD, O2, GB.broadcast_to(wide), ALU.mult))
        link(dve.tensor_tensor(G9[:], EQ, CD, ALU.add))
        link(dve.memset(PA[:], 0.0))
        dve.wait_ge(pos_rdy, 1)
        link(dve.tensor_copy(PA[:, 0:NE, 0, :], ps[:, 5, 0:16].rearrange("p (t e) -> p e t", t=2)))
        link(dve.tensor_copy(PA[:, 0:NE, 1, :], AS.rearrange("p t e -> p e t")))

        def overflow_flag():
            link(dve.tensor_reduce(GT[:, 0, :], ps[:, 5, 16:24], AX_X, ALU.max))
            link(dve.tensor_scalar(GT[:, 0, :], GT[:, 0, :], float(P), None, ALU.is_gt))
            link(dve.tensor_copy(CNT[0:1, 0:1], GT[0:1, 0, :]))
            dve.sem_inc(flag_rdy, 1)

        def experts(rnd):
            base = moe_base(rnd)
            n0 = 9 * rnd

            def onehot(src, n):
                dve.tensor_copy(CUR[:], src).then_inc(cur_done, 1)
                dve.wait_ge(cur_done, n)
                for t in range(XT):
                    ins = dve.tensor_scalar(ONEHOT[:, t, :], IOTA, CUR[:, 0, t:t + 1], CUR[:, 1, t:t + 1],
                                            ALU.is_equal, ALU.mult)
                ins.then_inc(onehot_rdy, 1)

            def hte(n):
                dve.wait_ge(hte_hi, n)
                dve.tensor_tensor(HTE[:, 1, :, :], ps[:, 2:4, :].rearrange("p b (k s) -> p (b k) s", k=4),
                                  HTE[:, 0, :, :].bitcast(F32), ALU.subtract).then_inc(hte_lo, 1)

            def ylo(n):
                dve.wait_ge(y_hi, n)
                dve.scalar_tensor_tensor(out=YS[:, 1, :].rearrange("p (a b) -> p a b", a=2), in0=ps[:, 4:6, :],
                                         scalar=GS[:, 0:1],
                                         in1=YS[:, 0, :].bitcast(F32).rearrange("p (a b) -> p a b", a=2),
                                         op0=ALU.mult, op1=ALU.subtract).then_inc(y_lo, 1)

            def accumulate(n, i, bank=7):
                t, h = i // 2, i % 2
                dve.wait_ge(comb_rdy, n * 4 + (i + 1))
                dve.wait_ge(acc_done, n * 4 + (i + 1))
                o = YACC[:, t, 512 * h:512 * h + 512]
                dve.tensor_tensor(o, o, ps[:, bank, :], ALU.add).then_inc(acc_done, 1)

            if rnd:
                dve.wait_ge(gather_rdy, 9)
                dve.tensor_scalar(PA[:, :, 0, :], PA[:, :, 0, :], -float(P), None, ALU.add).then_inc(cur_done, 1)
                dve.wait_ge(cur_done, 10)
            onehot(PA[:, 0, :, :], n0 + rnd + 1)
            if not rnd:
                overflow_flag()
                dve.memset(YACC[:], 0.0).then_inc(acc_done, 1)
            dve.memset(PTR[:].bitcast(F32), 0.0)
            dve.memset(ps[:, 4:6, :], 0.0)
            dve.memset(GS[:], 0.0).then_inc(gs_done, 1)
            def split(e, i):
                slot = (B_MOE + i) % SPL
                dve.wait_ge(hi_done, base + e * EB + (i + 1))
                dve.tensor_tensor(WLO[:, slot, :], WRAW[:, (B_MOE + i) % RAW, :], WHI[:, slot, :].bitcast(F32),
                                  ALU.subtract).then_inc(lo_done, 1)

            def rest(e, i):
                J = EJ * NE * rnd + e * EJ
                if i == 1:
                    hte(NE * rnd + e + 1)
                if i == 2:
                    ylo(n0 + e + 1)
                if 7 <= i < 11:
                    accumulate(n0 + e, i - 7)
                if i == 15:
                    dve.wait_ge(pt_done, NE * rnd + e + 1)
                    dve.wait_ge(y_lo, n0 + e + 1)
                    dve.tensor_copy(GS[:], ps[:, 7, bass.ds(e + 2 * P, 1)]).then_inc(gs_done, 1)
                if i == 21:
                    onehot(PA[:, bass.ds(e + 1, 1), :, :].rearrange("p o a t -> p (o a) t"), n0 + e + (rnd + 2))
                for j in range(EJ):
                    if i == 4 * j + 6:
                        dve.wait_ge(silu_done, FG + J + (j + 1))
                        if j >= 2:
                            dve.wait_ge(tr_ready, J + (j - 1))
                        dve.tensor_tensor(ACTN[:, j % 2, :], SIL[:, j % 2, :], ps[:, 2 * (j % 2) + 1, :],
                                          ALU.mult).then_inc(act_done, 1)
                    if i == 4 * j + 9:
                        dve.wait_ge(act_hi, J + (j + 1))
                        dve.tensor_tensor(ACTT[:, 1, 4 * j:4 * j + 4, :],
                                          ps[:, 6, :].rearrange("p (k s) -> p k s", k=4),
                                          ACTT[:, 0, 4 * j:4 * j + 4, :].bitcast(F32),
                                          ALU.subtract).then_inc(act_lo, 1)

            def blocks_of(e, first, last):
                for i in range(first, last):
                    split(e, i)
                    rest(e, i)

            for i in range(SPL):
                if rnd:
                    split(0, i)
                rest(0, i)
            with dve.Fori(0, NE - 1) as e:
                blocks_of(e, SPL, EB)
                blocks_of(e + 1, 0, SPL)
            blocks_of(NE - 1, SPL, EB)
            if not rnd:
                gates(3, 160)
            ylo(n0 + 9)
            for i in range(4):
                accumulate(n0 + 8, i, bank=i)
            dve.wait_ge(acc_done, (n0 + 9) * 4 + 1)

        experts(0)
        more = dve.value_load(CNT[0:1, 0:1], min_val=0, max_val=1)
        with dve.If(more > 0):
            experts(1)
        dve.end_ifs()

        fin = [0]

        def flink(ins):
            fin[0] += 1
            ins.then_inc(fin_chain, 1)
            dve.wait_ge(fin_chain, fin[0])

        gb, _, tmp, junk = POST[3]
        for t in range(XT):
            flink(dve.tensor_tensor_reduce(junk, YACC[:, t, :], YACC[:, t, :], 1.0, 0.0, ALU.mult, ALU.add,
                                           SS[:, 4 + t:5 + t]))
        rstd(4, 2, D, flink)
        for t in range(XT):
            flink(dve.scalar_tensor_tensor(out=tmp, in0=YACC[:, t, :], scalar=RSTD[:, 4 + t:5 + t], in1=gb[:, 0, :],
                                           op0=ALU.mult, op1=ALU.mult))
            flink(dve.tensor_tensor(RES[:, t, :], RES[:, t, :], tmp, ALU.add))
            dve.sem_inc(fin_rdy, 1)

    stack.close()


_INS = ["x", "c", "ctx", "c_ctx", "ada_w", "ada_b", "norm_g", "mix_in_w", "mix_out_w", "win_sink", "diff_qkv_w",
        "diff_out_w", "diff_lambda", "diff_subln_g", "ffn_in_w", "ffn_out_w", "router_w", "expert_in_w",
        "expert_out_w"]
_OUTS = [((1, 256, 1024), "float32")]


def kernel(**inputs):
    import numpy as _np
    import concourse.bacc as _bacc
    from concourse import mybir as _mybir
    from concourse.bass_utils import run_bass_kernel_spmd as _run

    nc = _bacc.Bacc("TRN2", target_bir_lowering=False, num_devices=1)
    arrays, args = {}, []
    for name in _INS + ["tables"]:
        a = constant_tables() if name == "tables" else _np.ascontiguousarray(inputs[name])
        arrays[f"in_{name}_dram"] = a
        args.append(nc.dram_tensor(f"in_{name}_dram", a.shape, _mybir.dt.from_np(a.dtype), kind="ExternalInput").ap())
    for i, (shape, dtype) in enumerate(_OUTS):
        dt = _mybir.dt.from_np(_np.dtype(dtype))
        args.append(nc.dram_tensor(f"out_{i}_dram", shape, dt, kind="ExternalOutput").ap())
    backbone(nc, *args)
    r = _run(nc, [arrays], core_ids=[0])
    got = tuple(r.results[0][f"out_{i}_dram"] for i in range(len(_OUTS)))
    return got[0]
```
